# Optimizing a Trainium2 kernel written in Bass

```python
import math
import jax
import jax.numpy as jnp
from jax import lax
import numpy as np

D_MODEL = 1024
BATCH = 1
SEQ = 256
DEPTH = 2
DEC_BATCH = 8
DEC_SEQ = 1
PAST_LEN = 2048
PAGE_SIZE = 128

N_MIX = 4
N_HEADS = 4
HEAD_DIM = 64
MIX_WIDTH = N_HEADS * HEAD_DIM
RWKV_W_RANK = 64
RWKV_A_RANK = 64
RWKV_G_RANK = 128
RWKV_COLS = 3 * MIX_WIDTH + RWKV_W_RANK + RWKV_A_RANK + RWKV_G_RANK
HGRN_COLS = 4 * MIX_WIDTH
RET_COLS = 4 * MIX_WIDTH
MLSTM_QK = 2 * MIX_WIDTH
MLSTM_COLS = 4 * MIX_WIDTH + 2 * N_HEADS
GATE_COLS = N_MIX * D_MODEL
IN_COLS = RWKV_COLS + HGRN_COLS + RET_COLS + MLSTM_COLS + GATE_COLS
MLSTM_CONV = 4
CHUNK = 64
RET_THETA = 10000.0
PEER_HEADS = 8
PEER_N_KEYS = 128
PEER_N_EXPERTS = PEER_N_KEYS * PEER_N_KEYS
PEER_TOPK = 16
PEER_QDIM = 128
PEER_QHALF = PEER_QDIM // 2
PEER_BLOCK = 256
NORM_EPS = 1e-6
RWKV_GN_EPS = 64e-5
HEAD_NORM_EPS = 1e-5
MASK_NEG = -1e30
LB_FLOOR = 1e-30

kernel_name = 'hybrid_rwkv7_hgrn2_retnet_mlstm_peer_step'

def rms_norm(x, g):
    xf = x.astype(jnp.float32)
    y = xf * lax.rsqrt(jnp.mean(xf * xf, axis=-1, keepdims=True) + NORM_EPS)
    return (y * g.astype(jnp.float32)).astype(x.dtype)

def head_norm(y, g=None, b=None, eps=HEAD_NORM_EPS, center=False):
    if center:
        y = y - jnp.mean(y, axis=-1, keepdims=True)
    y = y * lax.rsqrt(jnp.mean(y * y, axis=-1, keepdims=True) + eps)
    if g is not None:
        y = y * g.astype(jnp.float32).reshape(N_HEADS, HEAD_DIM)
    if b is not None:
        y = y + b.astype(jnp.float32).reshape(N_HEADS, HEAD_DIM)
    return y

def heads(z):
    return z.reshape(z.shape[:-1] + (N_HEADS, -1))

def to_chunks(z, L):
    B, T, H = z.shape[:3]
    z = z.reshape((B, T // L, L, H) + z.shape[3:])
    return jnp.transpose(z, (1, 0, 3, 2) + tuple(range(4, z.ndim)))

def from_chunks(z):
    nC, B, H, L, D = z.shape
    return jnp.transpose(z, (1, 0, 3, 2, 4)).reshape(B, nC * L, H, D)

def causal_mask(L):
    idx = jnp.arange(L)
    return idx[:, None] >= idx[None, :]

def rotary(z, pos):
    half = HEAD_DIM // 2
    inv = RET_THETA ** (-jnp.arange(half, dtype=jnp.float32) / half)
    ang = pos.astype(jnp.float32)[:, None] * inv[None, :]
    cos = jnp.cos(ang)[None, :, None, :]
    sin = jnp.sin(ang)[None, :, None, :]
    z1, z2 = z[..., :half], z[..., half:]
    return jnp.concatenate([z1 * cos - z2 * sin, z1 * sin + z2 * cos], axis=-1)

def rwkv7_mixer(p, shift_prev, S0, mu, w0, w_up, a0, a_up, g_up, k_k, k_a, r_k, ln_g, ln_b):
    B, T, _ = p.shape
    W = MIX_WIDTH
    p_prev = jnp.concatenate([shift_prev[:, None], p[:, :-1]], axis=1)
    xs = p + mu * (p_prev - p)
    r, k, v = xs[..., :W], xs[..., W:2 * W], xs[..., 2 * W:3 * W]
    o = 3 * W
    xw = xs[..., o:o + RWKV_W_RANK]
    o += RWKV_W_RANK
    xa = xs[..., o:o + RWKV_A_RANK]
    o += RWKV_A_RANK
    xg = xs[..., o:o + RWKV_G_RANK]
    w = w0 + jnp.tanh(xw) @ w_up
    log_decay = -jnp.exp(-jax.nn.softplus(-w) - 0.5)
    a = jax.nn.sigmoid(a0 + xa @ a_up)
    g = jax.nn.sigmoid(xg) @ g_up
    kk = heads(k * k_k)
    kk = kk / jnp.maximum(jnp.sqrt(jnp.sum(kk * kk, axis=-1, keepdims=True)), 1e-12)
    k = k * (1.0 + (a - 1.0) * k_a)
    r_h, k_h, v_h, a_h = heads(r), heads(k), heads(v), heads(a)
    wd = jnp.exp(heads(log_decay))

    def step(S, inp):
        r_t, w_t, k_t, v_t, kk_t, a_t = inp
        sa = jnp.einsum('bhvk,bhk->bhv', S, -kk_t)
        S = (S * w_t[:, :, None, :]
             + jnp.einsum('bhv,bhk->bhvk', sa, kk_t * a_t)
             + jnp.einsum('bhv,bhk->bhvk', v_t, k_t))
        return S, jnp.einsum('bhvk,bhk->bhv', S, r_t)

    tm = lambda z: jnp.moveaxis(z, 1, 0)
    S_T, y = lax.scan(step, S0, (tm(r_h), tm(wd), tm(k_h), tm(v_h), tm(kk), tm(a_h)))
    y = jnp.moveaxis(y, 0, 1)
    y = head_norm(y, ln_g, ln_b, eps=RWKV_GN_EPS, center=True)
    y = y + jnp.sum(r_h * k_h * r_k.reshape(N_HEADS, HEAD_DIM), axis=-1, keepdims=True) * v_h
    return y.reshape(B, T, W) * g, p[:, -1], S_T

def gla_chunked(q, k, v, log_f, S0):
    T = q.shape[1]
    L = math.gcd(T, CHUNK)
    causal = causal_mask(L)

    def step(S, inp):
        qc, kc, vc, gc = inp
        b = jnp.cumsum(gc, axis=2)
        o = jnp.einsum('bhtd,bhdv->bhtv', qc * jnp.exp(b), S)
        diff = jnp.where(causal[:, :, None], b[:, :, :, None, :] - b[:, :, None, :, :], MASK_NEG)
        A = jnp.einsum('bhtsd,bhsd->bhts', qc[:, :, :, None, :] * jnp.exp(diff), kc)
        o = o + jnp.einsum('bhts,bhsv->bhtv', A, vc)
        bL = b[:, :, -1:]
        S = S * jnp.exp(bL)[:, :, 0, :, None] + jnp.einsum('bhsd,bhsv->bhdv', kc * jnp.exp(bL - b), vc)
        return S, o

    S, o = lax.scan(step, S0, (to_chunks(q, L), to_chunks(k, L), to_chunks(v, L), to_chunks(log_f, L)))
    return from_chunks(o), S

def hgrn2_mixer(p, S0, lb, norm_g):
    B, T, _ = p.shape
    W = MIX_WIDTH
    q = jax.nn.silu(p[..., :W])
    f_pre = p[..., W:2 * W]
    i_in = p[..., 2 * W:3 * W]
    g = p[..., 3 * W:]
    log_f = jnp.logaddexp(jnp.log(jnp.maximum(lb, LB_FLOOR)),
                          jnp.log1p(-lb) + jax.nn.log_sigmoid(f_pre))
    k = -jnp.expm1(log_f)
    o, S = gla_chunked(heads(q), heads(k), heads(i_in), heads(log_f), S0)
    o = head_norm(o, norm_g).reshape(B, T, W) * jax.nn.silu(g)
    return o, S

def retention_chunked(q, k, v, S0):
    T = q.shape[1]
    L = math.gcd(T, CHUNK)
    lg = jnp.log(1.0 - 2.0 ** (-5.0 - jnp.arange(N_HEADS, dtype=jnp.float32)))
    idx = jnp.arange(L, dtype=jnp.float32)
    rel = idx[:, None] - idx[None, :]
    dmat = jnp.where(rel >= 0, jnp.exp(lg[:, None, None] * jnp.maximum(rel, 0.0)), 0.0)
    d_in = jnp.exp(lg[:, None] * (idx + 1.0))[..., None]
    d_st = jnp.exp(lg[:, None] * (L - 1.0 - idx))[..., None]
    g_L = jnp.exp(lg * L)[:, None, None]

    def step(S, inp):
        qc, kc, vc = inp
        att = jnp.einsum('bhtd,bhsd->bhts', qc, kc) * dmat
        o = jnp.einsum('bhts,bhsv->bhtv', att, vc) + jnp.einsum('bhtd,bhdv->bhtv', qc, S) * d_in
        S = S * g_L + jnp.einsum('bhsd,bhsv->bhdv', kc * d_st, vc)
        return S, o

    S, o = lax.scan(step, S0, (to_chunks(q, L), to_chunks(k, L), to_chunks(v, L)))
    return from_chunks(o), S

def retention_mixer(p, S0, pos0):
    B, T, _ = p.shape
    W = MIX_WIDTH
    pos = pos0 + jnp.arange(T)
    q = rotary(heads(p[..., :W]), pos)
    k = rotary(heads(p[..., W:2 * W]), pos) * HEAD_DIM ** -0.5
    v = heads(p[..., 2 * W:3 * W])
    g = p[..., 3 * W:]
    o, S = retention_chunked(q, k, v, S0)
    o = head_norm(o).reshape(B, T, W) * jax.nn.silu(g)
    return o, S

def mlstm_chunked(q, k, v, ig, lf, C0, n0, m0):
    T = q.shape[1]
    L = math.gcd(T, CHUNK)
    causal = causal_mask(L)

    def step(carry, inp):
        C, n, m = carry
        qc, kc, vc, igc, lfc = inp
        b = jnp.cumsum(lfc, axis=-1)
        log_d = jnp.where(causal, b[..., :, None] - b[..., None, :] + igc[..., None, :], MASK_NEG)
        m_inter = b + m[..., None]
        m_t = jnp.maximum(m_inter, jnp.max(log_d, axis=-1))
        sc = jnp.einsum('bhtd,bhsd->bhts', qc, kc) * jnp.exp(log_d - m_t[..., None])
        w_inter = jnp.exp(m_inter - m_t)
        num = jnp.einsum('bhts,bhsv->bhtv', sc, vc) + w_inter[..., None] * jnp.einsum('bhtd,bhdv->bhtv', qc, C)
        den = jnp.sum(sc, axis=-1) + w_inter * jnp.einsum('bhtd,bhd->bht', qc, n)
        h = num / jnp.maximum(jnp.abs(den), jnp.exp(-m_t))[..., None]
        m_L = m_t[..., -1]
        a_prev = jnp.exp(b[..., -1] + m - m_L)
        a_s = jnp.exp(igc + b[..., -1:] - b - m_L[..., None])
        C = C * a_prev[..., None, None] + jnp.einsum('bhsd,bhsv->bhdv', kc * a_s[..., None], vc)
        n = n * a_prev[..., None] + jnp.einsum('bhs,bhsd->bhd', a_s, kc)
        return (C, n, m_L), h

    (C, n, m), h = lax.scan(step, (C0, n0, m0),
                            (to_chunks(q, L), to_chunks(k, L), to_chunks(v, L),
                             to_chunks(ig, L), to_chunks(lf, L)))
    return from_chunks(h), C, n, m

def mlstm_mixer(p, conv_prev, C0, n0, m0, conv_w, conv_b, ig_b, fg_b, norm_g):
    B, T, _ = p.shape
    W = MIX_WIDTH
    H = N_HEADS
    qk_raw = p[..., :MLSTM_QK]
    full = jnp.concatenate([conv_prev, qk_raw], axis=1)
    qk = lax.conv_general_dilated(full, conv_w.astype(full.dtype)[:, None, :], window_strides=(1,),
                                  padding='VALID', dimension_numbers=('NWC', 'WIO', 'NWC'),
                                  feature_group_count=MLSTM_QK)
    qk = jax.nn.silu(qk + conv_b)
    q = heads(qk[..., :W])
    k = heads(qk[..., W:]) * HEAD_DIM ** -0.5
    v = heads(p[..., 2 * W:3 * W])
    ig = p[..., 3 * W:3 * W + H] + ig_b
    lf = jax.nn.log_sigmoid(p[..., 3 * W + H:3 * W + 2 * H] + fg_b)
    og = p[..., 3 * W + 2 * H:]
    h, C, n, m = mlstm_chunked(q, k, v, ig, lf, C0, n0, m0)
    h = jax.nn.sigmoid(og) * head_norm(h, norm_g, center=True).reshape(B, T, W)
    return h, full[:, -(MLSTM_CONV - 1):], C, n, m

def peer_ffn(xn, w_q, keys, U, V):
    B, T, D = xn.shape
    n = B * T
    xf = xn.reshape(n, D)
    q = (xf @ w_q).astype(jnp.float32).reshape(n, PEER_HEADS, 2, PEER_QHALF)
    s = jnp.einsum('nhcd,hckd->nhck', q, keys.astype(jnp.float32))
    s1, i1 = lax.top_k(s[:, :, 0], PEER_TOPK)
    s2, i2 = lax.top_k(s[:, :, 1], PEER_TOPK)
    cand = (s1[..., :, None] + s2[..., None, :]).reshape(n, PEER_HEADS, PEER_TOPK * PEER_TOPK)
    cidx = (i1[..., :, None] * PEER_N_KEYS + i2[..., None, :]).reshape(n, PEER_HEADS, PEER_TOPK * PEER_TOPK)
    top, sel = lax.top_k(cand, PEER_TOPK)
    eidx = jnp.take_along_axis(cidx, sel, axis=-1)
    gate = jax.nn.softmax(top, axis=-1)
    blk = math.gcd(n, PEER_BLOCK)
    nb = n // blk
    kk = PEER_HEADS * PEER_TOPK

    def block(args):
        xb, eb, gb = args
        hid = jax.nn.gelu(jnp.einsum('nkd,nd->nk', U[eb], xb).astype(jnp.float32), approximate=False)
        return jnp.einsum('nk,nkd->nd', (hid * gb).astype(xb.dtype), V[eb])

    out = lax.map(block, (xf.reshape(nb, blk, D), eidx.reshape(nb, blk, kk), gate.reshape(nb, blk, kk)))
    return out.reshape(B, T, D).astype(xn.dtype)

def hybrid_layer(x, st, pos0, P, l):
    B, T, _ = x.shape
    xn = rms_norm(x, P['ln1_g'][l])
    proj = (xn @ P['w_in'][l]).astype(jnp.float32)
    o1 = RWKV_COLS
    o2 = o1 + HGRN_COLS
    o3 = o2 + RET_COLS
    o4 = o3 + MLSTM_COLS
    y_a, shift_new, S_a = rwkv7_mixer(proj[..., :o1], st[0], st[1], P['rwkv_mu'][l], P['rwkv_w0'][l],
                                      P['rwkv_w_up'][l], P['rwkv_a0'][l], P['rwkv_a_up'][l],
                                      P['rwkv_g_up'][l], P['rwkv_k_k'][l], P['rwkv_k_a'][l],
                                      P['rwkv_r_k'][l], P['rwkv_ln_g'][l], P['rwkv_ln_b'][l])
    y_b, S_b = hgrn2_mixer(proj[..., o1:o2], st[2], P['hgrn_lb'][l], P['hgrn_norm_g'][l])
    y_c, S_c = retention_mixer(proj[..., o2:o3], st[3], pos0)
    y_d, conv_new, C_d, n_d, m_d = mlstm_mixer(proj[..., o3:o4], st[4], st[5], st[6], st[7],
                                               P['mlstm_conv_w'][l], P['mlstm_conv_b'][l],
                                               P['mlstm_ig_b'][l], P['mlstm_fg_b'][l],
                                               P['mlstm_norm_g'][l])
    gates = jax.nn.sigmoid(proj[..., o4:]).reshape(B, T, N_MIX, D_MODEL)
    ys = jnp.stack([y_a, y_b, y_c, y_d], axis=2)
    branch = jnp.einsum('btmw,mwd->btmd', ys, P['w_branch'][l].astype(jnp.float32))
    merged = jnp.sum(gates * branch, axis=2).astype(x.dtype)
    x = x + merged @ P['w_out'][l]
    x = x + peer_ffn(rms_norm(x, P['ln2_g'][l]), P['peer_w_q'][l], P['peer_keys'][l],
                     P['peer_u'][l], P['peer_v'][l])
    return x, (shift_new, S_a, S_b, S_c, conv_new, C_d, n_d, m_d)

def run_trunk(x, states, pos0, P):
    new = tuple([] for _ in states)
    for l in range(DEPTH):
        st = tuple(s[l].astype(jnp.float32) for s in states)
        x, st_new = hybrid_layer(x, st, pos0, P, l)
        for acc, s in zip(new, st_new):
            acc.append(s)
    return rms_norm(x, P['lnf_g']), tuple(jnp.stack(acc, axis=0) for acc in new)

def setup_inputs(seed: int = 0) -> dict:
    key = jax.random.key(seed)
    ks = iter(jax.random.split(key, 64))
    nrm = lambda shape, scale: scale * jax.random.normal(next(ks), shape, jnp.float32)
    gain = lambda shape: 1.0 + 0.02 * jax.random.normal(next(ks), shape, jnp.float32)
    Lr, W, H, Dh = DEPTH, MIX_WIDTH, N_HEADS, HEAD_DIM
    return {
        'x_prompt': nrm((BATCH, SEQ, D_MODEL), 1.0),
        'x_sample': nrm((DEC_BATCH, DEC_SEQ, D_MODEL), 1.0),
        'state_rwkv_shift': nrm((Lr, DEC_BATCH, RWKV_COLS), 1.0),
        'state_rwkv_S': nrm((Lr, DEC_BATCH, H, Dh, Dh), 0.3),
        'state_hgrn_S': nrm((Lr, DEC_BATCH, H, Dh, Dh), 0.3),
        'state_ret_S': nrm((Lr, DEC_BATCH, H, Dh, Dh), 1.0),
        'state_mlstm_conv': nrm((Lr, DEC_BATCH, MLSTM_CONV - 1, MLSTM_QK), 1.0),
        'state_mlstm_C': nrm((Lr, DEC_BATCH, H, Dh, Dh), 0.3),
        'state_mlstm_n': nrm((Lr, DEC_BATCH, H, Dh), 1.0),
        'state_mlstm_m': nrm((Lr, DEC_BATCH, H), 1.0),
        'ln1_g': gain((Lr, D_MODEL)),
        'w_in': nrm((Lr, D_MODEL, IN_COLS), D_MODEL ** -0.5),
        'rwkv_mu': jax.random.uniform(next(ks), (Lr, RWKV_COLS), jnp.float32, 0.0, 1.0),
        'rwkv_w0': jax.random.uniform(next(ks), (Lr, W), jnp.float32, -6.0, -1.0),
        'rwkv_w_up': nrm((Lr, RWKV_W_RANK, W), 0.1 * RWKV_W_RANK ** -0.5),
        'rwkv_a0': nrm((Lr, W), 0.1),
        'rwkv_a_up': nrm((Lr, RWKV_A_RANK, W), 0.5 * RWKV_A_RANK ** -0.5),
        'rwkv_g_up': nrm((Lr, RWKV_G_RANK, W), RWKV_G_RANK ** -0.5),
        'rwkv_k_k': 0.85 + nrm((Lr, W), 0.05),
        'rwkv_k_a': 1.0 + nrm((Lr, W), 0.05),
        'rwkv_r_k': nrm((Lr, W), 0.1),
        'rwkv_ln_g': gain((Lr, W)),
        'rwkv_ln_b': nrm((Lr, W), 0.02),
        'hgrn_lb_logits': nrm((Lr, W), 0.1),
        'hgrn_norm_g': gain((Lr, W)),
        'mlstm_conv_w': nrm((Lr, MLSTM_CONV, MLSTM_QK), MLSTM_CONV ** -0.5),
        'mlstm_conv_b': nrm((Lr, MLSTM_QK), 0.02),
        'mlstm_ig_b': nrm((Lr, H), 0.1),
        'mlstm_fg_b': jnp.linspace(3.0, 6.0, H, dtype=jnp.float32)[None, :] + nrm((Lr, H), 0.1),
        'mlstm_norm_g': gain((Lr, W)),
        'w_branch': nrm((Lr, N_MIX, W, D_MODEL), W ** -0.5),
        'w_out': nrm((Lr, D_MODEL, D_MODEL), D_MODEL ** -0.5),
        'ln2_g': gain((Lr, D_MODEL)),
        'peer_w_q': nrm((Lr, D_MODEL, PEER_HEADS * PEER_QDIM), D_MODEL ** -0.5),
        'peer_keys': nrm((Lr, PEER_HEADS, 2, PEER_N_KEYS, PEER_QHALF), PEER_QHALF ** -0.5),
        'peer_u': nrm((Lr, PEER_N_EXPERTS, D_MODEL), D_MODEL ** -0.5),
        'peer_v': nrm((Lr, PEER_N_EXPERTS, D_MODEL), PEER_HEADS ** -0.5),
        'lnf_g': gain((D_MODEL,)),
    }

def reference(x_prompt, x_sample, state_rwkv_shift, state_rwkv_S, state_hgrn_S, state_ret_S,
              state_mlstm_conv, state_mlstm_C, state_mlstm_n, state_mlstm_m,
              ln1_g, w_in, rwkv_mu, rwkv_w0, rwkv_w_up, rwkv_a0, rwkv_a_up, rwkv_g_up,
              rwkv_k_k, rwkv_k_a, rwkv_r_k, rwkv_ln_g, rwkv_ln_b, hgrn_lb_logits, hgrn_norm_g,
              mlstm_conv_w, mlstm_conv_b, mlstm_ig_b, mlstm_fg_b, mlstm_norm_g,
              w_branch, w_out, ln2_g, peer_w_q, peer_keys, peer_u, peer_v, lnf_g):
    lb_all = jax.nn.softmax(hgrn_lb_logits.astype(jnp.float32), axis=0)
    hgrn_lb = jnp.cumsum(lb_all, axis=0) - lb_all[0:1]
    P = dict(ln1_g=ln1_g, w_in=w_in, rwkv_mu=rwkv_mu, rwkv_w0=rwkv_w0, rwkv_w_up=rwkv_w_up,
             rwkv_a0=rwkv_a0, rwkv_a_up=rwkv_a_up, rwkv_g_up=rwkv_g_up, rwkv_k_k=rwkv_k_k,
             rwkv_k_a=rwkv_k_a, rwkv_r_k=rwkv_r_k, rwkv_ln_g=rwkv_ln_g, rwkv_ln_b=rwkv_ln_b,
             hgrn_lb=hgrn_lb, hgrn_norm_g=hgrn_norm_g, mlstm_conv_w=mlstm_conv_w,
             mlstm_conv_b=mlstm_conv_b, mlstm_ig_b=mlstm_ig_b, mlstm_fg_b=mlstm_fg_b,
             mlstm_norm_g=mlstm_norm_g, w_branch=w_branch, w_out=w_out, ln2_g=ln2_g,
             peer_w_q=peer_w_q, peer_keys=peer_keys, peer_u=peer_u, peer_v=peer_v, lnf_g=lnf_g)

    Bp = x_prompt.shape[0]
    z = lambda *shape: jnp.zeros((DEPTH, Bp) + shape, jnp.float32)
    prompt_init = (z(RWKV_COLS), z(N_HEADS, HEAD_DIM, HEAD_DIM), z(N_HEADS, HEAD_DIM, HEAD_DIM),
                   z(N_HEADS, HEAD_DIM, HEAD_DIM), z(MLSTM_CONV - 1, MLSTM_QK),
                   z(N_HEADS, HEAD_DIM, HEAD_DIM), z(N_HEADS, HEAD_DIM), z(N_HEADS))
    y_prompt, (p_rwkv_shift, p_rwkv_S, p_hgrn_S, p_ret_S, p_mlstm_conv, p_mlstm_C, p_mlstm_n,
               p_mlstm_m) = run_trunk(x_prompt, prompt_init, 0, P)

    sample_init = (state_rwkv_shift, state_rwkv_S, state_hgrn_S, state_ret_S, state_mlstm_conv,
                   state_mlstm_C, state_mlstm_n, state_mlstm_m)
    y_sample, (s_rwkv_shift, s_rwkv_S, s_hgrn_S, s_ret_S, s_mlstm_conv, s_mlstm_C, s_mlstm_n,
               s_mlstm_m) = run_trunk(x_sample, sample_init, PAST_LEN, P)

    return (y_prompt, y_sample,
            p_rwkv_shift, p_rwkv_S, p_hgrn_S, p_ret_S, p_mlstm_conv, p_mlstm_C, p_mlstm_n, p_mlstm_m,
            s_rwkv_shift, s_rwkv_S, s_hgrn_S, s_ret_S, s_mlstm_conv, s_mlstm_C, s_mlstm_n, s_mlstm_m)


_drawn_inputs = setup_inputs


def setup_inputs(seed=0):
    import zlib

    import numpy as np

    out = dict(_drawn_inputs(seed))
    spreads = {}
    factors = {'rwkv_w_up': 4.13, 'lnf_g': 2.726}
    for name, (base, spread) in spreads.items():
        noise = np.random.default_rng([zlib.crc32(name.encode()), seed]).standard_normal(out[name].shape)
        drawn = base * np.exp(spread * noise) if base else spread * noise
        out[name] = jnp.asarray(drawn.astype(out[name].dtype))
    for name, factor in factors.items():
        out[name] = (out[name] * factor).astype(out[name].dtype)
    return out
```

```python
from contextlib import ExitStack

import numpy as np

import concourse.bass as bass
from concourse import mybir

F32 = mybir.dt.float32
U32 = mybir.dt.uint32
ALU = mybir.AluOpType
ACT = mybir.ActivationFunctionType
AX_X = mybir.AxisListType.X

P = 128
D = 1024
KT = D // P
SEQ = 256
NS = 8
N = SEQ + NS
L = 2
H = 4
HD = 64
PR = H // 2
TT = SEQ // P
CH = 64
NCH = SEQ // CH
EXPERTS = 128 * 128
PH = 8
TOPK = 16
SLOTS = PH * TOPK
PAST = 2048
NQ = 3 * P
BLOCK = 2048
N_IN, N_MIXED = 32, 16
N_BLOCKS = N_IN + 4 + 4 + 4
ATT = SEQ + P
BIG = 3.0e38
PE_STEPS = ("lr", "kk", "rk", "tr", "bv", "rot", "if", "rows", "svt", "sa", "po", "mean", "var", "xt", "acc")
NORM_EPS, RWKV_EPS, HEAD_EPS = 1e-6, 64e-5, 1e-5

PAR = dict(mu=(0, 8), w0=(8, 2), a0=(10, 2), kk=(12, 2), ka=(14, 2), rk=(16, 2), ln_g=(18, 2), ln_b=(20, 2),
           hg=(22, 2), mg=(24, 2), cw=(26, 16), cb=(42, 4), ln1=(46, 8), ln2=(54, 8), ig_b=(62, 1), fg_b=(63, 1))
NPAR = 64
NGLOB = 8 + 2 * L
V_F, V_K, V_Q, V_V, V_RW = 0, 3, 6, 9, 12
RW_W, RW_K, RW_R, RW_KK, RW_KKA, RW_V = range(12, 18)
NVEC = 18
NGLA = 12


def constants():
    p = np.arange(P)
    head = p // HD
    t = {}
    t["ident"] = np.eye(P)
    t["ones"] = np.ones((P, P))
    t["headsum"] = (head[:, None] == head[None]).astype(np.float64)
    t["headmean"] = t["headsum"] / HD
    s, c = p[:, None], p[None]
    same = (s // CH) == (c // CH)
    strict, incl = same & (s < c), same & (s <= c)
    t["chunkmask"] = np.concatenate([strict, incl, strict, incl], 1)
    levels = []
    for k in range(6):
        b = 1 << k
        levels.append(-((s // (2 * b) == c // (2 * b)) & (s % (2 * b) >= b) & (c % (2 * b) < b)).astype(float))
    t["levels"] = np.concatenate(levels, 1)
    tri = (s <= c).astype(float)
    t["causal"] = np.concatenate([tri, np.ones((P, P)), tri], 1)
    lg = np.log(1.0 - 2.0 ** (-5.0 - np.arange(H)))
    rel = [np.arange(SEQ)[None] - s, np.arange(P, SEQ)[None] - (s + P)]
    t["decay"] = np.concatenate([np.where(r >= 0, np.exp(lg[h] * np.maximum(r, 0)), 0.0) for h in range(H) for r in rel], 1)
    t["decay_end"] = np.stack([np.exp(lg[h] * (SEQ - 1 - (p + P * st))) for st in range(TT) for h in range(H)], 1)
    t["decay_chan"] = np.stack([np.exp(lg[2 * pr + head]) for pr in range(PR)], 1)
    half = HD // 2
    inv = (10000.0 ** (-(np.arange(half, dtype=np.float32)) / np.float32(half))).astype(np.float32)
    pos = np.concatenate([np.arange(SEQ), np.full(NS, PAST)]).astype(np.float32)
    ang = (pos[None] * inv[p % half][:, None]).astype(np.float32).astype(np.float64)
    t["cos"], t["sin"] = np.cos(ang), np.sin(ang)
    rot = np.zeros((P, P))
    for q in range(P):
        if q % HD < half:
            rot[q + half, q] = -1.0
        else:
            rot[q - half, q] = 1.0
    t["rot"] = rot
    place = np.zeros((P, 191))
    place[p, HD - 1 + HD * head] = 1.0
    t["place"] = place
    t["channel"] = (p[:, None] % HD == np.arange(HD)[None]).astype(float)
    t["onespad"] = np.tile(np.repeat([0.0, 1.0, 0.0], HD), (P, 1))
    t["chunkstart"] = np.tile((np.arange(SEQ) % CH != 0).astype(float), (P, 1))
    t["rows"] = np.stack([head == 0, head == 1, -1.0 * (head == 0), -1.0 * (head == 1)], 1)
    t["iota16"] = np.tile(np.arange(16.0), (P, 1))
    t["quads"] = (p[:, None] // 4 == p[None] // 4).astype(float)
    b_of, h_of = p // 16, (p // 4) % 4
    t["samples"] = ((h_of[:, None] == np.repeat(np.arange(H), NS)[None]) & (b_of[:, None] == np.tile(np.arange(NS), H)[None]))
    t["group"] = (p[:, None] // 16 == np.arange(NS)[None]).astype(float)
    sel = np.zeros((P, H, P))
    for h in range(H):
        sel[h, h] = 1.0
    t["rowsel"] = sel.reshape(P, -1)
    pair = np.zeros((P, PR, P))
    for pr in range(PR):
        for q in range(P):
            pair[2 * pr + q // HD, pr, q] = 1.0
    t["pairsel"] = pair.reshape(P, -1)
    t["zero"] = np.zeros((P, SEQ))
    t["eps"] = np.tile([NORM_EPS, RWKV_EPS, HEAD_EPS, 1.0], (P, 1))
    at, n = {}, 0
    for k, v in t.items():
        at[k] = (n, v.shape[1])
        n += v.shape[1]
    return np.concatenate([np.asarray(v, np.float32) for v in t.values()], 1).astype(np.float32), at, n


_, CONST_AT, NCONST = constants()
ARENA = 22320


def build(nc, A, O):
    with ExitStack() as ctx:
        def sb(name, shape, dt=F32):
            return ctx.enter_context(nc.sbuf_tensor(name, shape, dt))

        sems = {}

        def sem(name, per_layer=True):
            s = ctx.enter_context(nc.semaphore(name))
            if per_layer:
                sems[name] = s
            return s

        x = sb("x", [P, KT, N])
        const = sb("const", [P, NCONST])
        glob = sb("glob", [P, NGLOB])
        lb_all = sb("lb_all", [P, L * PR])
        lb = sb("lb", [P, 3, PR])
        par = sb("par", [P, NPAR])
        wa_up = sb("wa_up", [P, 256])
        g_up = sb("g_up", [P, 256])
        w_if = sb("w_if", [P, KT, 8])
        st = sb("st", [P, 4, 16, HD])
        st_n = sb("st_n", [P, 16])
        st_shift = sb("st_shift", [P, 8, NS])
        st_conv = sb("st_conv", [P, 4, NS, 3])
        m_old = sb("m_old", [4, NS])
        xn = sb("xn", [P, KT, N])
        ring = sb("ring", [P, 5, BLOCK])
        layer_off = sb("layer_off", [P, 1])
        keyz = sb("keyz", [P, 2, 2, PR, SEQ])
        vpad = sb("vpad", [P, 2, H, 3 * HD])
        upad = sb("upad", [P, H, 3 * HD])
        out_shift = sb("sb_shift", [P, 8, NS + 1])
        out_conv = sb("sb_conv", [P, 4, NS + 1, 3])
        out_m = sb("sb_m", [4, NS + 1])
        small = sb("small", [P, 32])
        arena = sb("arena", [P, ARENA])

        ps = ctx.enter_context(nc.psum_tensor("ps", [P, 8, 512], F32))

        def C(name, n=None):
            a, w = CONST_AT[name]
            return const[:, a:a + (n or w)]

        def V(name, i=0, n=1):
            return par[:, PAR[name][0] + i:PAR[name][0] + i + n]

        top = [0]

        def carve(*shape, at=None, dt=F32):
            n = int(np.prod(shape))
            if at is None:
                at = top[0]
                top[0] += n
            assert at + n <= ARENA, (at, n)
            v = arena[:, at:at + n]
            if dt != F32:
                v = v.bitcast(dt)
            if len(shape) == 1:
                return v
            names = " ".join(f"d{i}" for i in range(len(shape)))
            return v.rearrange(f"p ({names}) -> p {names}", **{f"d{i}": s for i, s in enumerate(shape)})

        proj = carve(32, N)
        yy = carve(8, N)
        gg = carve(PR, N)
        vb = carve(PR, N)
        sv = carve(PR, NVEC, NS)
        emk = carve(PR, N)
        denk = carve(PR, N)
        sqs = carve(8, N, at=top[0])
        mix = top[0]
        diff = carve(8, N)
        loga, aa, kk, kn, kka, t1 = [carve(PR, N) for _ in range(6)]
        chunk_m = carve(8, 512, at=mix)
        al, kb = carve(PR, SEQ, at=mix), carve(PR, SEQ, at=mix + 512)
        e_p = carve(PR, SEQ, at=mix + 1024)
        e_n = carve(PR, SEQ, at=mix + 1536)
        rr = carve(TT, H, P, at=mix + 8 * N + 4 * PR * N)
        e_b = carve(PR, SEQ)
        kr = carve(PR, TT, 256)
        xm = carve(8, P, at=0)
        xt = carve(8, P, at=8 * P)
        alt, kbt = carve(TT, 256), carve(TT, 256)
        vc = carve(NCH, 256)
        bv = carve(TT, 256, at=mix - 2 * PR * N)
        pm = carve(256, at=mix - 2 * PR * N + 512)
        sb1 = carve(PR, P, at=mix - 2 * PR * N + 768)
        sbd = carve(PR, P)
        top[0] = mix
        qr, kq, u1, u2 = [carve(PR, N) for _ in range(4)]
        carve(112)
        att = carve(H, ATT)
        ktok = carve(TT, 256)
        sfin = carve(PR, P)
        nfin = carve(PR)
        cpad = carve(4, 288 + 3)
        cv = carve(4, 288, at=mix + 2 * PR * N)
        rows = carve(10, N)
        rowx = carve(280)
        ccol = carve(TT, H)
        fa = carve(PR, 2 * NS)
        top[0] = mix
        fp, kp, qp = [carve(PR, SEQ) for _ in range(3)]
        sgn = carve(PR, N)
        kv = carve(4, 512)
        ss = carve(4, 512)
        qs = carve(4, 512)
        hfin = carve(HD, PR)
        sel = carve(4, P)
        win = carve(4, P)
        top[0] = mix
        svt, svt2 = carve(PR, P), carve(PR, P)
        gv = carve(NVEC, 16)
        gvv = carve(4, HD)
        big1, big2 = carve(3, 16, HD), carve(16, HD)
        nq = carve(16)
        po = carve(4, 2, HD)
        pn = carve(1)
        sa, sab = carve(HD), carve(HD)
        rs8 = carve(8, N, at=mix + 8 * N)
        fg8 = carve(8, N, at=mix + 16 * N)
        gate4 = carve(2, 4, N, at=mix)
        gsum = carve(2, N, at=mix + 8 * N)
        merged = carve(8, N, at=0)
        rstd = yy[:, 0, :]
        rstd2 = carve(N, at=0)
        top[0] = 0
        xtok = carve(3, D)
        eidx = carve(3, SLOTS)
        gate_w = carve(3, SLOTS)
        peer0 = top[0]
        keys = carve(PH, 256)
        qpe = carve(PH, NQ)
        sc = carve(PH * 2, P)
        sc2 = carve(PH * 2, P)
        cand = carve(PH, TOPK, TOPK)
        oh = carve(SLOTS, TOPK)
        xrep = oh.rearrange("p a b -> p (a b)")[:, 0:KT * P].rearrange("p (a b) -> p a b", b=P)
        v16 = carve(PH, 2, TOPK)
        i16 = carve(PH, 2, TOPK, dt=U32)
        i16f = carve(PH, 2, TOPK)
        t16 = carve(PH, TOPK)
        j16 = carve(PH, TOPK, dt=U32)
        ja, jb = carve(SLOTS, dt=U32), carve(SLOTS, dt=U32)
        jaf, jbf = carve(SLOTS), carve(SLOTS)
        e1, e2 = carve(SLOTS), carve(SLOTS)
        tsum = carve(PH)
        sq2 = carve(8, N, at=peer0)
        assert top[0] <= ARENA
        top[0] = peer0
        urows = carve(8, D)
        acc = carve(3, D)
        hid, hge, wgt = [carve(2, 4) for _ in range(3)]
        ixu = carve(2, 4, dt=U32)
        ixv = carve(2, 4, dt=U32)
        es = carve(8, dt=U32)
        gs = carve(8)
        vrows = ring[:, 0:4, :].rearrange("p a (b c) -> p (a b) c", b=2)

        for name in (
                "act_bv act_co act_conv act_cv act_dt act_e act_em act_hg act_kk act_lr act_og act_proj act_q act_r0 act_r2 "
                "act_rt act_rt8 act_silu act_sv act_sv0 act_svt act_turn act_vpad act_wa act_wag act_xt act_y act_ysq "
                "dve_acc dve_att dve_cm dve_cum dve_cv dve_dt dve_hg dve_inv dve_kk2 dve_kr dve_kw dve_mg "
                "dve_pm dve_po dve_qk dve_qz dve_r dve_r1 dve_rk dve_route dve_rows dve_sa dve_sbd dve_shift dve_sq "
                "dve_sv dve_u dve_x dve_xn dve_xs dve_y2 dve_yc dve_yn dve_yy "
                "pe_cf pe_cm pe_co pe_ctr pe_ks pe_p pe_s pe_sc pe_ss pe_step pe_t pe_u pe_wo pe_wq "
                "pool_gla pool_hf pool_kz pool_rw pool_sa pool_st "
                "sp_dfin sp_hfin sp_keys sp_out sp_par sp_rw sp_sr sp_svr sp_svw sp_sw ").split():
            sem(name)
        once = {name: sem(name, False) for name in ("sp_once", "pool_zero", "dve_lb", "act_lb")}

        def S(name):
            return once[name] if name in once else sems[name]

        w_full = [sem(f"w_full{j}", False) for j in range(5)]
        w_free = [sem(f"w_free{j}", False) for j in range(5)]
        bank_full = [sem(f"bank_full{j}", False) for j in range(6)]
        bank_free = [sem(f"bank_free{j}", False) for j in range(6)]
        kv_done = sem("kv_done")
        sel_free = sem("sel_free")
        sel_full = sem("sel_full")
        win_free = sem("win_free")
        win_full = sem("win_full")
        ss_full = sem("ss_full")
        ss_free = sem("ss_free")
        qs_full = sem("qs_full")
        qs_free = sem("qs_free")
        gate_full = [sem(f"gate_full{j}", False) for j in range(2)]
        gate_free = [sem(f"gate_free{j}", False) for j in range(2)]
        ps_scores, ps_scores_free = sem("ps_scores", False), sem("ps_scores_free", False)
        scores, scores_free = sem("scores", False), sem("scores_free", False)
        top_full, top_exp = sem("top_full", False), sem("top_exp", False)
        u_full = [sem(f"u_full{j}", False) for j in range(2)]
        v_full = [sem(f"v_full{j}", False) for j in range(2)]
        u_free = [sem(f"u_free{j}", False) for j in range(2)]
        v_free = [sem(f"v_free{j}", False) for j in range(2)]
        hid_full = [sem(f"hid_full{j}", False) for j in range(2)]
        hid_gelu = [sem(f"hid_gelu{j}", False) for j in range(2)]
        arrive = sem("arrive", False)
        go = {e: sem(f"go_{e}", False) for e in ("pe", "act", "dve", "pool")}

        def step(name):
            return PE_STEPS.index(name) + 1

        def take(e, s, n):
            e.wait_ge(s, n)
            e.sem_clear(s)

        class Own:

            def __init__(self, e, name):
                self.e, self.s, self.n = e, sem(name, False), 0

            def clear(self):
                self.e.sem_clear(self.s)
                self.n = 0

            def __call__(self, ins):
                ins.then_inc(self.s, 1)
                self.n += 1
                self.e.wait_ge(self.s, self.n)

        def layer_end(e, name):
            e.sem_inc(arrive, 1)
            take(e, go[name], 1)

        GROUPS = 2 * SEQ // P * 16 // 2
        assert GROUPS == 32

        block = ctx.enter_context(nc.Block())

        def at1(v):
            return slice(v, v + 1) if isinstance(v, int) else bass.ds(v, 1)

        def bc(ap, k, shape):
            return ap.unsqueeze(k).to_broadcast(shape)

        @block.sync
        def _(e):
            e.dma_start(x[:, :, :], A["x"]).then_inc(S("sp_once"), 16)
            e.dma_start(const[:, :], A["const"]).then_inc(S("sp_once"), 16)
            e.dma_start(glob[:, :], A["glob"]).then_inc(S("sp_once"), 16)
            with e.Fori(0, L) as l:
                def lay(name):
                    return A[name][bass.ds(l, 1)]
                for dst, name in ((par[:, :], "par"), (wa_up[:, :], "wa_up"), (g_up[:, :], "g_up")):
                    e.dma_start(dst, lay(name).rearrange("a p c -> p (a c)")).then_inc(S("sp_par"), 16)
                e.dma_start(w_if[:, :, :].rearrange("p a b -> p (a b)"), lay("w_if").rearrange("a p c -> p (a c)")).then_inc(S("sp_par"), 16)
                for dst, name in ((st[:, :, :, :].rearrange("p a b c -> p (a b c)"), "st"), (st_n[:, :], "st_n"),
                                  (st_shift[:, :, :].rearrange("p a b -> p (a b)"), "st_shift"),
                                  (st_conv[:, :, :, :].rearrange("p a b c -> p (a b c)"), "st_conv"), (m_old[:, :], "m_old")):
                    e.dma_start(dst, lay(name).rearrange("a p c -> p (a c)")).then_inc(S("sp_par"), 16)

                def block_of(j, n):
                    take(e, w_free[j], 1)
                    e.dma_start(ring[:, j, :], A["w"][bass.ds(n, 1)].rearrange("a p c -> p (a c)")).then_inc(w_full[j], 16)

                with e.Fori(0, 4) as i:
                    for j in range(4):
                        block_of(j, l * N_BLOCKS + i * 4 + j)
                e.wait_ge(S("dve_sbd"), NCH + 1)
                e.dma_start(O["p_rw"][bass.ds(l, 1)].rearrange("a p c -> p (a c)"), sbd[:, :, :].rearrange("p a b -> p (a b)")).then_inc(S("sp_rw"), 16)
                e.wait_ge(S("pool_hf"), 1)
                e.dma_start(O["p_hg"][bass.ds(l, 1)].rearrange("a p c -> p (a c)"), hfin[:, :, :].rearrange("p a b -> p (a b)")).then_inc(S("sp_hfin"), 16)
                e.wait_ge(S("act_svt"), 1)
                e.dma_start(O["scratch"][0:NGLA * NS, :], svt[0:NGLA * NS, :, :].rearrange("p a b -> p (a b)")).then_inc(S("sp_svw"), 16)
                e.dma_start(O["scratch"][NGLA * NS:NVEC * NS, :], svt2[0:(NVEC - NGLA) * NS, :, :].rearrange("p a b -> p (a b)")).then_inc(S("sp_svw"), 16)
                e.wait_ge(S("sp_svw"), 32)
                e.dma_start(gv[:, :, :], O["scratch"].rearrange("(v b) (q k) -> (b q) v k", v=NVEC, k=16)).then_inc(S("sp_svr"), 16)
                for n, v in enumerate((V_V, V_V + 1, V_V + 2, RW_V)):
                    src = O["scratch"][v * NS:(v + 1) * NS, :].rearrange("b (h c) -> (b h) c", c=HD)
                    e.dma_start(gvv[:, n, :], bc(src, 1, [32, 4, HD])).then_inc(S("sp_svr"), 16)
                e.wait_ge(S("dve_shift"), 1)
                e.dma_start(O["shift"][bass.ds(l, 1)].rearrange("a p c -> p (a c)"), out_shift[:, :, :].rearrange("p a b -> p (a b)")).then_inc(S("sp_out"), 16)
                with e.Fori(0, 4) as i:
                    for j in range(5):
                        block_of(j, l * N_BLOCKS + N_MIXED + i * 5 + j)
                for k in range(2):
                    for j in range(4):
                        block_of(j, l * N_BLOCKS + 36 + 4 * k + j)
                e.wait_ge(S("pool_st"), 1)
                e.wait_ge(S("act_conv"), 1)
                e.wait_ge(S("dve_rows"), 1)
                for name, src in (("conv", out_conv[:, :, :, :].rearrange("p a b c -> p (a b c)")), ("m", out_m[:, :]),
                                  ("st", st[:, :, :, :].rearrange("p a b c -> p (a b c)")), ("st_n", st_n[:, :])):
                    e.dma_start(O[name][bass.ds(l, 1)].rearrange("a p c -> p (a c)"), src).then_inc(S("sp_out"), 16)
                e.wait_ge(S("dve_x"), KT)
                e.dma_start(keys[:, :, :].rearrange("p a b -> p (a b)"), lay("keys").rearrange("a p c -> p (a c)")).then_inc(S("sp_keys"), 16)
                e.wait_ge(S("dve_route"), 1)
                e.dma_start(O["scratch_i"][:, :], eidx[0:NS, 2, :]).then_inc(S("sp_sw"), 16)
                e.dma_start(O["scratch_g"][:, :], gate_w[0:NS, 2, :]).then_inc(S("sp_sw"), 16)
                e.wait_ge(S("sp_sw"), 32)
                e.dma_start(es, O["scratch_i"].rearrange("b (g j) -> (b g) j", j=8).bitcast(U32)).then_inc(S("sp_sr"), 16)
                e.dma_start(gs, O["scratch_g"].rearrange("b (g j) -> (b g) j", j=8)).then_inc(S("sp_sr"), 16)
                e.wait_ge(S("sp_out"), 5 * 16)
                e.wait_ge(arrive, 4)
                e.sem_clear(arrive)
                for s in sems.values():
                    e.sem_clear(s)
                for s in go.values():
                    e.sem_inc(s, 1)
            e.wait_ge(S("dve_xn"), 1)
            e.dma_start(O["y"], xn[:, :, :]).then_inc(S("sp_out"), 16)
            e.wait_ge(S("sp_out"), 16)

        @block.tensor
        def _(e):
            mm = e.matmul

            def bank(b, n=N, lo=0):
                return ps[:, b, lo:lo + n]

            def sum_squares(sq_, k):
                e.wait_ge(S("dve_sq"), k)
                for kt in range(KT):
                    i = mm(bank(0), C("ones"), sq_[:, kt, :], start=kt == 0, stop=kt == KT - 1)
                i.then_inc(S("pe_ss"), 1)

            e.wait_ge(S("sp_once"), 48)
            for j in range(5):
                e.sem_inc(w_free[j], 1)
            with e.Fori(0, L) as l:
                sum_squares(sqs, 1)
                e.wait_ge(S("dve_xn"), 1)
                with e.Fori(0, 4) as i:
                    for t in range(8):
                        b = t % 2
                        if b == 0:
                            take(e, w_full[t // 2], 16)
                        take(e, bank_free[b], 1)
                        for kt in range(KT):
                            at = b * D + kt * P
                            m = mm(bank(b), ring[:, t // 2, at:at + P], xn[:, kt, :], start=kt == 0, stop=kt == KT - 1)
                        m.then_inc(bank_full[b], 1)
                e.wait_ge(S("sp_par"), 16 * 9)

                e.wait_ge(S("act_lr"), 1)
                e.wait_ge(S("act_proj"), 1)
                for pr in range(PR):
                    c = slice(pr * P, pr * P + P)
                    mm(bank(2 + pr), wa_up[0:HD, c], proj[0:HD, 6, :], start=True, stop=True)
                    mm(bank(4 + pr), wa_up[HD:P, c], proj[HD:P, 6, :], start=True, stop=True)
                    m = mm(bank(6 + pr), g_up[:, c], proj[:, 7, :], start=True, stop=True)
                m.then_inc(S("pe_step"), 1)
                e.wait_ge(S("dve_kk2"), 1)
                for pr in range(PR):
                    m = mm(bank(pr), C("headsum"), t1[:, pr, :], start=True, stop=True)
                m.then_inc(S("pe_step"), 1)
                e.wait_ge(S("act_wag"), 2)
                e.wait_ge(S("dve_rk"), 1)
                for pr in range(PR):
                    m = mm(bank(2 + pr), C("headsum"), t1[:, pr, :], start=True, stop=True)
                m.then_inc(S("pe_step"), 1)
                e.wait_ge(S("dve_kr"), 1)
                for n, src in enumerate((proj[:, 4:6, :], al, kb)):
                    for tt in range(TT):
                        for pr in range(PR):
                            m = e.transpose(ps[:, 4 + n, tt * 256 + pr * P:tt * 256 + pr * P + P], src[:, pr, tt * P:tt * P + P], C("ident"))
                m.then_inc(S("pe_step"), 1)
                e.wait_ge(S("pool_kz"), 1)
                for n in range(TT * H):
                    tt, h = divmod(n, H)
                    pr, q = divmod(h, 2)
                    b = (7, 0, 1)[n % 3]
                    if n >= 3:
                        e.wait_ge(S("dve_cm"), n - 2)
                    mm(bank(b, 256), keyz[:, 0, q, pr, tt * P:tt * P + P], kr[:, pr, tt, :], start=True, stop=True)
                    mm(bank(b, 256, 256), keyz[:, 1, q, pr, tt * P:tt * P + P], kr[:, pr, tt, :], start=True, stop=True)\
                        .then_inc(S("pe_cm"), 1)
                e.wait_ge(S("act_vpad"), 1)
                e.wait_ge(S("dve_cm"), 8)
                for n in range(TT * H):
                    tt, h = divmod(n, H)
                    m = mm(bank(2, HD, tt * 256 + h * HD), chunk_m[:, n, 256:384], vpad[:, tt, h, HD:2 * HD], start=True, stop=True)
                m.then_inc(S("pe_step"), 1)
                for k in range(6):
                    for tt in range(TT):
                        e.wait_ge(S("dve_inv"), max(2 * k + tt, 1))
                        for h in range(H):
                            n = tt * H + h
                            m = mm(bank(3 + tt, P, h * P), chunk_m[:, n, 0:P], xm[:, n, :], start=True, stop=True)
                        m.then_inc(S("pe_t"), 1)
                    for tt in range(TT):
                        e.wait_ge(S("dve_r"), 2 * k + tt + 1)
                        for h in range(H):
                            n = tt * H + h
                            mm(bank(5 + tt, P, h * P), xt[:, n, :], rr[:, tt, h, :], start=True, stop=True)
                        for h in range(H):
                            n = tt * H + h
                            m = mm(bank((7, 0)[tt], P, h * P), rr[:, tt, h, :], xt[:, n, :], start=True, stop=True)
                        m.then_inc(S("pe_p"), 1)
                for c in range(NCH):
                    tt, cp = c // 2, HD * (c % 2)
                    e.wait_ge(S("dve_sbd"), c + 1)
                    if c == 0:
                        e.wait_ge(S("dve_inv"), 13)
                    for pr in range(PR):
                        m = mm(bank(3, P, pr * P), kr[:, pr, tt, 0:P], sbd[:, pr, :], start=True, stop=True)
                    m.then_inc(S("pe_ks"), 1)
                    e.wait_ge(S("dve_pm"), c + 1)
                    for h in range(H):
                        m = mm(bank(4, HD, h * HD), xt[:, tt * H + h, :], pm[:, h * HD:h * HD + HD], start=True, stop=True)
                    m.then_inc(S("pe_u"), 1)
                    e.wait_ge(S("dve_u"), c + 1)
                    if c:
                        e.wait_ge(S("act_y"), c)
                    for pr in range(PR):
                        out = bank(5, CH, pr * CH)
                        mm(out, sbd[:, pr, :], kr[:, pr, tt, P + cp:P + cp + CH], start=True, stop=False)
                        for q in range(2):
                            n = tt * H + 2 * pr + q
                            pad = slice(HD - HD * q, 3 * HD - HD * q)
                            mm(out, upad[:, 2 * pr + q, pad], chunk_m[:, n, P + cp:P + cp + CH], start=False, stop=False)
                            m = mm(out, vpad[:, tt, 2 * pr + q, pad], chunk_m[:, n, 384 + cp:384 + cp + CH], start=False, stop=q == 1)
                    for pr in range(PR):
                        out = bank(6, P, pr * P)
                        mm(out, alt[:, tt, pr * P:pr * P + P], upad[:, 2 * pr:2 * pr + 2, HD:2 * HD], start=True, stop=False)
                        m = mm(out, kbt[:, tt, pr * P:pr * P + P], vc[:, c, pr * P:pr * P + P], start=False, stop=True)
                    m.then_inc(S("pe_s"), 1)

                def causal(mixer, q_, k_tiles, v_tiles):
                    e.wait_ge(S("dve_qk"), mixer + 1)
                    for n, src in enumerate((v_tiles, k_tiles)):
                        for tt in range(TT):
                            for pr in range(PR):
                                m = e.transpose(ps[:, 4 + n, tt * 256 + pr * P:tt * 256 + pr * P + P], src[:, pr, tt * P:tt * P + P], C("ident"))
                    m.then_inc(S("pe_ctr"), 1)
                    e.wait_ge(S("pool_kz"), mixer + 2)
                    for h in range(H):
                        pr, q = divmod(h, 2)
                        b = 6 + h % 2
                        if h >= 2:
                            e.wait_ge(S("dve_att"), 4 * mixer + h - 1)
                        mm(bank(b, SEQ), keyz[:, mixer, q, pr, 0:P], q_[:, pr, 0:SEQ], start=True, stop=True)
                        mm(bank(b, P, SEQ), keyz[:, mixer, q, pr, P:SEQ], q_[:, pr, P:SEQ], start=True, stop=True).then_inc(S("pe_sc"), 1)
                    e.wait_ge(S("act_cv"), mixer + 1)
                    e.wait_ge(S("dve_att"), 4 * mixer + 4)
                    def over_keys(out, late, values):
                        for q, tt in ((0, 0), (0, 1), (1, 1), (1, 0)):
                            h = 2 * pr + q
                            pad = HD - HD * q
                            if tt:
                                m = mm(late, values(tt, h, pad), att[:, h, SEQ:ATT], start=False, stop=False, skip_group_check=True)
                            else:
                                m = mm(out, values(tt, h, pad), att[:, h, 0:SEQ], start=q == 0, stop=q == 1)
                        return m

                    for pr in range(PR):
                        m = over_keys(bank(pr, SEQ), bank(pr, P, P), lambda tt, h, pad: vpad[:, tt, h, pad:pad + P])
                    if mixer:
                        a = CONST_AT["onespad"][0]
                        for pr in range(PR):
                            m = over_keys(bank(2 + pr, SEQ), bank(2 + pr, P, P), lambda tt, h, pad: const[:, a + pad:a + pad + P])
                    m.then_inc(S("pe_co"), 1)
                    e.wait_ge(S("dve_kw"), mixer + 1)
                    for pr in range(PR):
                        for tt in range(TT):
                            m = mm(bank(6, P, pr * P), ktok[:, tt, pr * P:pr * P + P], vpad[:, tt, 2 * pr:2 * pr + 2, HD:2 * HD],
                                   start=tt == 0, stop=tt == TT - 1)
                    if mixer:
                        for pr in range(PR):
                            for tt in range(TT):
                                m = mm(bank(6, 1, 256 + pr), ktok[:, tt, pr * P:pr * P + P], C("ones", 1), start=tt == 0, stop=tt == TT - 1)
                    m.then_inc(S("pe_cf"), 1)

                e.wait_ge(S("act_y"), NCH)
                e.wait_ge(S("dve_sbd"), NCH + 1)
                for t in range(4):
                    m = mm(bank(t), C("rot"), proj[:, 16 + t, :], start=True, stop=True)
                m.then_inc(S("pe_step"), 1)
                causal(0, qr, kq, proj[:, 20:22, :])
                for g in range(2):
                    for kt in range(KT):
                        m = mm(ps[0:4, 2 + g, 0:N], w_if[:, kt, 4 * g:4 * g + 4], xn[:, kt, :], start=kt == 0, stop=kt == KT - 1)
                m.then_inc(S("pe_step"), 1)
                e.wait_ge(S("dve_rows"), 1)
                e.wait_ge(S("act_co"), 1)
                a = CONST_AT["rowsel"][0]
                for h in range(H):
                    mm(bank(h // 2, SEQ, SEQ * (h % 2)), const[0:4, a + h * P:a + h * P + P], rows[0:4, 5, 0:SEQ], start=True, stop=True)
                a = CONST_AT["pairsel"][0]
                for pr in range(PR):
                    mm(bank(2 + pr, 280), const[0:4, a + pr * P:a + pr * P + P], rowx[0:4, 0:280], start=True, stop=True)
                for tt in range(TT):
                    m = e.transpose(ps[:, 4, tt * H:tt * H + H], rows[0:4, 6, tt * P:tt * P + P], C("ident")[0:4, 0:4])
                m.then_inc(S("pe_step"), 1)
                e.wait_ge(S("act_em"), 1)
                causal(1, qr, kq, proj[:, 28:30, :])

                e.wait_ge(S("dve_hg"), 1)
                e.wait_ge(S("act_co"), 2)
                def spread(u, v):
                    e.wait_ge(kv_done, v + 1)
                    e.sem_inc(sel_free, 1)
                    e.wait_ge(sel_full, v + 1)
                    mm(bank(u, 512), sel[:, u, :], proj[:, 12:14, 0:SEQ], start=True, stop=True).then_inc(bank_full[u], 1)

                def gather_out(u, v, start=False, stop=False):
                    e.wait_ge(qs_full, v + 1)
                    e.wait_ge(win_full, v + 1)
                    mm(bank(4, 512), win[:, u, :], qs[:, u, :], start=start, stop=stop).then_inc(qs_free, 1)

                for u in range(4):
                    spread(u, u)
                for u in range(4):
                    spread(u, u + 4)
                    gather_out(u, u, start=u == 0)
                with e.Fori(2, HD // 4) as i:
                    for u in range(4):
                        spread(u, i * 4 + u)
                        gather_out(u, i * 4 - 4 + u)
                for u in range(4):
                    gather_out(u, HD - 4 + u, stop=u == 3)
                e.wait_ge(kv_done, HD + 4)

                e.wait_ge(S("dve_sv"), 1)
                e.wait_ge(S("act_sv"), 1)
                for pr in range(PR):
                    e.transpose(ps[0:NGLA * NS, 5, pr * P:pr * P + P], sv[:, pr, 0:NGLA, :].rearrange("p a b -> p (a b)"), C("ident"))
                    m = e.transpose(ps[0:(NVEC - NGLA) * NS, 6, pr * P:pr * P + P], sv[:, pr, NGLA:NVEC, :].rearrange("p a b -> p (a b)"), C("ident"))
                m.then_inc(S("pe_step"), 1)
                e.wait_ge(S("dve_sa"), 1)
                mm(bank(7, HD), C("quads"), sa, start=True, stop=True).then_inc(S("pe_step"), 1)
                e.wait_ge(S("dve_po"), 1)
                for m_ in range(4):
                    mm(bank(5, 32, 32 * m_), po[:, m_, :, :].rearrange("p a b -> p (a b)"), C("samples"), start=True, stop=True)
                mm(bank(5, 32, 128), pn.to_broadcast([P, P]), C("samples"), start=True, stop=True).then_inc(S("pe_step"), 1)

                e.wait_ge(S("dve_yy"), 1)
                for t in (0, 1, 6, 7):
                    m = mm(bank(t), C("headmean"), yy[:, t, :], start=True, stop=True)
                m.then_inc(S("pe_step"), 1)
                e.wait_ge(S("act_ysq"), 1)
                e.wait_ge(S("dve_yc"), 1)
                for t in range(8):
                    m = mm(bank(t), C("headmean"), rs8[:, t, :], start=True, stop=True)
                m.then_inc(S("pe_step"), 1)

                e.wait_ge(S("act_rt8"), 1)
                e.wait_ge(S("dve_yn"), 1)
                with e.Fori(0, 4) as i:
                    for o in range(2):
                        for m_ in range(4):
                            j = 2 * o + m_ // 2
                            if m_ % 2 == 0:
                                take(e, w_full[j], 16)
                            b = m_ % 2
                            take(e, bank_free[b], 1)
                            for kt in range(KT):
                                at = (m_ % 2) * D + kt * P
                                m = mm(bank(b), ring[:, j, at:at + P], xn[:, kt, :], start=kt == 0, stop=kt == KT - 1)
                            m.then_inc(bank_full[b], 1)
                        if o == 0:
                            take(e, w_full[4], 16)
                        for m_ in range(4):
                            take(e, bank_free[2 + m_], 1)
                            for k in range(2):
                                at = o * D + (2 * m_ + k) * P
                                m = mm(bank(2 + m_), ring[:, 4, at:at + P], yy[:, 2 * m_ + k, :], start=k == 0, stop=k == 1)
                            m.then_inc(bank_full[2 + m_], 1)
                e.wait_ge(S("dve_mg"), 1)

                def project(src, tag, done):
                    for o in range(KT):
                        j = o // 2
                        if o % 2 == 0:
                            take(e, w_full[j], 16)
                        if o >= 2:
                            e.wait_ge(S(done), o - 1)
                        for kt in range(KT):
                            at = (o % 2) * D + kt * P
                            m = mm(bank(o % 2), ring[:, j, at:at + P], src[:, kt, :], start=kt == 0, stop=kt == KT - 1)
                        m.then_inc(S(tag), 1)

                project(merged, "pe_wo", "dve_x")
                sum_squares(sqs, 2)
                e.wait_ge(S("dve_xn"), 2)
                project(xn, "pe_wq", "act_q")
                e.wait_ge(S("dve_qz"), 1)
                for tt in range(3):
                    for g in range(2):
                        b = 2 + 2 * tt + g
                        for k in range(4):
                            kt = 4 * g + k
                            if tt < 2:
                                m = e.transpose(ps[:, b, k * P:k * P + P], xn[:, kt, tt * P:tt * P + P], C("ident"))
                            else:
                                m = mm(bank(b, P, k * P), xrep[:, kt, :], C("ident"), start=True, stop=True)
                m.then_inc(S("pe_step"), 1)
                e.wait_ge(S("act_q"), KT)
                e.wait_ge(S("sp_keys"), 16)
                e.wait_ge(S("dve_qz"), 1)
                e.wait_ge(S("act_xt"), 1)
                for i in range(3):
                    take(e, ps_scores_free, 1)
                    for h in range(PH):
                        m = mm(bank(h // 2, 256, 256 * (h % 2)), qpe[:, h, i * P:i * P + P], keys[:, h, :], start=True, stop=True)
                    m.then_inc(ps_scores, 1)
                take(e, ps_scores_free, 1)
                e.wait_ge(S("dve_acc"), 1)
                for tt in range(TT):
                    for kt in range(KT):
                        e.transpose(ps[:, 2 * tt + kt // 4, (kt % 4) * P:(kt % 4) * P + P], acc[:, tt, kt * P:kt * P + P], C("ident"))
                for kt in range(KT):
                    m = mm(bank(4, NS, NS * kt), acc[:, 2, kt * P:kt * P + P], C("group"), start=True, stop=True)
                m.then_inc(S("pe_step"), 1)
                layer_end(e, "pe")
            sum_squares(sqs, 1)

        @block.scalar
        def _(e):
            own = Own(e, "act_own")
            act = e.activation

            def bank(b, n=N, lo=0, p0=0, p1=P):
                return ps[p0:p1, b, lo:lo + n]

            def eps(i):
                a = CONST_AT["eps"][0]
                return const[:, a + i:a + i + 1]

            def root(k, to):
                e.wait_ge(S("pe_ss"), k)
                act(to, bank(0), ACT.Sqrt, bias=eps(0), scale=1.0 / D).then_inc(S("act_rt"), 1)

            e.wait_ge(S("sp_once"), 48)
            e.wait_ge(S("dve_lb"), 1)
            own(act(lb_all[:, :], lb_all[:, :], ACT.Exp))
            e.sem_inc(S("act_lb"), 1)
            with e.Fori(0, L) as l:
                own.clear()
                root(1, rstd)
                for b in range(2):
                    e.sem_inc(bank_free[b], 1)
                with e.Fori(0, 4) as i:
                    for t in range(8):
                        b = t % 2
                        take(e, bank_full[b], 1)
                        act(proj[:, bass.ds(i * 8 + t, 1), :].rearrange("p a n -> p (a n)"), bank(b), ACT.Copy).then_inc(bank_free[b], 1)
                        if b:
                            e.sem_inc(w_free[t // 2], 1)
                for b in range(2):
                    take(e, bank_free[b], 1)
                e.sem_inc(S("act_proj"), 1)
                e.wait_ge(S("sp_par"), 16 * 9)
                e.wait_ge(S("dve_xs"), 1)
                act(proj[0:HD, 6, :], proj[0:HD, 6, :], ACT.Tanh)
                act(proj[:, 7, :], proj[:, 7, :], ACT.Sigmoid).then_inc(S("act_lr"), 1)
                e.wait_ge(S("pe_step"), step("lr"))
                for pr in range(PR):
                    act(loga[:, pr, :], bank(2 + pr), ACT.Sigmoid, bias=V("w0", pr))
                    act(aa[:, pr, :], bank(4 + pr), ACT.Sigmoid, bias=V("a0", pr)).then_inc(S("act_wa"), 1)
                for pr in range(PR):
                    act(gg[:, pr, :], bank(6 + pr), ACT.Copy).then_inc(S("act_wag"), 1)
                e.wait_ge(S("pe_step"), step("kk"))
                for pr in range(PR):
                    i = act(t1[:, pr, :], bank(pr), ACT.Sqrt)
                i.then_inc(S("act_kk"), 1)
                e.wait_ge(S("dve_cum"), 1)
                act(e_b[:, :, :], al[:, :, :], ACT.Exp)
                act(e_n[:, :, :], al[:, :, :], ACT.Exp, scale=-1.0)
                act(e_p[:, :, :], kb[:, :, :], ACT.Exp).then_inc(S("act_e"), 1)
                act(sv[:, :, RW_W, :], loga[:, :, SEQ:N], ACT.Exp).then_inc(S("act_sv0"), 1)
                e.wait_ge(S("pe_step"), step("tr"))
                e.wait_ge(S("pool_kz"), 1)
                for tt in range(TT):
                    src = bank(4, 256, 256 * tt)
                    act(vpad[:, tt, :, HD:2 * HD], src.rearrange("p (h c) -> p h c", c=HD), ACT.Copy)
                    for q in range(2):
                        act(vc[:, 2 * tt + q, :], src, ACT.Copy, scale=C("rows")[:, q:q + 1])
                    act(alt[:, tt, :], bank(5, 256, 256 * tt), ACT.Copy)
                    i = act(kbt[:, tt, :], bank(6, 256, 256 * tt), ACT.Copy)
                i.then_inc(S("act_vpad"), 1)
                e.wait_ge(S("pe_step"), step("bv"))
                act(bv[:, :, :].rearrange("p a b -> p (a b)"), bank(2, 512), ACT.Copy).then_inc(S("act_bv"), 1)
                for c in range(NCH):
                    e.wait_ge(S("pe_s"), c + 1)
                    act(yy[:, 0:2, c * CH:c * CH + CH], bank(5, 2 * CH).rearrange("p (a b) -> p a b", b=CH), ACT.Copy).then_inc(S("act_y"), 1)

                def causal(mixer):
                    e.wait_ge(S("pe_ctr"), mixer + 1)
                    for tt in range(TT):
                        act(vpad[:, tt, :, HD:2 * HD], bank(4, 256, 256 * tt).rearrange("p (h c) -> p h c", c=HD), ACT.Copy)
                    act(ktok[:, :, :].rearrange("p a b -> p (a b)"), bank(5, 512), ACT.Copy).then_inc(S("act_cv"), 1)
                    e.wait_ge(S("pe_co"), mixer + 1)
                    for pr in range(PR):
                        act(yy[:, 4 + 2 * mixer + pr, 0:SEQ], bank(pr, SEQ), ACT.Copy)
                        if mixer:
                            act(denk[:, pr, 0:SEQ], bank(2 + pr, SEQ), ACT.Abs)
                    e.wait_ge(S("pe_cf"), mixer + 1)
                    if mixer:
                        e.wait_ge(S("sp_dfin"), 16)
                        act(nfin, bank(6, PR, 256), ACT.Copy)
                    act(sfin[:, :, :].rearrange("p a b -> p (a b)"), bank(6, 256), ACT.Copy).then_inc(S("act_co"), 1)
                    e.wait_ge(S("act_co"), mixer + 1)
                    e.dma_start(O["p_ret" if not mixer else "p_ml"][bass.ds(l, 1)].rearrange("a p c -> p (a c)"), sfin[:, :, :].rearrange("p a b -> p (a b)")).then_inc(S("sp_dfin"), 16)
                    if mixer:
                        e.dma_start(O["p_n"][bass.ds(l, 1)].rearrange("a p c -> p (a c)"), nfin).then_inc(S("sp_dfin"), 16)

                causal(0)
                e.wait_ge(S("pe_step"), step("if"))
                act(rows[0:4, 0, :], ps[0:4, 2, 0:N], ACT.Identity, bias=V("ig_b")[0:4, :])
                act(rows[0:4, 1, :], ps[0:4, 3, 0:N], ACT.Identity, bias=V("fg_b")[0:4, :]).then_inc(S("act_r0"), 1)
                e.wait_ge(S("dve_r1"), 1)
                own(act(rows[0:4, 3, :], rows[0:4, 2, :], ACT.Exp, scale=-1.0))
                act(rows[0:4, 3, :], rows[0:4, 3, :], ACT.Ln, bias=const[0:4, CONST_AT["eps"][0] + 3:CONST_AT["eps"][0] + 4]).then_inc(S("act_r2"), 1)
                e.wait_ge(S("dve_cv"), 1)
                for t in range(4):
                    dst, src = (qr, kq)[t // 2][:, t % 2, :], cv[:, t, :]
                    act(dst[:, 0:SEQ], src[:, 0:SEQ], ACT.Silu, bias=V("cb", t))
                    act(dst[:, SEQ:N], src[:, SEQ:288].rearrange("p (b j) -> p b j", j=4)[:, :, 3], ACT.Silu, bias=V("cb", t)).then_inc(S("act_silu"), 1)
                act(out_conv[:, :, 0, :], cpad[:, :, SEQ:SEQ + 3], ACT.Copy)
                for t in range(4):
                    i = act(out_conv[:, t, 1:NS + 1, :], cpad[:, t, SEQ + 3:].rearrange("p (b j) -> p b j", j=4)[:, :, 1:4], ACT.Copy)
                i.then_inc(S("act_conv"), 1)
                e.wait_ge(S("pe_step"), step("rows"))
                for pr in range(PR):
                    act(emk[:, pr, :], bank(2 + pr), ACT.Exp, scale=-1.0)
                    i = act(fa[:, pr, :], bank(2 + pr, 2 * NS, N), ACT.Exp)
                i.then_inc(S("act_em"), 1)
                e.wait_ge(S("dve_dt"), 1)
                act(att[:, :, :], att[:, :, :], ACT.Exp).then_inc(S("act_dt"), 1)
                causal(1)
                e.wait_ge(S("sp_dfin"), 48)
                for t, n in ((10, 0), (11, 1)):
                    act(sgn[:, n, :], proj[:, t, :], ACT.Sigmoid, scale=-1.0)
                for t in (10, 11, ):
                    own(act(proj[:, t, :], proj[:, t, :], ACT.Sigmoid))
                act(proj[:, 8:10, :], proj[:, 8:10, :], ACT.Silu).then_inc(S("act_hg"), 1)
                e.wait_ge(S("sp_rw"), 16)
                with e.Fori(0, HD // 4) as i:
                    for u in range(4):
                        e.wait_ge(sel_free, i * 4 + u + 1)
                        e.sem_inc(S("act_turn"), 1)
                        act(sel[:, u, :], C("headsum"), ACT.Copy, scale=const[:, bass.ds(CONST_AT["channel"][0] + i * 4 + u, 1)]).then_inc(sel_full, 1)
                        e.wait_ge(win_free, i * 4 + u + 1)
                        e.sem_inc(S("act_turn"), 1)
                        act(win[:, u, :], const[:, bass.ds(CONST_AT["place"][0] + HD - 1 - i * 4 - u, P)], ACT.Copy).then_inc(win_full, 1)
                e.wait_ge(S("dve_sv"), 1)
                act(sv[:, :, V_Q, :], proj[:, 8:10, SEQ:N], ACT.Copy)
                act(sv[:, :, V_V, :], proj[:, 12:14, SEQ:N], ACT.Copy)
                act(sv[:, :, V_V + 1, :], proj[:, 20:22, SEQ:N], ACT.Copy)
                act(sv[:, :, V_V + 2, :], proj[:, 28:30, SEQ:N], ACT.Copy).then_inc(S("act_sv"), 1)
                e.wait_ge(S("dve_y2"), 1)
                e.wait_ge(S("pe_step"), step("svt"))
                e.wait_ge(S("sp_hfin"), 16)
                act(svt[0:NGLA * NS, :, :].rearrange("p a b -> p (a b)"), bank(5, 256, p1=NGLA * NS), ACT.Copy)
                act(svt2[0:(NVEC - NGLA) * NS, :, :].rearrange("p a b -> p (a b)"), bank(6, 256, p1=(NVEC - NGLA) * NS), ACT.Copy).then_inc(S("act_svt"), 1)
                act(proj[:, 14:16, :], proj[:, 14:16, :], ACT.Silu)
                act(proj[:, 22:24, :], proj[:, 22:24, :], ACT.Silu)
                act(proj[:, 30:32, :], proj[:, 30:32, :], ACT.Sigmoid).then_inc(S("act_og"), 1)
                e.wait_ge(S("dve_yc"), 1)
                act(rs8[:, :, :], yy[:, :, :], ACT.Square).then_inc(S("act_ysq"), 1)
                e.wait_ge(S("pe_step"), step("var"))
                for t in range(8):
                    i = act(fg8[:, t, :], bank(t), ACT.Sqrt, bias=eps(1 if t < 2 else 2))
                i.then_inc(S("act_rt8"), 1)
                for b in range(6):
                    e.sem_inc(bank_free[b], 1)
                with e.Fori(0, 4) as i:
                    for o in range(2):
                        take(e, gate_free[o], 1)
                        for m_ in range(4):
                            b = m_ % 2
                            take(e, bank_full[b], 1)
                            a = act(gate4[:, o, m_, :], bank(b), ACT.Sigmoid)
                            a.then_inc(bank_free[b], 1)
                            if m_ % 2:
                                e.sem_inc(w_free[2 * o + m_ // 2], 1)
                        act(small[:, 0:1], small[:, 0:1], ACT.Copy).then_inc(gate_full[o], 1)
                for b in range(2):
                    take(e, bank_free[b], 1)
                root(2, rstd)
                for o in range(KT):
                    e.wait_ge(S("pe_wq"), o + 1)
                    act(qpe[:, o, 0:N], bank(o % 2), ACT.Copy).then_inc(S("act_q"), 1)
                    if o % 2:
                        e.sem_inc(w_free[o // 2], 1)
                e.wait_ge(S("pe_step"), step("xt"))
                for tt in range(3):
                    for g in range(2):
                        i = act(xtok[:, tt, g * 512:g * 512 + 512], bank(2 + 2 * tt + g, 512), ACT.Copy)
                i.then_inc(S("act_xt"), 1)
                e.sem_inc(ps_scores_free, 1)
                with e.Fori(0, 3) as i:
                    take(e, ps_scores, 1)
                    take(e, scores_free, 1)
                    for b in range(4):
                        a = act(sc[:, 4 * b:4 * b + 4, :].rearrange("p a b -> p (a b)"), bank(b, 512), ACT.Copy)
                    a.then_inc(scores, 1)
                    take(e, top_full, 1)
                    act(t16[:, :, :], t16[:, :, :], ACT.Exp).then_inc(top_exp, 1)
                def gelu(h):
                    take(e, hid_full[h], 1)
                    act(hge[:, h, :], hid[:, h, :], ACT.Gelu).then_inc(hid_gelu[h], 1)
                for tt in range(TT):
                    with e.Fori(0, 16) as _i:
                        gelu(0)
                        gelu(1)
                gelu(0)
                gelu(1)
                layer_end(e, "act")
            root(1, rstd)

        @block.gpsimd
        def _(e):
            own = Own(e, "pool_own")
            tt_ = e.tensor_tensor
            for t in (keyz, vpad, upad):
                n = len(t.shape) - 1
                names = " ".join(f"d{i}" for i in range(n))
                idx = tuple(slice(None) for _ in t.shape)
                i = e.memset(t[idx].rearrange(f"p {names} -> p ({names})"), 0.0)
                i.then_inc(S("pool_zero"), 1)
            e.wait_ge(S("pool_zero"), 3)
            for j in range(2):
                e.sem_inc(u_free[j], 1)
                e.sem_inc(v_free[j], 1)
            with e.Fori(0, L) as l:
                own.clear()

                def by_head(n, src):
                    for q in range(2):
                        h = slice(HD * q, HD * q + HD)
                        i = e.tensor_copy(keyz[h, n, q, :, :], src[h, :, :])
                    return i

                e.wait_ge(S("dve_kr"), 1)
                e.wait_ge(S("pool_zero"), 3)
                by_head(0, al)
                by_head(1, kb).then_inc(S("pool_kz"), 1)
                e.wait_ge(S("dve_qk"), 1)
                e.wait_ge(S("pe_cm"), 8)
                by_head(0, kq[:, :, 0:SEQ]).then_inc(S("pool_kz"), 1)
                e.wait_ge(S("dve_qk"), 2)
                by_head(1, kq[:, :, 0:SEQ]).then_inc(S("pool_kz"), 1)
                e.wait_ge(S("dve_hg"), 1)
                e.sem_inc(qs_free, 4)
                with e.Fori(0, HD // 4) as i:
                    own.clear()
                    for u in range(4):
                        e.wait_ge(qs_free, i * 4 + u + 1)
                        e.sem_inc(win_free, 1)
                        e.wait_ge(ss_full, i * 4 + u + 1)
                        tt_(qs[:, u, :], ss[:, u, :], qp[:, :, :].rearrange("p a b -> p (a b)"), ALU.mult).then_inc(qs_full, 1)
                        e.tensor_copy(hfin[:, bass.ds(i * 4 + u, 1), :].rearrange("p a b -> p (a b)"), ss[:, u, SEQ - 1::SEQ]).then_inc(ss_free, 1)
                own.clear()
                e.wait_ge(qs_free, HD + 4)
                e.wait_ge(ss_free, HD + 4)
                e.sem_inc(S("pool_hf"), 1)
                e.wait_ge(S("sp_svr"), 16 * 5)
                e.wait_ge(S("sp_par"), 16 * 9)
                rw = st[:, 3, :, :]

                def over_v(v, n=1):
                    return bc(gv[:, v:v + n, :], 3, [P, n, 16, HD]) if n > 1 else bc(gv[:, v, :], 2, [P, 16, HD])

                own(tt_(big2, rw, over_v(RW_KK), ALU.mult))
                e.sem_inc(S("pool_sa"), 1)
                gla = st[:, 0:3, :, :]
                own(tt_(gla, gla, over_v(V_F, 3), ALU.mult))
                for m in range(3):
                    i = tt_(big1[:, m, :, :], over_v(V_K + m), bc(gvv[:, m, :], 1, [P, 16, HD]), ALU.mult)
                own(i)
                own(tt_(gla, gla, big1, ALU.add))
                own(tt_(big1, gla, over_v(V_Q, 3), ALU.mult))
                own(tt_(st_n[:, :], st_n[:, :], gv[:, V_F + 2, :], ALU.mult))
                own(tt_(st_n[:, :], st_n[:, :], gv[:, V_K + 2, :], ALU.add))
                own(tt_(nq, st_n[:, :], gv[:, V_Q + 2, :], ALU.mult))
                e.sem_inc(S("pool_gla"), 1)
                own(tt_(rw, rw, over_v(RW_W), ALU.mult))
                e.wait_ge(S("dve_sa"), 2)
                own(tt_(big2, over_v(RW_KKA), bc(sab, 1, [P, 16, HD]), ALU.mult))
                own(tt_(rw, rw, big2, ALU.add))
                own(tt_(big2, over_v(RW_K), bc(gvv[:, 3, :], 1, [P, 16, HD]), ALU.mult))
                own(tt_(rw, rw, big2, ALU.add))
                own(tt_(big2, rw, over_v(RW_R), ALU.mult))
                e.sem_inc(S("pool_st"), 1)
                e.sem_inc(S("pool_rw"), 1)
                e.wait_ge(S("dve_route"), 1)
                e.wait_ge(S("sp_sr"), 32)
                u_rows = A["peer_u"]
                v_rows = A["peer_v"]
                own.clear()

                def fetch(h, src, table, rows_, ix, full, free):
                    take(e, free[h], 1)
                    own(e.tensor_copy(ix[:, h, :], src))
                    for j in range(4):
                        e.indirect_dma_start(out=rows_[:, 4 * h + j, :], out_offset=None, in_=table,
                                             in_offset=bass.IndirectOffsetOnAxis(ap=ix[:, h, j:j + 1], axis=0)).then_inc(full[h], 16)

                for tt in range(TT):
                    with e.Fori(0, 16) as i:
                        own.clear()
                        for h in range(2):
                            src = eidx[:, tt, bass.ds(i * 8 + 4 * h, 4)].bitcast(U32)
                            fetch(h, src, u_rows, urows, ixu, u_full, u_free)
                            fetch(h, src, v_rows, vrows, ixv, v_full, v_free)
                    own.clear()
                for h in range(2):
                    fetch(h, es[:, 4 * h:4 * h + 4], u_rows, urows, ixu, u_full, u_free)
                    fetch(h, es[:, 4 * h:4 * h + 4], v_rows, vrows, ixv, v_full, v_free)
                layer_end(e, "pool")

        @block.vector
        def _(e):
            own = Own(e, "dve_own")
            tt_, ts, stt = e.tensor_tensor, e.tensor_scalar, e.scalar_tensor_tensor

            def bank(b, n=N, lo=0, p0=0, p1=P):
                return ps[p0:p1, b, lo:lo + n]

            def squares(sq_):
                tt_(sq_[:, :, :], x[:, :, :], x[:, :, :], ALU.mult).then_inc(S("dve_sq"), 1)

            def norm(k, gain):
                e.wait_ge(S("act_rt"), k)
                own(e.reciprocal(rstd, rstd))
                for kt in range(KT):
                    i = stt(xn[:, kt, :], x[:, kt, :], gain(kt), rstd, ALU.mult, ALU.mult)
                i.then_inc(S("dve_xn"), 1)

            e.memset(layer_off[:, :], 0.0)
            own(e.memset(small[:, :], 0.0))
            e.wait_ge(S("sp_once"), 48)
            lg = glob[:, 8:8 + 2 * L].rearrange("p (a b) -> p a b", b=PR)
            la = lb_all[:, :].rearrange("p (a b) -> p a b", b=PR)
            own(tt_(small[:, 0:2], lg[:, 0, :], lg[:, 1, :], ALU.max))
            tt_(la, lg, bc(small[:, 0:2], 1, [P, L, PR]), ALU.subtract).then_inc(S("dve_lb"), 1)
            e.wait_ge(S("act_lb"), 1)
            own(tt_(small[:, 2:4], la[:, 0, :], la[:, 1, :], ALU.add))
            own(e.reciprocal(small[:, 2:4], small[:, 2:4]))
            own(tt_(la, la, bc(small[:, 2:4], 1, [P, L, PR]), ALU.mult))
            own(tt_(la[:, 1, :], la[:, 1, :], la[:, 0, :], ALU.add))
            own(tt_(la[:, 1, :], la[:, 1, :], la[:, 0, :], ALU.subtract))
            own(tt_(la[:, 0, :], la[:, 0, :], la[:, 0, :], ALU.subtract))
            with e.Fori(0, L) as l:
                own.clear()
                squares(sqs)
                e.wait_ge(S("sp_par"), 16 * 9)
                norm(1, lambda kt: V("ln1", kt))
                own(ts(lb[:, 0, :], lb_all[:, bass.ds(l * PR, PR)], 1e-30, None, ALU.max))
                own(ts(lb[:, 1, :], lb_all[:, bass.ds(l * PR, PR)], -1.0, 1.0, ALU.mult, ALU.add))
                own(tt_(lb[:, 2, :], lb[:, 0, :], lb_all[:, bass.ds(l * PR, PR)], ALU.subtract))

                e.wait_ge(S("act_proj"), 1)
                raw = proj[:, 0:8, :]
                e.tensor_copy(out_shift[:, :, :], raw[:, :, SEQ - 1:N]).then_inc(S("dve_shift"), 1)
                tt_(diff[:, :, 1:SEQ], raw[:, :, 0:SEQ - 1], raw[:, :, 1:SEQ], ALU.subtract)
                ts(diff[:, :, 0:1], raw[:, :, 0:1], -1.0, None, ALU.mult)
                own(tt_(diff[:, :, SEQ:N], st_shift[:, :, :], raw[:, :, SEQ:N], ALU.subtract))
                for t in (6, 7, 0, 1, 2, 3, 4, 5):
                    i = stt(proj[:, t, :], diff[:, t, :], V("mu", t), proj[:, t, :], ALU.mult, ALU.add)
                    if t == 7:
                        i.then_inc(S("dve_xs"), 1)
                own(i)
                r, k, v = proj[:, 0:2, :], proj[:, 2:4, :], proj[:, 4:6, :]
                for pr in range(PR):
                    i = ts(kk[:, pr, :], k[:, pr, :], V("kk", pr), None, ALU.mult)
                own(i)
                tt_(t1, kk, kk, ALU.mult).then_inc(S("dve_kk2"), 1)
                e.wait_ge(S("act_kk"), 1)
                own(ts(t1, t1, 1e-12, None, ALU.max))
                own(e.reciprocal(t1, t1))
                own(tt_(kk, kk, t1, ALU.mult))
                e.wait_ge(S("act_wa"), 2)
                for pr in range(PR):
                    i = ts(kn[:, pr, :], aa[:, pr, :], 1.0, V("ka", pr), ALU.subtract, ALU.mult)
                ts(loga, loga, -float(np.exp(-0.5)), None, ALU.mult)
                own(i)
                own(stt(kn, kn, 1.0, k, ALU.add, ALU.mult))
                for pr in range(PR):
                    own(stt(t1[:, pr, :], r[:, pr, :], V("rk", pr), kn[:, pr, :], ALU.mult, ALU.mult))
                e.sem_inc(S("dve_rk"), 1)
                for pr in range(PR):
                    i = e.tensor_tensor_scan(al[:, pr, :], C("chunkstart"), loga[:, pr, 0:SEQ], 0.0, ALU.mult, ALU.add)
                own(i)
                tt_(kb, al, loga[:, :, 0:SEQ], ALU.subtract).then_inc(S("dve_cum"), 1)
                tt_(kka, kk, aa, ALU.mult)
                for n, src in ((RW_K, kn), (RW_R, r), (RW_KK, kk), (RW_V, v)):
                    e.tensor_copy(sv[:, :, n, :], src[:, :, SEQ:N])
                own(tt_(sv[:, :, RW_KKA, :], kk[:, :, SEQ:N], aa[:, :, SEQ:N], ALU.mult))
                e.wait_ge(S("act_e"), 1)
                q4 = lambda t: t[:, :, 0:SEQ].rearrange("p a (b c) -> p a b c", c=P)
                tt_(kr[:, :, :, 0:P], q4(kk), q4(e_p), ALU.mult)
                tt_(kr[:, :, :, P:256], q4(r), q4(e_b), ALU.mult)
                tt_(al, kka[:, :, 0:SEQ], e_n, ALU.mult)
                tt_(kb, kn[:, :, 0:SEQ], e_n, ALU.mult).then_inc(S("dve_kr"), 1)
                e.wait_ge(S("pe_step"), step("rk"))
                for pr in range(PR):
                    i = tt_(vb[:, pr, :], bank(2 + pr), v[:, pr, :], ALU.mult)
                own(i)
                e.wait_ge(S("act_vpad"), 1)
                e.wait_ge(S("pool_kz"), 1)
                for n in range(TT * H):
                    e.wait_ge(S("pe_cm"), n + 1)
                    tt_(chunk_m[:, n, :], bank((7, 0, 1)[n % 3], 512), C("chunkmask"), ALU.mult).then_inc(S("dve_cm"), 1)
                e.wait_ge(S("dve_cm"), 8)
                e.wait_ge(S("act_sv0"), 1)
                ident8 = bc(C("ident"), 1, [P, 8, P])
                e.tensor_copy(xm, ident8)
                e.tensor_copy(xt, ident8).then_inc(S("dve_inv"), 1)
                for k_ in range(6):
                    lev = CONST_AT["levels"][0] + k_ * P
                    for tt in range(TT):
                        e.wait_ge(S("pe_t"), 2 * k_ + tt + 1)
                        tt_(rr[:, tt, :, :], bank(3 + tt, 512).rearrange("p (a b) -> p a b", b=P), bc(const[:, lev:lev + P], 1, [P, H, P]), ALU.mult)\
                            .then_inc(S("dve_r"), 1)
                    for tt in range(TT):
                        e.wait_ge(S("pe_p"), 2 * k_ + tt + 1)
                        for b, m_ in ((5 + tt, xm), ((7, 0)[tt], xt)):
                            d = m_[:, tt * H:tt * H + H, :].rearrange("p a b -> p (a b)")
                            i = tt_(d, d, bank(b, 512), ALU.add)
                        i.then_inc(S("dve_inv"), 1)
                e.wait_ge(S("dve_inv"), 13)
                own(e.memset(sbd, 0.0))
                e.sem_inc(S("dve_sbd"), 1)
                e.wait_ge(S("act_bv"), 1)
                for c in range(NCH):
                    tt, q = divmod(c, 2)
                    e.wait_ge(S("pe_ks"), c + 1)
                    tt_(pm, bank(3, 256), bv[:, tt, :], ALU.add).then_inc(S("dve_pm"), 1)
                    e.wait_ge(S("pe_u"), c + 1)
                    ts(upad[:, :, HD:2 * HD], bank(4, 256).rearrange("p (h c) -> p h c", c=HD), C("rows")[:, 2 + q:3 + q], None, ALU.mult)\
                        .then_inc(S("dve_u"), 1)
                    e.wait_ge(S("pe_s"), c + 1)
                    own(tt_(sb1, sbd, bank(6, 256).rearrange("p (a b) -> p a b", b=P), ALU.add))
                    for pr in range(PR):
                        at = c * CH + CH - 1
                        i = stt(sbd[:, pr, :], sb1[:, pr, :], e_b[:, pr, at:at + 1], C("headsum"), ALU.mult, ALU.mult)
                    i.then_inc(S("dve_sbd"), 1)
                e.wait_ge(S("dve_sbd"), NCH + 1)
                e.wait_ge(S("act_y"), NCH)
                e.wait_ge(S("pe_step"), step("rot"))
                for t in range(4):
                    sc_ = 1.0 if t < 2 else HD ** -0.5
                    dst = (qr, kq)[t // 2][:, t % 2, :]
                    stt(u1[:, 0, :], proj[:, 16 + t, :], sc_, C("cos"), ALU.mult, ALU.mult)
                    own(stt(u2[:, 0, :], bank(t), sc_, C("sin"), ALU.mult, ALU.mult))
                    i = tt_(dst, u1[:, 0, :], u2[:, 0, :], ALU.add)
                    own(i)
                for n, src in ((V_K + 1, kq), (V_Q + 1, qr)):
                    e.tensor_copy(sv[:, :, n, :], src[:, :, SEQ:N])
                own(e.tensor_copy(sv[:, :, V_F + 1, :], bc(C("decay_chan"), 2, [P, PR, NS])))
                e.sem_inc(S("dve_qk"), 1)

                def causal(mixer, last):
                    for h in range(H):
                        e.wait_ge(S("pe_sc"), 4 * mixer + h + 1)
                        a = CONST_AT["decay"][0] + h * ATT
                        d = att[:, h, :] if mixer else const[:, a:a + ATT]
                        tt_(att[:, h, :], bank(6 + h % 2, ATT), d, ALU.mult).then_inc(S("dve_att"), 1)
                    e.wait_ge(S("act_cv"), mixer + 1)
                    kt4 = ktok[:, :, :].rearrange("p a (h c) -> p a h c", c=HD)
                    for tt in range(TT):
                        i = tt_(kt4[:, tt, :, :], kt4[:, tt, :, :], bc(last(tt), 2, [P, H, HD]), ALU.mult)
                    i.then_inc(S("dve_kw"), 1)

                a_end = CONST_AT["decay_end"][0]
                causal(0, lambda tt: const[:, a_end + tt * H:a_end + tt * H + H])
                R = lambda n, lo=0, hi=N: rows[0:4, n, lo:hi]
                e.wait_ge(S("act_r0"), 1)
                own(stt(R(2), R(1), -1.0, R(1), ALU.mult, ALU.max))
                e.sem_inc(S("dve_r1"), 1)
                e.wait_ge(S("act_co"), 1)
                e.memset(cpad[:, :, 0:3], 0.0)
                e.tensor_copy(cpad[:, :, 3:SEQ + 3], proj[:, 24:28, 0:SEQ])
                for t in range(4):
                    own_s = cpad[:, t, SEQ + 3:].rearrange("p (b j) -> p b j", j=4)
                    e.tensor_copy(own_s[:, :, 0:3], st_conv[:, t, :, :])
                    i = e.tensor_copy(own_s[:, :, 3:4], proj[:, 24 + t, SEQ:N].unsqueeze(2))
                own(i)
                for j in range(4):
                    for t in range(4):
                        w = V("cw", 4 * t + j)
                        src = cpad[:, t, j:j + 288]
                        i = ts(cv[:, t, :], src, w, None, ALU.mult) if j == 0 else stt(cv[:, t, :], src, w, cv[:, t, :], ALU.mult, ALU.add)
                    if j < 3:
                        own(i)
                i.then_inc(S("dve_cv"), 1)
                e.wait_ge(S("act_r2"), 1)
                own(stt(R(4), R(1), 0.0, R(3), ALU.min, ALU.subtract))
                zero4 = const[0:4, CONST_AT["zero"][0]:CONST_AT["zero"][0] + SEQ]
                own(e.tensor_tensor_scan(R(7, 0, SEQ), R(4, 0, SEQ), zero4, 0.0, ALU.add, ALU.add))
                own(e.tensor_tensor_scan(rowx[0:4, 0:SEQ], R(4, 0, SEQ), R(0, 0, SEQ), 0.0, ALU.add, ALU.max))
                tt_(R(5, 0, SEQ), R(7, 0, SEQ), rowx[0:4, 0:SEQ], ALU.subtract)
                tt_(R(6, 0, SEQ), R(0, 0, SEQ), R(7, 0, SEQ), ALU.subtract)
                own(tt_(R(8, 0, NS), R(4, SEQ, N), m_old[:, :], ALU.add))
                own(tt_(rowx[0:4, SEQ:N], R(8, 0, NS), R(0, SEQ, N), ALU.max))
                tt_(rowx[0:4, N:N + NS], R(8, 0, NS), rowx[0:4, SEQ:N], ALU.subtract)
                tt_(rowx[0:4, N + NS:N + 2 * NS], R(0, SEQ, N), rowx[0:4, SEQ:N], ALU.subtract)
                own(e.tensor_copy(out_m[:, :], rowx[0:4, SEQ - 1:N]))
                e.sem_inc(S("dve_rows"), 1)
                e.wait_ge(S("act_silu"), 4)
                own(ts(kq, kq, HD ** -0.5, None, ALU.mult))
                e.wait_ge(S("act_em"), 1)
                own(e.tensor_copy(ccol, bank(4, 2 * H).rearrange("p (a b) -> p a b", b=H)))
                e.tensor_copy(sv[:, :, V_Q + 2, :], qr[:, :, SEQ:N])
                e.tensor_copy(sv[:, :, V_F + 2, :], fa[:, :, 0:NS])
                tt_(sv[:, :, V_K + 2, :], kq[:, :, SEQ:N], fa[:, :, NS:2 * NS], ALU.mult)
                for h in range(H):
                    src = bank(h // 2, SEQ, SEQ * (h % 2))
                    ts(att[:, h, 0:SEQ], src, ccol[:, 0, h:h + 1], 0.0, ALU.add, ALU.min)
                    i = ts(att[:, h, SEQ:ATT], src[:, P:SEQ], ccol[:, 1, h:h + 1], 0.0, ALU.add, ALU.min)
                own(i)
                e.sem_inc(S("dve_dt"), 1)
                e.sem_inc(S("dve_qk"), 1)
                e.wait_ge(S("act_dt"), 1)
                own(tt_(att, att, bc(C("causal"), 1, [P, H, ATT]), ALU.mult))
                e.tensor_copy(small[:, 16:20], att[:, :, SEQ - 1])
                own(e.tensor_copy(small[:, 20:24], att[:, :, ATT - 1]))
                causal(1, lambda tt: small[:, 16 + 4 * tt:20 + 4 * tt])
                e.wait_ge(S("act_hg"), 1)
                for pr in range(PR):
                    ts(proj[:, 10 + pr, :], proj[:, 10 + pr, :], lb[:, 1, pr:pr + 1], lb[:, 0, pr:pr + 1], ALU.mult, ALU.add)
                    i = ts(sgn[:, pr, :], sgn[:, pr, :], lb[:, 1, pr:pr + 1], lb[:, 2, pr:pr + 1], ALU.mult, ALU.subtract)
                own(i)
                e.tensor_copy(sv[:, :, V_F, :], proj[:, 10:12, SEQ:N])
                e.tensor_copy(sv[:, :, V_K, :], sgn[:, :, SEQ:N])
                e.tensor_copy(qp, proj[:, 8:10, 0:SEQ])
                e.tensor_copy(kp, sgn[:, :, 0:SEQ])
                own(e.tensor_copy(fp, proj[:, 10:12, 0:SEQ]))
                own(e.memset(fp[:, :, 0:1], 0.0))
                e.sem_inc(kv_done, 4)
                e.sem_inc(ss_free, 4)
                e.sem_inc(S("dve_hg"), 1)
                e.sem_inc(S("dve_sv"), 1)
                flat = lambda t: t[:, :, :].rearrange("p a b -> p (a b)")
                with e.Fori(0, HD // 4) as i:
                    own.clear()
                    for u in range(4):
                        take(e, bank_full[u], 1)
                        e.wait_ge(ss_free, i * 4 + u + 1)
                        tt_(kv[:, u, :], bank(u, 512), flat(kp), ALU.mult).then_inc(kv_done, 1)
                        e.wait_ge(kv_done, i * 4 + u + 5)
                        e.tensor_tensor_scan(ss[:, u, :], flat(fp), kv[:, u, :], 0.0, ALU.mult, ALU.add).then_inc(ss_full, 1)
                own.clear()
                e.wait_ge(S("sp_hfin"), 16)
                own(e.tensor_copy(yy[:, 2:4, 0:SEQ], bank(4, 512).rearrange("p (a b) -> p a b", b=SEQ)))
                e.sem_inc(S("dve_y2"), 1)

                e.wait_ge(S("pool_sa"), 1)
                e.tensor_reduce(sa, big2.rearrange("p k v -> p v k"), AX_X, ALU.add).then_inc(S("dve_sa"), 1)
                e.wait_ge(S("pe_step"), step("sa"))
                ts(sab, bank(7, HD), -1.0, None, ALU.mult).then_inc(S("dve_sa"), 1)
                e.wait_ge(S("pool_gla"), 1)
                for m in range(3):
                    e.tensor_reduce(po[:, m, 0, :], big1[:, m, :, :].rearrange("p k v -> p v k"), AX_X, ALU.add)
                e.tensor_reduce(pn, nq, AX_X, ALU.add)
                e.wait_ge(S("pool_rw"), 1)
                own(e.tensor_reduce(po[:, 3, 0, :], big2.rearrange("p k v -> p v k"), AX_X, ALU.add))
                e.tensor_copy(po[:, :, 1, :], po[:, :, 0, :]).then_inc(S("dve_po"), 1)
                e.wait_ge(S("pe_step"), step("po"))
                for q in range(2):
                    p0, p1 = HD * q, HD * q + HD
                    part = lambda lo, n: bank(5, n * 2 * NS, lo, p0, p1).rearrange("p (a q b) -> p a q b", q=2, b=NS)[:, :, q, :]
                    e.tensor_copy(yy[p0:p1, 2:8, SEQ:N], part(0, 6))
                    e.tensor_copy(yy[p0:p1, 0:2, SEQ:N], part(96, 2))
                    i = e.tensor_copy(denk[p0:p1, :, SEQ:N], part(128, 2))
                own(i)
                own(stt(denk, denk, -1.0, denk, ALU.mult, ALU.max))
                own(tt_(denk, denk, emk, ALU.max))
                own(e.reciprocal(denk, denk))
                own(tt_(yy[:, 6:8, :], yy[:, 6:8, :], denk, ALU.mult))
                e.sem_inc(S("dve_yy"), 1)
                e.wait_ge(S("pe_step"), step("mean"))
                for t in (0, 1, 6, 7):
                    i = tt_(yy[:, t, :], yy[:, t, :], bank(t), ALU.subtract)
                own(i)
                e.sem_inc(S("dve_yc"), 1)
                e.wait_ge(S("act_rt8"), 1)
                e.wait_ge(S("act_og"), 1)
                own(e.reciprocal(fg8, fg8))
                own(tt_(yy, yy, fg8, ALU.mult))
                for pr in range(PR):
                    i = ts(yy[:, pr, :], yy[:, pr, :], V("ln_g", pr), V("ln_b", pr), ALU.mult, ALU.add)
                    stt(yy[:, 2 + pr, :], yy[:, 2 + pr, :], V("hg", pr), proj[:, 14 + pr, :], ALU.mult, ALU.mult)
                    stt(yy[:, 6 + pr, :], yy[:, 6 + pr, :], V("mg", pr), proj[:, 30 + pr, :], ALU.mult, ALU.mult)
                tt_(yy[:, 4:6, :], yy[:, 4:6, :], proj[:, 22:24, :], ALU.mult)
                own(i)
                own(tt_(yy[:, 0:2, :], yy[:, 0:2, :], vb, ALU.add))
                own(tt_(yy[:, 0:2, :], yy[:, 0:2, :], gg, ALU.mult))
                e.sem_inc(S("dve_yn"), 1)
                for o in range(2):
                    e.sem_inc(gate_free[o], 1)
                with e.Fori(0, 4) as i:
                    own.clear()
                    for o in range(2):
                        take(e, gate_full[o], 1)
                        for m in range(4):
                            take(e, bank_full[2 + m], 1)
                            own(tt_(gate4[:, o, m, :], gate4[:, o, m, :], bank(2 + m), ALU.mult))
                            e.sem_inc(bank_free[2 + m], 1)
                        own(tt_(gate4[:, o, 0:2, :], gate4[:, o, 0:2, :], gate4[:, o, 2:4, :], ALU.add))
                        own(tt_(merged[:, bass.ds(i * 2 + o, 1), :].rearrange("p a n -> p (a n)"), gate4[:, o, 0, :], gate4[:, o, 1, :], ALU.add))
                        e.sem_inc(gate_free[o], 1)
                    e.sem_inc(w_free[4], 1)
                for o in range(2):
                    take(e, gate_free[o], 1)
                for m in range(4):
                    take(e, bank_free[2 + m], 1)
                own.clear()
                e.sem_inc(S("dve_mg"), 1)
                for o in range(KT):
                    e.wait_ge(S("pe_wo"), o + 1)
                    tt_(x[:, o, :], x[:, o, :], bank(o % 2), ALU.add).then_inc(S("dve_x"), 1)
                    if o % 2:
                        e.sem_inc(w_free[o // 2], 1)
                e.wait_ge(S("dve_x"), KT)
                squares(sqs)
                norm(2, lambda kt: V("ln2", kt))
                e.wait_ge(S("dve_xn"), 2)
                own(e.memset(qpe[:, :, N:NQ], 0.0))
                own(e.tensor_copy(xrep.rearrange("p a (b c) -> p a b c", c=16), bc(xn[:, :, SEQ:N], 3, [P, KT, NS, 16])))
                e.sem_inc(S("dve_qz"), 1)
                e.sem_inc(scores_free, 1)
                with e.Fori(0, 3) as i:
                    own.clear()
                    take(e, scores, 1)
                    e.sem_inc(ps_scores_free, 1)

                    def top16(n, src, tmp, val, idx):
                        for c in range(n):
                            j = e.max(val(c)[:, 0:8], src(c))
                        own(j)
                        for c in range(n):
                            e.max_index(idx(c)[:, 0:8], val(c)[:, 0:8], src(c))
                            j = e.match_replace(tmp(c), val(c)[:, 0:8], src(c), -BIG)
                        own(j)
                        for c in range(n):
                            j = e.max(val(c)[:, 8:16], tmp(c))
                        own(j)
                        for c in range(n):
                            j = e.max_index(idx(c)[:, 8:16], val(c)[:, 8:16], tmp(c))
                        own(j)

                    v16f, i16r = (t.rearrange("p a b c -> p (a b) c") for t in (v16, i16))
                    top16(2 * PH, lambda c: sc[:, c, :], lambda c: sc2[:, c, :], lambda c: v16f[:, c, :], lambda c: i16r[:, c, :])
                    e.sem_inc(scores_free, 1)
                    own(e.tensor_copy(i16f, i16))
                    own(tt_(cand, bc(v16[:, :, 0, :], 3, [P, PH, TOPK, TOPK]), bc(v16[:, :, 1, :], 2, [P, PH, TOPK, TOPK]), ALU.add))
                    cf = cand.rearrange("p a b c -> p a (b c)")
                    c2 = sc2.rearrange("p (a b) c -> p a (b c)", b=2)
                    top16(PH, lambda c: cf[:, c, :], lambda c: c2[:, c, :], lambda c: t16[:, c, :], lambda c: j16[:, c, :])
                    own(tt_(e1.rearrange("p (a b) -> p a b", b=TOPK), t16, t16[:, :, 0:1].to_broadcast([P, PH, TOPK]), ALU.subtract))
                    own(e.tensor_copy(t16, e1.rearrange("p (a b) -> p a b", b=TOPK)))
                    e.sem_inc(top_full, 1)
                    jf = j16.rearrange("p a b -> p (a b)")
                    ts(ja, jf, 4, None, ALU.logical_shift_right)
                    own(ts(jb, jf, 15, None, ALU.bitwise_and))
                    e.tensor_copy(jaf, ja)
                    own(e.tensor_copy(jbf, jb))
                    for n, (jx, ex) in enumerate(((jaf, e1), (jbf, e2))):
                        own(tt_(oh, bc(jx, 2, [P, SLOTS, TOPK]), bc(C("iota16"), 1, [P, SLOTS, TOPK]), ALU.is_equal))
                        oh4 = oh.rearrange("p (a b) c -> p a b c", b=TOPK)
                        own(tt_(oh4, oh4, bc(i16f[:, :, n, :], 2, [P, PH, TOPK, TOPK]), ALU.mult))
                        own(e.tensor_reduce(ex, oh, AX_X, ALU.add))
                    own(stt(e1, e1, 128.0, e2, ALU.mult, ALU.add))
                    own(ts(eidx[:, bass.ds(i, 1), :].rearrange("p a b -> p (a b)").bitcast(U32), e1, layer_off[:, 0:1], None, ALU.add))
                    take(e, top_exp, 1)
                    own(e.tensor_reduce(tsum, t16, AX_X, ALU.add))
                    own(e.reciprocal(tsum, tsum))
                    own(tt_(gate_w[:, bass.ds(i, 1), :].rearrange("p a (b c) -> p (a b) c", c=TOPK), t16, bc(tsum, 2, [P, PH, TOPK]), ALU.mult))
                take(e, scores_free, 1)
                own.clear()
                own(ts(layer_off[:, :], layer_off[:, :], float(EXPERTS), None, ALU.add))
                e.sem_inc(S("dve_route"), 1)
                own(e.memset(acc, 0.0))
                e.wait_ge(S("sp_sr"), 32)

                def dots(h, tt, nth):
                    e.wait_ge(u_full[h], nth * 64)
                    for j in range(4):
                        i = stt(urows[:, 4 * h + j, :], urows[:, 4 * h + j, :], 1.0, xtok[:, tt, :], ALU.mult, ALU.mult, accum_out=hid[:, h, j:j + 1])
                    own(i)
                    e.sem_inc(u_free[h], 1)
                    e.sem_inc(hid_full[h], 1)

                def weights(h, gates_):
                    take(e, hid_gelu[h], 1)
                    own(tt_(wgt[:, h, :], hge[:, h, :], gates_, ALU.mult))

                def sums(h, tt, nth):
                    e.wait_ge(v_full[h], nth * 64)
                    for j in range(4):
                        own(stt(acc[:, tt, :], vrows[:, 4 * h + j, :], wgt[:, h, j:j + 1], acc[:, tt, :], ALU.mult, ALU.add))
                    e.sem_inc(v_free[h], 1)

                per = GROUPS + 1
                for tt in range(TT):
                    nth = lambda i: l * per + (tt * 16 + 1) + i
                    gw = lambda i, h: gate_w[:, tt, bass.ds(i * 8 + 4 * h, 4)]
                    own.clear()
                    dots(0, tt, nth(0))
                    dots(1, tt, nth(0))
                    weights(0, gate_w[:, tt, 0:4])
                    sums(0, tt, nth(0))
                    with e.Fori(1, 16) as i:
                        own.clear()
                        dots(0, tt, nth(i))
                        weights(1, gw(i - 1, 1))
                        sums(1, tt, nth(i - 1))
                        dots(1, tt, nth(i))
                        weights(0, gw(i, 0))
                        sums(0, tt, nth(i))
                    own.clear()
                    weights(1, gate_w[:, tt, 124:128])
                    sums(1, tt, nth(15))
                last = (l + 1) * per
                dots(0, 2, last)
                dots(1, 2, last)
                for h in range(2):
                    weights(h, gs[:, 4 * h:4 * h + 4])
                    sums(h, 2, last)
                e.sem_inc(S("dve_acc"), 1)
                e.wait_ge(S("pe_step"), step("acc"))
                for tt in range(TT):
                    for g in range(2):
                        d = x[:, 4 * g:4 * g + 4, tt * P:tt * P + P]
                        tt_(d, d, bank(2 * tt + g, 512).rearrange("p (a b) -> p a b", b=P), ALU.add)
                own(tt_(x[:, :, SEQ:N], x[:, :, SEQ:N], bank(4, NS * KT).rearrange("p (a b) -> p a b", b=NS), ALU.add))
                layer_end(e, "dve")
            own.clear()
            squares(sqs)
            norm(1, lambda kt: glob[:, kt:kt + 1])


INS = dict(x=[P, KT * N], const=[P, NCONST], glob=[P, NGLOB], par=[L, P, NPAR], wa_up=[L, P, 256], g_up=[L, P, 256],
           w_if=[L, P, KT * 8], st=[L, P, 4 * 16 * HD], st_n=[L, P, 16], st_shift=[L, P, 8 * NS], st_conv=[L, P, 4 * NS * 3],
           m_old=[L, 4, NS], keys=[L, P, PH * 256], w=[L * N_BLOCKS, P, BLOCK], peer_u=[L * EXPERTS, D], peer_v=[L * EXPERTS, D])
OUTS = dict(y=[P, KT * N], shift=[L, P, 8 * (NS + 1)], conv=[L, P, 4 * (NS + 1) * 3], m=[L, 4, NS + 1], st=[L, P, 4 * 16 * HD],
            st_n=[L, P, 16], p_rw=[L, P, 2 * P], p_ret=[L, P, 2 * P], p_ml=[L, P, 2 * P], p_n=[L, P, PR], p_hg=[L, P, HD * PR])


def kernel(**inputs):
    import concourse.bacc as bacc
    from concourse.bass_utils import run_bass_kernel_spmd

    a = {k: np.asarray(v) for k, v in inputs.items()}

    def chan(z):
        z = np.moveaxis(z, -1, 0)
        return np.moveaxis(z.reshape((z.shape[0] // P, P) + z.shape[1:]), 1, 0)

    def per_layer(f):
        return np.stack([f(l) for l in range(L)])

    vec = lambda name: (lambda l: chan(a[name][l]).reshape(P, -1))
    tokens = np.concatenate([a["x_prompt"].reshape(SEQ, D), a["x_sample"].reshape(NS, D)])
    order = ["rwkv_mu", "rwkv_w0", "rwkv_a0", "rwkv_k_k", "rwkv_k_a", "rwkv_r_k", "rwkv_ln_g", "rwkv_ln_b", "hgrn_norm_g", "mlstm_norm_g"]

    def params(l):
        cols = [vec(n)(l) for n in order]
        cols.append(chan(a["mlstm_conv_w"][l]).reshape(P, -1))
        cols += [vec(n)(l) for n in ("mlstm_conv_b", "ln1_g", "ln2_g")]
        for n in ("mlstm_ig_b", "mlstm_fg_b"):
            c = np.zeros((P, 1), a[n].dtype)
            c[:H, 0] = a[n][l]
            cols.append(c)
        return np.concatenate(cols, 1)

    o4 = 4 * D
    gate0 = o4 + 8

    def tiles(w):
        k, c = w.shape[0] // P, w.shape[1] // P
        return w.reshape(k, P, c, P).transpose(2, 1, 0, 3).reshape(c, P, k * P)

    def blocks(l):
        w = a["w_in"][l]
        m0 = 3 * D
        mixed = np.concatenate([w[:, :m0 + 768], w[:, m0 + 776:m0 + 1032]], 1)
        t = list(tiles(mixed))
        gt = tiles(w[:, gate0:]).reshape(4, 8, P, D)
        br = np.stack([tiles(a["w_branch"][l, m]) for m in range(4)], 1)
        for i in range(4):
            for o in (2 * i, 2 * i + 1):
                t += [gt[m, o] for m in range(4)]
            t += [br[o].transpose(1, 0, 2).reshape(P, D) for o in (2 * i, 2 * i + 1)]
        t += list(tiles(a["w_out"][l])) + list(tiles(a["peer_w_q"][l]))
        t = np.stack(t)
        return t.reshape(N_BLOCKS, 2, P, D).transpose(0, 2, 1, 3).reshape(N_BLOCKS, P, BLOCK)

    def state(l):
        s = [a["state_hgrn_S"][l], a["state_ret_S"][l], a["state_mlstm_C"][l], a["state_rwkv_S"][l].transpose(0, 1, 3, 2)]
        return np.stack(s, 2).reshape(NS, H, 4, 4, 16, HD).transpose(0, 1, 3, 2, 4, 5).reshape(P, -1)

    def keyblocks(l):
        k = a["peer_keys"][l]
        z = np.zeros((2, HD, PH, 2, P), k.dtype)
        for c in range(2):
            z[c, :, :, c, :] = k[:, c].transpose(2, 0, 1)
        return z.reshape(P, -1)

    w_gates = a["w_in"][:, :, 3 * D + 768:3 * D + 776]
    feed = dict(
        x=chan(tokens).reshape(P, -1), const=constants()[0],
        glob=np.concatenate([chan(a["lnf_g"]).reshape(P, -1), chan(a["hgrn_lb_logits"]).transpose(0, 2, 1).reshape(P, -1)], 1),
        par=per_layer(params), wa_up=np.concatenate([a["rwkv_w_up"], a["rwkv_a_up"]], 1), g_up=a["rwkv_g_up"],
        w_if=w_gates.reshape(L, KT, P, 8).transpose(0, 2, 1, 3).reshape(L, P, -1),
        st=per_layer(state),
        st_n=a["state_mlstm_n"].reshape(L, P, 16),
        st_shift=per_layer(lambda l: chan(a["state_rwkv_shift"][l]).reshape(P, -1)),
        st_conv=per_layer(lambda l: chan(a["state_mlstm_conv"][l]).reshape(P, -1)),
        m_old=a["state_mlstm_m"].transpose(0, 2, 1),
        keys=per_layer(keyblocks), w=np.concatenate([blocks(l) for l in range(L)]),
        peer_u=a["peer_u"].reshape(L * EXPERTS, D), peer_v=a["peer_v"].reshape(L * EXPERTS, D))
    nc = bacc.Bacc("TRN2", target_bir_lowering=False, num_devices=1)
    A = {k: nc.dram_tensor(f"in_{k}", INS[k], F32, kind="ExternalInput").ap() for k in INS}
    O = {k: nc.dram_tensor(f"out_{k}", OUTS[k], F32, kind="ExternalOutput").ap() for k in OUTS}
    O["scratch"] = nc.dram_tensor("scratch", [NVEC * NS, 256], F32, kind="Internal").ap()
    O["scratch_i"] = nc.dram_tensor("scratch_i", [NS, SLOTS], F32, kind="Internal").ap()
    O["scratch_g"] = nc.dram_tensor("scratch_g", [NS, SLOTS], F32, kind="Internal").ap()
    A["x"] = A["x"].rearrange("p (a b) -> p a b", b=N)
    O["y"] = O["y"].rearrange("p (a b) -> p a b", b=N)
    build(nc, A, O)
    feed = {f"in_{k}": np.ascontiguousarray(feed[k]).reshape(INS[k]) for k in INS}
    r = run_bass_kernel_spmd(nc, [feed], core_ids=[0]).results[0]
    o = {k: np.asarray(r[f"out_{k}"]) for k in OUTS}

    y = o["y"].reshape(P, KT, N).transpose(2, 1, 0).reshape(N, D)
    shift = o["shift"].reshape(L, P, 8, NS + 1).transpose(0, 3, 2, 1).reshape(L, NS + 1, D)
    conv = o["conv"].reshape(L, P, 4, NS + 1, 3).transpose(0, 3, 4, 2, 1).reshape(L, NS + 1, 3, 512)
    m = o["m"].transpose(0, 2, 1)
    st = o["st"].reshape(L, NS, H, 4, 4, 16, HD).transpose(0, 4, 1, 2, 3, 5, 6).reshape(L, 4, NS, H, HD, HD)

    def pair_blocks(z):
        z = z.reshape(L, 2, HD, PR, 2, HD)
        return np.stack([z[:, h % 2, :, h // 2, h % 2, :] for h in range(H)], 1)[:, None]

    p_rw = pair_blocks(o["p_rw"]).transpose(0, 1, 2, 4, 3)
    p_hg = o["p_hg"].reshape(L, 2, HD, HD, PR).transpose(0, 4, 1, 2, 3).reshape(L, 1, H, HD, HD)
    p_n = o["p_n"].reshape(L, 2, HD, PR).transpose(0, 3, 1, 2).reshape(L, 1, H, HD)
    return (y[:SEQ][None], y[SEQ:, None], shift[:, 0:1], p_rw, p_hg, pair_blocks(o["p_ret"]), conv[:, 0:1],
            pair_blocks(o["p_ml"]), p_n, m[:, 0:1],
            shift[:, 1:], st[:, 3].transpose(0, 1, 2, 4, 3), st[:, 0], st[:, 1], conv[:, 1:], st[:, 2],
            o["st_n"].reshape(L, NS, H, HD), m[:, 1:])
```

```python
from contextlib import ExitStack

import numpy as np

import concourse.bass as bass
from concourse import mybir

F32 = mybir.dt.float32
U32 = mybir.dt.uint32
ALU = mybir.AluOpType
ACT = mybir.ActivationFunctionType
AX_X = mybir.AxisListType.X

P = 128
D = 1024
KT = D // P
SEQ = 256
NS = 8
N = SEQ + NS
L = 2
H = 4
HD = 64
PR = H // 2
TT = SEQ // P
CH = 64
NCH = SEQ // CH
EXPERTS = 128 * 128
PH = 8
TOPK = 16
SLOTS = PH * TOPK
PAST = 2048
BLOCK = 2048
N_IN, N_MIXED = 32, 16
N_BLOCKS = N_IN + 4 + 4 + 4
VB = 8
HALF_AFTER = (0, 1, 2, 4, 5, 6, 8, 9, 10, 12, 13, 14)
EARLY_GATES = 8
RWKV_GATES = 4
GATES_AT = (3, 10, 2, 1)
VAR_BANKS = (0, 1, 4, 5, 6, 7, 0, 1)
BRANCH_BANKS = (0, 1, 4, 5)
BRANCH_SLOTS = (4, 0, 1, 2)
STRETCHES = (1, 3, 4, 5, 7, 8, 9, 11, 12, 13, 14, 16)
EXP_AT = (4, 13)
TILE_AFTER = HALF_AFTER[1::2]
ATT = SEQ + P
BIG = 3.0e38
PE_STEPS = ("lr", "kk", "rk", "tr", "bv", "rot", "if", "rows", "svt", "sa", "po", "mean", "xt", "acc")
NORM_EPS, RWKV_EPS, HEAD_EPS = 1e-6, 64e-5, 1e-5

HG, RW, RT, ML = 0, 8, 16, 24
ACT_STEPS = ("hv", "hg", "proj", "lr", "kk", "e", "sv0", "vpad", "bv", "r0", "r2", "conv", "em", "dt", "sv", "svt", "og", "ysq", "xt")
PAR = dict(mu=(0, 8), w0=(8, 2), a0=(10, 2), kk=(12, 2), ka=(14, 2), rk=(16, 2), ln_g=(18, 2), ln_b=(20, 2),
           hg=(22, 2), mg=(24, 2), cw=(26, 16), cb=(42, 4), ln1=(46, 8), ln2=(54, 8), ig_b=(62, 1), fg_b=(63, 1))
NPAR = 64
NGLOB = 8 + 2 * L
V_F, V_K, V_Q, V_V, V_RW = 0, 3, 6, 9, 12
RW_W, RW_K, RW_R, RW_KK, RW_KKA, RW_V = range(12, 18)
NVEC = 18
NGLA = 12


def constants():
    p = np.arange(P)
    head = p // HD
    t = {}
    t["ident"] = np.eye(P)
    t["ones"] = np.ones((P, P))
    t["headsum"] = (head[:, None] == head[None]).astype(np.float64)
    t["headmean"] = t["headsum"] / HD
    s, c = p[:, None], p[None]
    same = (s // CH) == (c // CH)
    strict, incl = same & (s < c), same & (s <= c)
    t["chunkmask"] = np.concatenate([strict, incl, strict, incl], 1)
    levels = []
    for k in range(6):
        b = 1 << k
        levels.append(-((s // (2 * b) == c // (2 * b)) & (s % (2 * b) >= b) & (c % (2 * b) < b)).astype(float))
    t["levels"] = np.concatenate(levels, 1)
    tri = (s <= c).astype(float)
    t["causal"] = np.concatenate([tri, np.ones((P, P)), tri], 1)
    lg = np.log(1.0 - 2.0 ** (-5.0 - np.arange(H)))
    rel = [np.arange(SEQ)[None] - s, np.arange(P, SEQ)[None] - (s + P)]
    t["decay"] = np.concatenate([np.where(r >= 0, np.exp(lg[h] * np.maximum(r, 0)), 0.0) for h in range(H) for r in rel], 1)
    t["decay_end"] = np.stack([np.exp(lg[h] * (SEQ - 1 - (p + P * st))) for st in range(TT) for h in range(H)], 1)
    t["decay_chan"] = np.stack([np.exp(lg[2 * pr + head]) for pr in range(PR)], 1)
    half = HD // 2
    inv = (10000.0 ** (-(np.arange(half, dtype=np.float32)) / np.float32(half))).astype(np.float32)
    pos = np.concatenate([np.arange(SEQ), np.full(NS, PAST)]).astype(np.float32)
    ang = (pos[None] * inv[p % half][:, None]).astype(np.float32).astype(np.float64)
    t["cos"], t["sin"] = np.cos(ang), np.sin(ang)
    rot = np.zeros((P, P))
    for q in range(P):
        if q % HD < half:
            rot[q + half, q] = -1.0
        else:
            rot[q - half, q] = 1.0
    t["rot"] = rot
    place = np.zeros((P, 191))
    place[p, HD - 1 + HD * head] = 1.0
    t["place"] = place
    t["channel"] = (p[:, None] % HD == np.arange(HD)[None]).astype(float)
    t["onespad"] = np.tile(np.repeat([0.0, 1.0, 0.0], HD), (P, 1))
    t["chunkstart"] = np.tile((np.arange(SEQ) % CH != 0).astype(float), (P, 1))
    t["rows"] = np.stack([head == 0, head == 1, -1.0 * (head == 0), -1.0 * (head == 1)], 1)
    t["iota16"] = np.tile(np.arange(16.0), (P, 1))
    t["quads"] = (p[:, None] // 4 == p[None] // 4).astype(float)
    b_of, h_of = p // 16, (p // 4) % 4
    t["samples"] = ((h_of[:, None] == np.repeat(np.arange(H), NS)[None]) & (b_of[:, None] == np.tile(np.arange(NS), H)[None]))
    t["group"] = (p[:, None] // 16 == np.arange(NS)[None]).astype(float)
    sel = np.zeros((P, H, P))
    for h in range(H):
        sel[h, h] = 1.0
    t["rowsel"] = sel.reshape(P, -1)
    pair = np.zeros((P, PR, P))
    for pr in range(PR):
        for q in range(P):
            pair[2 * pr + q // HD, pr, q] = 1.0
    t["pairsel"] = pair.reshape(P, -1)
    t["zero"] = np.zeros((P, SEQ))
    t["eps"] = np.tile([NORM_EPS, RWKV_EPS, HEAD_EPS, 1.0], (P, 1))
    at, n = {}, 0
    for k, v in t.items():
        at[k] = (n, v.shape[1])
        n += v.shape[1]
    return np.concatenate([np.asarray(v, np.float32) for v in t.values()], 1).astype(np.float32), at, n


_, CONST_AT, NCONST = constants()
ARENA = 22352


def build(nc, A, O):
    with ExitStack() as ctx:
        def sb(name, shape, dt=F32):
            return ctx.enter_context(nc.sbuf_tensor(name, shape, dt))

        sems = {}

        def sem(name, per_layer=True):
            s = ctx.enter_context(nc.semaphore(name))
            if per_layer:
                sems[name] = s
            return s

        x = sb("x", [P, KT, N])
        const = sb("const", [P, NCONST])
        glob = sb("glob", [P, NGLOB])
        lb_all = sb("lb_all", [P, L * PR])
        lb = sb("lb", [P, 3, PR])
        par = sb("par", [P, NPAR])
        wa_up = sb("wa_up", [P, 256])
        g_up = sb("g_up", [P, 256])
        w_if = sb("w_if", [P, KT, 8])
        st = sb("st", [P, 4, 16, HD])
        st_n = sb("st_n", [P, 16])
        st_shift = sb("st_shift", [P, 8, NS])
        st_conv = sb("st_conv", [P, 4, NS, 3])
        m_old = sb("m_old", [4, NS])
        xn = sb("xn", [P, KT, N])
        ring = sb("ring", [P, 5, BLOCK])
        layer_off = sb("layer_off", [P, 1])
        keyz = sb("keyz", [P, 2, 2, PR, SEQ])
        vpad = sb("vpad", [P, 2, H, 3 * HD])
        upad = sb("upad", [P, H, 3 * HD])
        out_shift = sb("sb_shift", [P, 8, NS + 1])
        out_conv = sb("sb_conv", [P, 4, NS + 1, 3])
        out_m = sb("sb_m", [4, NS + 1])
        small = sb("small", [P, 32])
        arena = sb("arena", [P, ARENA])

        ps = ctx.enter_context(nc.psum_tensor("ps", [P, 8, 512], F32))

        def C(name, n=None):
            a, w = CONST_AT[name]
            return const[:, a:a + (n or w)]

        def V(name, i=0, n=1):
            return par[:, PAR[name][0] + i:PAR[name][0] + i + n]

        top = [0]

        def carve(*shape, at=None, dt=F32):
            n = int(np.prod(shape))
            if at is None:
                at = top[0]
                top[0] += n
            assert at + n <= ARENA, (at, n)
            v = arena[:, at:at + n]
            if dt != F32:
                v = v.bitcast(dt)
            if len(shape) == 1:
                return v
            names = " ".join(f"d{i}" for i in range(len(shape)))
            return v.rearrange(f"p ({names}) -> p {names}", **{f"d{i}": s for i, s in enumerate(shape)})

        proj = carve(32, N)
        yy = carve(8, N)
        gg = carve(PR, N)
        vb = carve(PR, N)
        sv = carve(PR, NVEC, NS)
        emk = carve(PR, N)
        denk = carve(PR, N)
        sqs = carve(8, N, at=top[0])
        mix = top[0]
        diff = carve(8, N)
        loga, aa, kk, kn, kka, t1 = [carve(PR, N) for _ in range(6)]
        chunk_m = carve(8, 512, at=mix)
        al, kb = carve(PR, SEQ, at=mix), carve(PR, SEQ, at=mix + 512)
        e_p = carve(PR, SEQ, at=mix + 1024)
        e_n = carve(PR, SEQ, at=mix + 1536)
        rr = carve(TT, H, P, at=mix + 8 * N + 4 * PR * N)
        e_b = carve(PR, SEQ)
        kr = carve(PR, TT, 256)
        xm = carve(8, P, at=RW * N)
        xt = carve(8, P, at=RW * N + 8 * P)
        alt, kbt = carve(TT, 256), carve(TT, 256)
        vc = carve(NCH, 256)
        bv = carve(TT, 256, at=mix - 2 * PR * N)
        pm = carve(256, at=mix - 2 * PR * N + 512)
        sb1 = carve(PR, P, at=mix - 2 * PR * N + 768)
        sbd2 = carve(2, PR, P)
        sbd = sbd2[:, NCH % 2, :, :]
        top[0] = mix
        qr, kq, u1, u2 = [carve(PR, N) for _ in range(4)]
        carve(112)
        att = carve(H, ATT)
        ktok = carve(TT, 256)
        sfin = carve(PR, P)
        nfin = carve(PR)
        cpad = carve(4, 288 + 3)
        cv = carve(4, 288, at=mix + 2 * PR * N)
        rows = carve(10, N)
        rowx = carve(280)
        ccol = carve(TT, H)
        fa = carve(PR, 2 * NS)
        top[0] = mix
        fp, kp, qp = [carve(PR, SEQ) for _ in range(3)]
        sgn = carve(PR, N)
        kv = carve(VB, 512)
        ss = carve(4, 512)
        hfin = carve(HD, PR)
        win = carve(4, P)
        top[0] = mix
        svt, svt2 = carve(PR, P), carve(PR, P)
        gv = carve(NVEC, 16)
        gvv = carve(4, HD)
        big1, big2 = carve(3, 16, HD), carve(16, HD)
        nq = carve(16)
        po = carve(4, 2, HD)
        pn = carve(1)
        sa, sab = carve(HD), carve(HD)
        more_gates = carve(6, N)
        rs8 = carve(8, N, at=mix)
        fg8 = carve(8, N, at=mix + 8 * N)
        merged = carve(8, N, at=mix)
        used_up = [t for t in range(32) if t not in (HG + 6, HG + 7, RT + 6, RT + 7, ML + 6, ML + 7)]
        gates = [proj[:, t, :] for t in used_up] + [more_gates[:, t, :] for t in range(32 - len(used_up))]
        rstd = yy[:, 0, :]
        top[0] = 0
        xtok = carve(3, D)
        eidx = carve(TT, SLOTS)
        gate_w = carve(TT, SLOTS)
        eidx_s, gate_s = carve(TOPK), carve(TOPK)
        es, gs = carve(8, dt=U32), carve(8)
        sc_s = carve(2, P)
        urows = carve(8, D)
        peer0 = top[0]
        top[0] -= 8 * D
        keys = carve(PH, 256)
        qpe = carve(PH, SEQ)
        qz = carve(PH, NS * PH)
        sc0 = carve(PH * 2, P)
        xrep = carve(KT, P)
        assert top[0] <= peer0
        top[0] = peer0
        sc1 = carve(PH * 2, P)
        acc1 = [carve(D, at=peer0 + k * D) for k in range(2)]
        sc2 = carve(PH * 2, P)
        cand = carve(PH, TOPK, TOPK)
        oh = carve(PH, TOPK, TOPK, at=top[0] - PH * TOPK * TOPK)
        v16 = carve(PH, 2, TOPK)
        i16 = carve(PH, 2, TOPK, dt=U32)
        i16f = carve(PH, 2, TOPK)
        t16 = carve(PH, TOPK)
        j16 = carve(PH, TOPK, dt=U32)
        ja, jb = carve(PH, TOPK, dt=U32), carve(PH, TOPK, dt=U32)
        jaf, jbf = carve(PH, TOPK), carve(PH, TOPK)
        e1, e2 = carve(PH, TOPK), carve(PH, TOPK)
        tsum = carve(PH)
        hid, hge, wgt = [carve(2, 4) for _ in range(3)]
        ixu = carve(2, 4, dt=U32)
        ixv = carve(2, 4, dt=U32)
        acc = [carve(D)] + acc1
        assert top[0] <= ARENA
        vrows = ring[:, 0:4, :].rearrange("p a (b c) -> p (a b) c", b=2)

        for name in (
                "act_co act_cv act_ps act_q act_rt act_silu act_step act_top act_turn act_var act_wa act_wag act_y "
                "dve_acc dve_att dve_cm dve_cum dve_cv dve_dt dve_hg dve_inv dve_kk2 dve_kr dve_kw dve_mg dve_pm "
                "dve_po dve_qk dve_qz dve_r dve_r1 dve_rk dve_route dve_rows dve_sa dve_sbd dve_shift dve_sq dve_sv "
                "dve_top dve_u dve_x dve_xn dve_xs dve_yc dve_yn dve_yy "
                "pe_cf pe_cm pe_co pe_ctr pe_hg pe_ks pe_p pe_ps pe_s pe_sc pe_ss pe_y pe_step pe_t pe_u pe_var pe_wo "
                "pe_wq "
                "pool_gla pool_hf pool_kz pool_rw pool_sa pool_st pool_turn "
                "sp_dfin sp_hfin sp_keys sp_out sp_par sp_rw sp_sr sp_svr sp_svw sp_sw sp_vw ").split():
            sem(name)
        once = {name: sem(name, False) for name in ("sp_once", "pool_zero", "dve_lb", "act_lb")}

        def S(name):
            return once[name] if name in once else sems[name]

        w_full = [sem(f"w_full{j}", False) for j in range(5)]
        w_free = [sem(f"w_free{j}", False) for j in range(5)]
        bank_full = [sem(f"bank_full{j}", False) for j in range(8)]
        bank_free = [sem(f"bank_free{j}", False) for j in range(8)]
        value_full = [sem(f"value_full{j}", False) for j in range(VB)]
        out_done = sem("out_done")
        win_full = sem("win_full")
        ss_full = sem("ss_full")
        qs_full = sem("qs_full")
        u_full = [sem(f"u_full{j}", False) for j in range(2)]
        v_full = [sem(f"v_full{j}", False) for j in range(2)]
        u_free = [sem(f"u_free{j}", False) for j in range(2)]
        v_free = [sem(f"v_free{j}", False) for j in range(2)]
        hid_full = [sem(f"hid_full{j}", False) for j in range(2)]
        hid_gelu = [sem(f"hid_gelu{j}", False) for j in range(2)]
        arrive = sem("arrive", False)
        go = {e: sem(f"go_{e}", False) for e in ("pe", "act", "dve", "pool")}

        def step(name):
            steps = PE_STEPS if name.startswith("pe_") else ACT_STEPS
            return steps.index(name.split("_")[1]) + 1

        def take(e, s, n):
            e.wait_ge(s, n)
            e.sem_clear(s)

        class Own:

            def __init__(self, e, name):
                self.e, self.s, self.n = e, sem(name, False), 0

            def clear(self):
                self.e.sem_clear(self.s)
                self.n = 0

            def __call__(self, ins):
                ins.then_inc(self.s, 1)
                self.n += 1
                self.e.wait_ge(self.s, self.n)

        def layer_end(e, name):
            e.sem_inc(arrive, 1)
            take(e, go[name], 1)

        GROUPS = 2 * SEQ // P * 16 // 2
        assert GROUPS == 32

        block = ctx.enter_context(nc.Block())

        def at1(v):
            return slice(v, v + 1) if isinstance(v, int) else bass.ds(v, 1)

        def bc(ap, k, shape):
            return ap.unsqueeze(k).to_broadcast(shape)

        @block.sync
        def _(e):
            e.dma_start(x[:, :, :], A["x"]).then_inc(S("sp_once"), 16)
            e.dma_start(const[:, :], A["const"]).then_inc(S("sp_once"), 16)
            e.dma_start(glob[:, :], A["glob"]).then_inc(S("sp_once"), 16)
            with e.Fori(0, L) as l:
                def lay(name):
                    return A[name][bass.ds(l, 1)]
                for dst, name in ((par[:, :], "par"), (wa_up[:, :], "wa_up"), (g_up[:, :], "g_up")):
                    e.dma_start(dst, lay(name).rearrange("a p c -> p (a c)")).then_inc(S("sp_par"), 16)
                e.dma_start(w_if[:, :, :].rearrange("p a b -> p (a b)"), lay("w_if").rearrange("a p c -> p (a c)")).then_inc(S("sp_par"), 16)
                for dst, name in ((st[:, :, :, :].rearrange("p a b c -> p (a b c)"), "st"), (st_n[:, :], "st_n"),
                                  (st_shift[:, :, :].rearrange("p a b -> p (a b)"), "st_shift"),
                                  (st_conv[:, :, :, :].rearrange("p a b c -> p (a b c)"), "st_conv"), (m_old[:, :], "m_old")):
                    e.dma_start(dst, lay(name).rearrange("a p c -> p (a c)")).then_inc(S("sp_par"), 16)

                def block_of(j, n):
                    take(e, w_free[j], 1)
                    e.dma_start(ring[:, j, :], A["w"][bass.ds(n, 1)].rearrange("a p c -> p (a c)")).then_inc(w_full[j], 16)

                for j in range(4):
                    block_of(j, l * N_BLOCKS + j)
                e.wait_ge(S("act_step"), step("act_hv"))
                e.dma_start(O["scratch_v"].rearrange("r p t -> p r t"), proj[:, HG + 4:HG + 6, 0:SEQ]).then_inc(S("sp_vw"), 16)
                for j in range(2):
                    block_of(j, l * N_BLOCKS + 4 + j)
                e.wait_ge(S("sp_vw"), 16)
                by_value = O["scratch_v"].rearrange("r (q v) t -> q v r t", q=2)

                def spread(u, v):
                    for q in range(2):
                        to = kv[q * HD:q * HD + HD, u % VB, :].rearrange("d (r t) -> d r t", r=PR)
                        e.dma_start(to, by_value[q, at1(v), :, :].to_broadcast([HD, PR, SEQ])).then_inc(value_full[u % VB], 16)

                for u in range(VB):
                    spread(u, u)

                def sixteen(i, last):
                    for u in range(16):
                        if not last or u < 16 - VB:
                            e.wait_ge(ss_full, i * 16 + u + 1)
                            spread(u, i * 16 + u + VB)
                        k = {2: 2, 8: 3, 13: 4}.get(u)
                        if k is not None:
                            block_of(k % 3, l * N_BLOCKS + 4 + i * 3 + k)

                with e.Fori(0, HD // 16 - 1) as i:
                    sixteen(i, False)
                sixteen(HD // 16 - 1, True)
                e.wait_ge(S("pool_hf"), 1)
                e.dma_start(O["p_hg"][bass.ds(l, 1)].rearrange("a p c -> p (a c)"), hfin[:, :, :].rearrange("p a b -> p (a b)")).then_inc(S("sp_hfin"), 16)
                e.wait_ge(S("dve_sbd"), NCH + 1)
                e.dma_start(O["p_rw"][bass.ds(l, 1)].rearrange("a p c -> p (a c)"), sbd[:, :, :].rearrange("p a b -> p (a b)")).then_inc(S("sp_rw"), 16)
                for j in range(2, 4):
                    block_of(j, l * N_BLOCKS + N_MIXED + j)
                block_of(4, l * N_BLOCKS + N_IN)
                for j in range(4):
                    block_of(j, l * N_BLOCKS + N_MIXED + 4 + j)
                e.wait_ge(S("act_step"), step("act_svt"))
                e.dma_start(O["scratch"][0:NGLA * NS, :], svt[0:NGLA * NS, :, :].rearrange("p a b -> p (a b)")).then_inc(S("sp_svw"), 16)
                e.dma_start(O["scratch"][NGLA * NS:NVEC * NS, :], svt2[0:(NVEC - NGLA) * NS, :, :].rearrange("p a b -> p (a b)")).then_inc(S("sp_svw"), 16)
                e.wait_ge(S("sp_svw"), 32)
                e.dma_start(gv[:, :, :], O["scratch"].rearrange("(v b) (q k) -> (b q) v k", v=NVEC, k=16)).then_inc(S("sp_svr"), 16)
                for n, v in enumerate((V_V, V_V + 1, V_V + 2, RW_V)):
                    src = O["scratch"][v * NS:(v + 1) * NS, :].rearrange("b (h c) -> (b h) c", c=HD)
                    e.dma_start(gvv[:, n, :], bc(src, 1, [32, 4, HD])).then_inc(S("sp_svr"), 16)
                e.wait_ge(S("dve_shift"), 1)
                e.dma_start(O["shift"][bass.ds(l, 1)].rearrange("a p c -> p (a c)"), out_shift[:, :, :].rearrange("p a b -> p (a b)")).then_inc(S("sp_out"), 16)
                with e.Fori(2, 4) as i:
                    for j in range(4):
                        block_of(j, l * N_BLOCKS + N_MIXED + i * 4 + j)
                for j in range(3):
                    block_of(j, l * N_BLOCKS + N_IN + 1 + j)
                for k in range(2):
                    for j in range(4):
                        block_of(j, l * N_BLOCKS + N_IN + 4 + 4 * k + j)
                e.wait_ge(S("pool_st"), 1)
                e.wait_ge(S("act_step"), step("act_conv"))
                e.wait_ge(S("dve_rows"), 1)
                for name, src in (("conv", out_conv[:, :, :, :].rearrange("p a b c -> p (a b c)")), ("m", out_m[:, :]),
                                  ("st", st[:, :, :, :].rearrange("p a b c -> p (a b c)")), ("st_n", st_n[:, :])):
                    e.dma_start(O[name][bass.ds(l, 1)].rearrange("a p c -> p (a c)"), src).then_inc(S("sp_out"), 16)
                e.wait_ge(S("dve_x"), KT)
                e.dma_start(keys[:, :, :].rearrange("p a b -> p (a b)"), lay("keys").rearrange("a p c -> p (a c)")).then_inc(S("sp_keys"), 16)
                e.wait_ge(S("dve_route"), 2)
                e.dma_start(O["scratch_i"][:, :], eidx_s[0:NS * PH, :]).then_inc(S("sp_sw"), 16)
                e.dma_start(O["scratch_g"][:, :], gate_s[0:NS * PH, :]).then_inc(S("sp_sw"), 16)
                e.wait_ge(S("sp_sw"), 32)
                e.dma_start(es, O["scratch_i"].rearrange("r (g j) -> (r g) j", j=8).bitcast(U32)).then_inc(S("sp_sr"), 16)
                e.dma_start(gs, O["scratch_g"].rearrange("r (g j) -> (r g) j", j=8)).then_inc(S("sp_sr"), 16)
                e.wait_ge(S("sp_out"), 5 * 16)
                e.wait_ge(S("sp_rw"), 16)
                e.wait_ge(S("sp_hfin"), 16)
                e.wait_ge(S("sp_dfin"), 48)
                e.wait_ge(arrive, 4)
                e.sem_clear(arrive)
                for s in sems.values():
                    e.sem_clear(s)
                for s in go.values():
                    e.sem_inc(s, 1)
            e.wait_ge(S("dve_xn"), 1)
            e.dma_start(O["y"], xn[:, :, :]).then_inc(S("sp_out"), 16)
            e.wait_ge(S("sp_out"), 16)

        @block.tensor
        def _(e):
            mm = e.matmul

            def bank(b, n=N, lo=0):
                return ps[:, b, lo:lo + n]

            def sum_squares(sq_, k):
                e.wait_ge(S("dve_sq"), k)
                for kt in range(KT):
                    i = mm(bank(0), C("ones"), sq_[:, kt, :], start=kt == 0, stop=kt == KT - 1)
                i.then_inc(S("pe_ss"), 1)

            e.wait_ge(S("sp_once"), 48)
            for j in range(5):
                e.sem_inc(w_free[j], 1)
            with e.Fori(0, L) as l:
                sum_squares(sqs, 1)
                e.wait_ge(S("dve_xn"), 1)

                def half_tile(t, half):
                    b = t % 2
                    if not half:
                        if b == 0:
                            take(e, w_full[t // 2], 16)
                        take(e, bank_free[b], 1)
                    for kt in range(4 * half, 4 * half + 4):
                        at = b * D + kt * P
                        m = mm(bank(b), ring[:, t // 2, at:at + P], xn[:, kt, :], start=kt == 0, stop=kt == KT - 1)
                    if half:
                        m.then_inc(bank_full[b], 1)

                for t in range(8):
                    half_tile(t, 0)
                    half_tile(t, 1)
                nothing = C("zero", P)
                mm(bank(4, 512), nothing, const[:, 0:512], start=True, stop=False)
                with e.Fori(0, HD // 16) as i:
                    for u in range(16):
                        e.wait_ge(qs_full, i * 16 + u + 1)
                        e.wait_ge(win_full, i * 16 + u + 1)
                        mm(bank(4, 512), win[:, u % 4, :], ss[:, u % 4, :], start=False, stop=False, skip_group_check=True).then_inc(out_done, 1)
                        if u in HALF_AFTER:
                            half_tile(*divmod(HALF_AFTER.index(u), 2))
                mm(bank(4, 512), nothing, const[:, 0:512], start=False, stop=True).then_inc(S("pe_hg"), 1)
                e.wait_ge(S("sp_par"), 16 * 9)

                gate = iter(range(32))

                def gate_tiles(n, banks=2):
                    for g in [next(gate) for _ in range(n)]:
                        b, j = banks + g % 2, g // 2 % 4
                        if g % 2 == 0:
                            take(e, w_full[j], 16)
                        take(e, bank_free[b], 1)
                        for kt in range(KT):
                            at = (g % 2) * D + kt * P
                            m = mm(bank(b), ring[:, j, at:at + P], xn[:, kt, :], start=kt == 0, stop=kt == KT - 1)
                        m.then_inc(bank_full[b], 1)

                e.wait_ge(S("act_step"), step("act_lr"))
                e.wait_ge(S("act_step"), step("act_proj"))
                for pr in range(PR):
                    c = slice(pr * P, pr * P + P)
                    mm(bank(2 + pr), wa_up[0:HD, c], proj[0:HD, RW + 6, :], start=True, stop=True)
                    mm(bank(4 + pr), wa_up[HD:P, c], proj[HD:P, RW + 6, :], start=True, stop=True)
                    m = mm(bank(6 + pr), g_up[:, c], proj[:, RW + 7, :], start=True, stop=True)
                m.then_inc(S("pe_step"), 1)
                e.wait_ge(S("dve_kk2"), 1)
                for pr in range(PR):
                    m = mm(bank(pr), C("headsum"), t1[:, pr, :], start=True, stop=True)
                m.then_inc(S("pe_step"), 1)
                gate_tiles(RWKV_GATES // 2, 6)
                e.wait_ge(S("act_wag"), 2)
                e.wait_ge(S("dve_rk"), 1)
                for pr in range(PR):
                    m = mm(bank(2 + pr), C("headsum"), t1[:, pr, :], start=True, stop=True)
                m.then_inc(S("pe_step"), 1)
                gate_tiles(RWKV_GATES // 2, 6)
                for b in (6, 7):
                    take(e, bank_free[b], 1)
                e.wait_ge(S("dve_kr"), 1)
                for n, src in enumerate((proj[:, RW + 4:RW + 6, :], al, kb)):
                    for tt in range(TT):
                        for pr in range(PR):
                            m = e.transpose(ps[:, 4 + n, tt * 256 + pr * P:tt * 256 + pr * P + P], src[:, pr, tt * P:tt * P + P], C("ident"))
                m.then_inc(S("pe_step"), 1)
                e.wait_ge(S("pool_kz"), 1)
                for n in range(TT * H):
                    tt, h = divmod(n, H)
                    pr, q = divmod(h, 2)
                    b = (7, 0, 1)[n % 3]
                    if n >= 3:
                        e.wait_ge(S("dve_cm"), n - 2)
                    mm(bank(b, 256), keyz[:, 0, q, pr, tt * P:tt * P + P], kr[:, pr, tt, :], start=True, stop=True)
                    mm(bank(b, 256, 256), keyz[:, 1, q, pr, tt * P:tt * P + P], kr[:, pr, tt, :], start=True, stop=True)\
                        .then_inc(S("pe_cm"), 1)
                e.wait_ge(S("act_step"), step("act_vpad"))
                e.wait_ge(S("dve_cm"), 8)
                for n in range(TT * H):
                    tt, h = divmod(n, H)
                    m = mm(bank(2, HD, tt * 256 + h * HD), chunk_m[:, n, 256:384], vpad[:, tt, h, HD:2 * HD], start=True, stop=True)
                m.then_inc(S("pe_step"), 1)
                for k in range(6):
                    for tt in range(TT):
                        e.wait_ge(S("dve_inv"), max(2 * k + tt, 1))
                        for h in range(H):
                            n = tt * H + h
                            m = mm(bank(3 + tt, P, h * P), chunk_m[:, n, 0:P], xm[:, n, :], start=True, stop=True)
                        m.then_inc(S("pe_t"), 1)
                    for tt in range(TT):
                        e.wait_ge(S("dve_r"), 2 * k + tt + 1)
                        for h in range(H):
                            n = tt * H + h
                            mm(bank(5 + tt, P, h * P), xt[:, n, :], rr[:, tt, h, :], start=True, stop=True)
                        for h in range(H):
                            n = tt * H + h
                            m = mm(bank((7, 0)[tt], P, h * P), rr[:, tt, h, :], xt[:, n, :], start=True, stop=True)
                        m.then_inc(S("pe_p"), 1)
                for c in range(NCH):
                    tt, cp = c // 2, HD * (c % 2)
                    e.wait_ge(S("dve_sbd"), c + 1)
                    if c == 0:
                        e.wait_ge(S("dve_inv"), 13)
                    now = sbd2[:, c % 2, :, :]
                    for pr in range(PR):
                        m = mm(bank(3, P, pr * P), kr[:, pr, tt, 0:P], now[:, pr, :], start=True, stop=True)
                    m.then_inc(S("pe_ks"), 1)
                    e.wait_ge(S("dve_pm"), c + 1)
                    for h in range(H):
                        m = mm(bank(4, HD, h * HD), xt[:, tt * H + h, :], pm[:, h * HD:h * HD + HD], start=True, stop=True)
                    m.then_inc(S("pe_u"), 1)
                    e.wait_ge(S("dve_u"), c + 1)
                    for pr in range(PR):
                        out = bank(6, P, pr * P)
                        mm(out, alt[:, tt, pr * P:pr * P + P], upad[:, 2 * pr:2 * pr + 2, HD:2 * HD], start=True, stop=False)
                        m = mm(out, kbt[:, tt, pr * P:pr * P + P], vc[:, c, pr * P:pr * P + P], start=False, stop=True)
                    m.then_inc(S("pe_s"), 1)
                    if c:
                        e.wait_ge(S("act_y"), c)
                    for pr in range(PR):
                        out = bank(5, CH, pr * CH)
                        mm(out, now[:, pr, :], kr[:, pr, tt, P + cp:P + cp + CH], start=True, stop=False)
                        for q in range(2):
                            n = tt * H + 2 * pr + q
                            pad = slice(HD - HD * q, 3 * HD - HD * q)
                            mm(out, upad[:, 2 * pr + q, pad], chunk_m[:, n, P + cp:P + cp + CH], start=False, stop=False)
                            m = mm(out, vpad[:, tt, 2 * pr + q, pad], chunk_m[:, n, 384 + cp:384 + cp + CH], start=False, stop=q == 1)
                    m.then_inc(S("pe_y"), 1)

                def causal(mixer, q_, k_tiles, v_tiles):
                    e.wait_ge(S("dve_qk"), mixer + 1)
                    for n, src in enumerate((v_tiles, k_tiles)):
                        for tt in range(TT):
                            for pr in range(PR):
                                m = e.transpose(ps[:, 4 + n, tt * 256 + pr * P:tt * 256 + pr * P + P], src[:, pr, tt * P:tt * P + P], C("ident"))
                    m.then_inc(S("pe_ctr"), 1)
                    e.wait_ge(S("pool_kz"), mixer + 2)
                    for h in range(H):
                        pr, q = divmod(h, 2)
                        b = 6 + h % 2
                        if h >= 2:
                            e.wait_ge(S("dve_att"), 4 * mixer + h - 1)
                        mm(bank(b, SEQ), keyz[:, mixer, q, pr, 0:P], q_[:, pr, 0:SEQ], start=True, stop=True)
                        mm(bank(b, P, SEQ), keyz[:, mixer, q, pr, P:SEQ], q_[:, pr, P:SEQ], start=True, stop=True).then_inc(S("pe_sc"), 1)
                    e.wait_ge(S("act_cv"), mixer + 1)
                    e.wait_ge(S("dve_att"), 4 * mixer + 4)
                    def over_keys(out, late, values):
                        for q, tt in ((0, 0), (0, 1), (1, 1), (1, 0)):
                            h = 2 * pr + q
                            pad = HD - HD * q
                            if tt:
                                m = mm(late, values(tt, h, pad), att[:, h, SEQ:ATT], start=False, stop=False, skip_group_check=True)
                            else:
                                m = mm(out, values(tt, h, pad), att[:, h, 0:SEQ], start=q == 0, stop=q == 1)
                        return m

                    for pr in range(PR):
                        m = over_keys(bank(pr, SEQ), bank(pr, P, P), lambda tt, h, pad: vpad[:, tt, h, pad:pad + P])
                    if mixer:
                        a = CONST_AT["onespad"][0]
                        for pr in range(PR):
                            m = over_keys(bank(2 + pr, SEQ), bank(2 + pr, P, P), lambda tt, h, pad: const[:, a + pad:a + pad + P])
                    m.then_inc(S("pe_co"), 1)
                    e.wait_ge(S("dve_kw"), mixer + 1)
                    for pr in range(PR):
                        for tt in range(TT):
                            m = mm(bank(6, P, pr * P), ktok[:, tt, pr * P:pr * P + P], vpad[:, tt, 2 * pr:2 * pr + 2, HD:2 * HD],
                                   start=tt == 0, stop=tt == TT - 1)
                    if mixer:
                        for pr in range(PR):
                            for tt in range(TT):
                                m = mm(bank(6, 1, 256 + pr), ktok[:, tt, pr * P:pr * P + P], C("ones", 1), start=tt == 0, stop=tt == TT - 1)
                    m.then_inc(S("pe_cf"), 1)

                e.wait_ge(S("act_y"), NCH)
                e.wait_ge(S("dve_sbd"), NCH + 1)
                for t in range(4):
                    m = mm(bank(t), C("rot"), proj[:, RT + t, :], start=True, stop=True)
                m.then_inc(S("pe_step"), 1)
                causal(0, qr, kq, proj[:, RT + 4:RT + 6, :])
                for g in range(2):
                    for kt in range(KT):
                        m = mm(ps[0:4, 2 + g, 0:N], w_if[:, kt, 4 * g:4 * g + 4], xn[:, kt, :], start=kt == 0, stop=kt == KT - 1)
                m.then_inc(S("pe_step"), 1)
                gate_tiles(EARLY_GATES - RWKV_GATES, 6)
                for b in (6, 7):
                    take(e, bank_free[b], 1)
                e.wait_ge(S("dve_rows"), 1)
                e.wait_ge(S("act_co"), 1)
                a = CONST_AT["rowsel"][0]
                for h in range(H):
                    mm(bank(h // 2, SEQ, SEQ * (h % 2)), const[0:4, a + h * P:a + h * P + P], rows[0:4, 5, 0:SEQ], start=True, stop=True)
                a = CONST_AT["pairsel"][0]
                for pr in range(PR):
                    mm(bank(2 + pr, 280), const[0:4, a + pr * P:a + pr * P + P], rowx[0:4, 0:280], start=True, stop=True)
                for tt in range(TT):
                    m = e.transpose(ps[:, 4, tt * H:tt * H + H], rows[0:4, 6, tt * P:tt * P + P], C("ident")[0:4, 0:4])
                m.then_inc(S("pe_step"), 1)
                e.wait_ge(S("act_step"), step("act_em"))
                causal(1, qr, kq, proj[:, ML + 4:ML + 6, :])

                e.wait_ge(S("dve_sv"), 1)
                e.wait_ge(S("act_step"), step("act_sv"))
                for pr in range(PR):
                    e.transpose(ps[0:NGLA * NS, 5, pr * P:pr * P + P], sv[:, pr, 0:NGLA, :].rearrange("p a b -> p (a b)"), C("ident"))
                    m = e.transpose(ps[0:(NVEC - NGLA) * NS, 6, pr * P:pr * P + P], sv[:, pr, NGLA:NVEC, :].rearrange("p a b -> p (a b)"), C("ident"))
                m.then_inc(S("pe_step"), 1)
                gate_tiles(GATES_AT[0])
                e.wait_ge(S("dve_sa"), 1)
                mm(bank(7, HD), C("quads"), sa, start=True, stop=True).then_inc(S("pe_step"), 1)
                gate_tiles(GATES_AT[1])
                e.wait_ge(S("dve_po"), 1)
                for m_ in range(4):
                    mm(bank(5, 32, 32 * m_), po[:, m_, :, :].rearrange("p a b -> p (a b)"), C("samples"), start=True, stop=True)
                mm(bank(5, 32, 128), pn.to_broadcast([P, P]), C("samples"), start=True, stop=True).then_inc(S("pe_step"), 1)

                gate_tiles(GATES_AT[2])
                e.wait_ge(S("dve_yy"), 1)
                for t in (0, 1, 6, 7):
                    m = mm(bank(t), C("headmean"), yy[:, t, :], start=True, stop=True)
                m.then_inc(S("pe_step"), 1)
                gate_tiles(GATES_AT[3])
                e.wait_ge(S("act_step"), step("act_ysq"))
                e.wait_ge(S("dve_yc"), 1)
                for t in range(8):
                    if t >= 6:
                        e.wait_ge(S("act_var"), t - 5)
                    mm(bank(VAR_BANKS[t]), C("headmean"), rs8[:, t, :], start=True, stop=True).then_inc(S("pe_var"), 1)
                gate_tiles(32 - EARLY_GATES - sum(GATES_AT))
                for b in (2, 3):
                    take(e, bank_free[b], 1)
                e.wait_ge(S("dve_yn"), 1)
                for o in range(KT):
                    j = BRANCH_SLOTS[o // 2]
                    if o % 2 == 0:
                        take(e, w_full[j], 16)
                    for m_, b in enumerate(BRANCH_BANKS):
                        take(e, bank_free[b], 1)
                        for k in range(2):
                            at = (o % 2) * D + (2 * m_ + k) * P
                            m = mm(bank(b), ring[:, j, at:at + P], yy[:, 2 * m_ + k, :], start=k == 0, stop=k == 1)
                        m.then_inc(bank_full[b], 1)
                e.wait_ge(S("dve_mg"), 1)

                def project(src, tag, done):
                    for o in range(KT):
                        j = o // 2
                        if o % 2 == 0:
                            take(e, w_full[j], 16)
                        if o >= 2:
                            e.wait_ge(S(done), o - 1)
                        for kt in range(KT):
                            at = (o % 2) * D + kt * P
                            m = mm(bank(o % 2), ring[:, j, at:at + P], src[:, kt, :], start=kt == 0, stop=kt == KT - 1)
                        m.then_inc(S(tag), 1)

                project(merged, "pe_wo", "dve_x")
                sum_squares(sqs, 2)
                e.wait_ge(S("dve_xn"), 2)
                e.wait_ge(S("sp_keys"), 16)
                for o in range(KT + 1):
                    if o < KT:
                        if o % 2 == 0:
                            take(e, w_full[o // 2], 16)
                        if o >= 2:
                            e.wait_ge(S("act_q"), 2 * (o - 1))
                        for kt in range(KT):
                            at = (o % 2) * D + kt * P
                            m = mm(bank(6 + o % 2), ring[:, o // 2, at:at + P], xn[:, kt, :], start=kt == 0, stop=kt == KT - 1)
                        m.then_inc(S("pe_wq"), 1)
                    if o:
                        h = o - 1
                        e.wait_ge(S("act_q"), 2 * o)
                        mm(bank(h // 2, 256, 256 * (h % 2)), qpe[:, h, 0:P], keys[:, h, :], start=True, stop=True).then_inc(S("pe_ps"), 1)
                for h in range(PH):
                    m = mm(ps[0:NS * PH, 4, 0:256], qz[:, h, :], keys[:, h, :], start=h == 0, stop=h == PH - 1)
                m.then_inc(S("pe_ps"), 1)
                e.wait_ge(S("dve_qz"), 1)
                e.wait_ge(S("act_ps"), 5)
                for tt in range(3):
                    for g in range(2):
                        b = 2 + 2 * tt + g
                        for k in range(4):
                            kt = 4 * g + k
                            if tt < 2:
                                m = e.transpose(ps[:, b, k * P:k * P + P], xn[:, kt, tt * P:tt * P + P], C("ident"))
                            else:
                                m = mm(bank(b, P, k * P), xrep[:, kt, :], C("ident"), start=True, stop=True)
                m.then_inc(S("pe_step"), 1)
                e.wait_ge(S("act_step"), step("act_xt"))
                for h in range(PH):
                    m = mm(bank(h // 2, 256, 256 * (h % 2)), qpe[:, h, P:SEQ], keys[:, h, :], start=True, stop=True)
                m.then_inc(S("pe_ps"), 1)
                e.wait_ge(S("dve_acc"), 1)
                for tt in range(TT):
                    for kt in range(KT):
                        e.transpose(ps[:, 2 * tt + kt // 4, (kt % 4) * P:(kt % 4) * P + P], acc[tt][:, kt * P:kt * P + P], C("ident"))
                for kt in range(KT):
                    m = mm(bank(4, NS, NS * kt), acc[2][:, kt * P:kt * P + P], C("group"), start=True, stop=True)
                m.then_inc(S("pe_step"), 1)
                layer_end(e, "pe")
            sum_squares(sqs, 1)

        @block.scalar
        def _(e):
            own = Own(e, "act_own")
            act = e.activation

            def bank(b, n=N, lo=0, p0=0, p1=P):
                return ps[p0:p1, b, lo:lo + n]

            def eps(i):
                a = CONST_AT["eps"][0]
                return const[:, a + i:a + i + 1]

            def root(k, to):
                e.wait_ge(S("pe_ss"), k)
                act(to, bank(0), ACT.Sqrt, bias=eps(0), scale=1.0 / D).then_inc(S("act_rt"), 1)

            e.wait_ge(S("sp_once"), 48)
            e.wait_ge(S("dve_lb"), 1)
            own(act(lb_all[:, :], lb_all[:, :], ACT.Exp))
            e.sem_inc(S("act_lb"), 1)
            with e.Fori(0, L) as l:
                own.clear()
                root(1, rstd)
                for b in range(2):
                    e.sem_inc(bank_free[b], 1)
                def column_tile(t, dst):
                    b = t % 2
                    take(e, bank_full[b], 1)
                    act(dst, bank(b), ACT.Copy).then_inc(bank_free[b], 1)
                    if b:
                        e.sem_inc(w_free[t // 2], 1)

                for t in range(8):
                    column_tile(t, proj[:, HG + t, :])
                act(sgn[:, :, :], proj[:, HG + 2:HG + 4, :], ACT.Sigmoid, scale=-1.0).then_inc(S("act_step"), 1)
                own(act(proj[:, HG + 2:HG + 4, :], proj[:, HG + 2:HG + 4, :], ACT.Sigmoid))
                act(proj[:, HG:HG + 2, :], proj[:, HG:HG + 2, :], ACT.Silu).then_inc(S("act_step"), 1)
                with e.Fori(0, HD // 16) as i:
                    for u in range(16):
                        e.wait_ge(out_done, i * 16 + u + 1)
                        e.sem_inc(S("act_turn"), 1)
                        act(win[:, u % 4, :], const[:, bass.ds(CONST_AT["place"][0] + HD - 1 - i * 16 - u, P)], ACT.Copy).then_inc(win_full, 1)
                        for t in [t for t, after in enumerate(TILE_AFTER) if u == min(after + 3, 15)]:
                            column_tile(t, proj[:, bass.ds(i * 6 + RW + t, 1), :].rearrange("p a n -> p (a n)"))
                for b in range(2):
                    take(e, bank_free[b], 1)
                e.sem_inc(S("act_step"), 1)
                e.wait_ge(S("sp_par"), 16 * 9)
                act(sv[:, :, V_Q, :], proj[:, HG:HG + 2, SEQ:N], ACT.Copy)
                act(sv[:, :, V_V, :], proj[:, HG + 4:HG + 6, SEQ:N], ACT.Copy)
                gate = iter(range(32))

                def gate_tiles(n, banks=2):
                    for g in [next(gate) for _ in range(n)]:
                        b = banks + g % 2
                        take(e, bank_full[b], 1)
                        act(gates[g], bank(b), ACT.Sigmoid if g >= EARLY_GATES else ACT.Copy).then_inc(bank_free[b], 1)
                        if g % 2:
                            e.sem_inc(w_free[g // 2 % 4], 1)

                e.wait_ge(S("dve_xs"), 1)
                act(proj[0:HD, RW + 6, :], proj[0:HD, RW + 6, :], ACT.Tanh)
                act(proj[:, RW + 7, :], proj[:, RW + 7, :], ACT.Sigmoid).then_inc(S("act_step"), 1)
                e.wait_ge(S("pe_step"), step("pe_lr"))
                for pr in range(PR):
                    act(loga[:, pr, :], bank(2 + pr), ACT.Sigmoid, bias=V("w0", pr))
                    act(aa[:, pr, :], bank(4 + pr), ACT.Sigmoid, bias=V("a0", pr)).then_inc(S("act_wa"), 1)
                for pr in range(PR):
                    act(gg[:, pr, :], bank(6 + pr), ACT.Copy).then_inc(S("act_wag"), 1)
                e.wait_ge(S("act_wag"), 2)
                for b in (6, 7):
                    e.sem_inc(bank_free[b], 1)
                e.wait_ge(S("pe_step"), step("pe_kk"))
                for pr in range(PR):
                    i = act(t1[:, pr, :], bank(pr), ACT.Sqrt)
                i.then_inc(S("act_step"), 1)
                gate_tiles(RWKV_GATES // 2, 6)
                e.wait_ge(S("dve_cum"), 1)
                act(e_b[:, :, :], al[:, :, :], ACT.Exp)
                act(e_n[:, :, :], al[:, :, :], ACT.Exp, scale=-1.0)
                act(e_p[:, :, :], kb[:, :, :], ACT.Exp).then_inc(S("act_step"), 1)
                act(sv[:, :, RW_W, :], loga[:, :, SEQ:N], ACT.Exp).then_inc(S("act_step"), 1)
                gate_tiles(RWKV_GATES // 2, 6)
                e.wait_ge(S("pe_step"), step("pe_tr"))
                e.wait_ge(S("pool_kz"), 1)
                for tt in range(TT):
                    src = bank(4, 256, 256 * tt)
                    act(vpad[:, tt, :, HD:2 * HD], src.rearrange("p (h c) -> p h c", c=HD), ACT.Copy)
                    for q in range(2):
                        act(vc[:, 2 * tt + q, :], src, ACT.Copy, scale=C("rows")[:, q:q + 1])
                    act(alt[:, tt, :], bank(5, 256, 256 * tt), ACT.Copy)
                    i = act(kbt[:, tt, :], bank(6, 256, 256 * tt), ACT.Copy)
                i.then_inc(S("act_step"), 1)
                e.wait_ge(S("pe_step"), step("pe_bv"))
                act(bv[:, :, :].rearrange("p a b -> p (a b)"), bank(2, 512), ACT.Copy).then_inc(S("act_step"), 1)
                for c in range(NCH):
                    e.wait_ge(S("pe_y"), c + 1)
                    act(yy[:, 0:2, c * CH:c * CH + CH], bank(5, 2 * CH).rearrange("p (a b) -> p a b", b=CH), ACT.Copy).then_inc(S("act_y"), 1)

                def causal(mixer):
                    e.wait_ge(S("pe_ctr"), mixer + 1)
                    for tt in range(TT):
                        act(vpad[:, tt, :, HD:2 * HD], bank(4, 256, 256 * tt).rearrange("p (h c) -> p h c", c=HD), ACT.Copy)
                    act(ktok[:, :, :].rearrange("p a b -> p (a b)"), bank(5, 512), ACT.Copy).then_inc(S("act_cv"), 1)
                    e.wait_ge(S("pe_co"), mixer + 1)
                    for pr in range(PR):
                        act(yy[:, 4 + 2 * mixer + pr, 0:SEQ], bank(pr, SEQ), ACT.Copy)
                        if mixer:
                            act(denk[:, pr, 0:SEQ], bank(2 + pr, SEQ), ACT.Abs)
                    e.wait_ge(S("pe_cf"), mixer + 1)
                    if mixer:
                        e.wait_ge(S("sp_dfin"), 16)
                        act(nfin, bank(6, PR, 256), ACT.Copy)
                    act(sfin[:, :, :].rearrange("p a b -> p (a b)"), bank(6, 256), ACT.Copy).then_inc(S("act_co"), 1)
                    e.wait_ge(S("act_co"), mixer + 1)
                    e.dma_start(O["p_ret" if not mixer else "p_ml"][bass.ds(l, 1)].rearrange("a p c -> p (a c)"), sfin[:, :, :].rearrange("p a b -> p (a b)")).then_inc(S("sp_dfin"), 16)
                    if mixer:
                        e.dma_start(O["p_n"][bass.ds(l, 1)].rearrange("a p c -> p (a c)"), nfin).then_inc(S("sp_dfin"), 16)

                causal(0)
                e.wait_ge(S("pe_step"), step("pe_if"))
                act(rows[0:4, 0, :], ps[0:4, 2, 0:N], ACT.Identity, bias=V("ig_b")[0:4, :])
                act(rows[0:4, 1, :], ps[0:4, 3, 0:N], ACT.Identity, bias=V("fg_b")[0:4, :]).then_inc(S("act_step"), 1)
                e.wait_ge(S("dve_r1"), 1)
                own(act(rows[0:4, 3, :], rows[0:4, 2, :], ACT.Exp, scale=-1.0))
                act(rows[0:4, 3, :], rows[0:4, 3, :], ACT.Ln, bias=const[0:4, CONST_AT["eps"][0] + 3:CONST_AT["eps"][0] + 4]).then_inc(S("act_step"), 1)
                for b in (6, 7):
                    e.sem_inc(bank_free[b], 1)
                gate_tiles(2, 6)
                e.wait_ge(S("dve_cv"), 1)
                for t in range(4):
                    dst, src = (qr, kq)[t // 2][:, t % 2, :], cv[:, t, :]
                    act(dst[:, 0:SEQ], src[:, 0:SEQ], ACT.Silu, bias=V("cb", t))
                    act(dst[:, SEQ:N], src[:, SEQ:288].rearrange("p (b j) -> p b j", j=4)[:, :, 3], ACT.Silu, bias=V("cb", t)).then_inc(S("act_silu"), 1)
                act(out_conv[:, :, 0, :], cpad[:, :, SEQ:SEQ + 3], ACT.Copy)
                for t in range(4):
                    i = act(out_conv[:, t, 1:NS + 1, :], cpad[:, t, SEQ + 3:].rearrange("p (b j) -> p b j", j=4)[:, :, 1:4], ACT.Copy)
                i.then_inc(S("act_step"), 1)
                gate_tiles(EARLY_GATES - RWKV_GATES - 2, 6)
                e.wait_ge(S("pe_step"), step("pe_rows"))
                for pr in range(PR):
                    act(emk[:, pr, :], bank(2 + pr), ACT.Exp, scale=-1.0)
                    i = act(fa[:, pr, :], bank(2 + pr, 2 * NS, N), ACT.Exp)
                i.then_inc(S("act_step"), 1)
                e.wait_ge(S("dve_dt"), 1)
                act(att[:, :, :], att[:, :, :], ACT.Exp).then_inc(S("act_step"), 1)
                causal(1)
                e.wait_ge(S("dve_sv"), 1)
                e.wait_ge(S("sp_dfin"), 48)
                act(sv[:, :, V_V + 1, :], proj[:, RT + 4:RT + 6, SEQ:N], ACT.Copy)
                act(sv[:, :, V_V + 2, :], proj[:, ML + 4:ML + 6, SEQ:N], ACT.Copy).then_inc(S("act_step"), 1)
                e.wait_ge(S("pe_step"), step("pe_svt"))
                act(svt[0:NGLA * NS, :, :].rearrange("p a b -> p (a b)"), bank(5, 256, p1=NGLA * NS), ACT.Copy)
                act(svt2[0:(NVEC - NGLA) * NS, :, :].rearrange("p a b -> p (a b)"), bank(6, 256, p1=(NVEC - NGLA) * NS), ACT.Copy).then_inc(S("act_step"), 1)
                act(proj[:, HG + 6:HG + 8, :], proj[:, HG + 6:HG + 8, :], ACT.Silu)
                act(proj[:, RT + 6:RT + 8, :], proj[:, RT + 6:RT + 8, :], ACT.Silu)
                act(proj[:, HG:HG + 6, :], proj[:, HG:HG + 6, :], ACT.Sigmoid)
                act(proj[:, RW:RW + EARLY_GATES - 6, :], proj[:, RW:RW + EARLY_GATES - 6, :], ACT.Sigmoid)
                act(proj[:, ML + 6:ML + 8, :], proj[:, ML + 6:ML + 8, :], ACT.Sigmoid).then_inc(S("act_step"), 1)
                for b in (2, 3):
                    e.sem_inc(bank_free[b], 1)
                gate_tiles(sum(GATES_AT[:3]))
                e.wait_ge(S("dve_yc"), 1)
                act(rs8[:, :, :], yy[:, :, :], ACT.Square).then_inc(S("act_step"), 1)
                gate_tiles(GATES_AT[3])
                for t in range(8):
                    e.wait_ge(S("pe_var"), t + 1)
                    act(fg8[:, t, :], bank(VAR_BANKS[t]), ACT.Sqrt, bias=eps(1 if t < 2 else 2)).then_inc(S("act_var"), 1)
                e.wait_ge(S("act_var"), 8)
                for b in BRANCH_BANKS:
                    e.sem_inc(bank_free[b], 1)
                gate_tiles(32 - EARLY_GATES - sum(GATES_AT))
                root(2, rstd)
                e.wait_ge(S("dve_qz"), 1)
                for o in range(KT + 1):
                    if o < KT:
                        e.wait_ge(S("pe_wq"), o + 1)
                        act(qpe[:, o, :], bank(6 + o % 2, SEQ), ACT.Copy).then_inc(S("act_q"), 1)
                        own_cols = qz[:, o, :].rearrange("p (b h) -> p b h", h=PH)[:, :, o]
                        act(own_cols, bank(6 + o % 2, NS, SEQ), ACT.Copy).then_inc(S("act_q"), 1)
                        if o % 2:
                            e.sem_inc(w_free[o // 2], 1)
                    if o and o % 2 == 0:
                        b = o // 2 - 1
                        e.wait_ge(S("pe_ps"), o)
                        act(sc0[:, 4 * b:4 * b + 4, :].rearrange("p a b -> p (a b)"), bank(b, 512), ACT.Copy).then_inc(S("act_ps"), 1)
                e.wait_ge(S("pe_ps"), PH + 1)
                act(sc_s[0:NS * PH, :, :].rearrange("p a b -> p (a b)"), ps[0:NS * PH, 4, 0:256], ACT.Copy).then_inc(S("act_ps"), 1)
                e.wait_ge(S("pe_step"), step("pe_xt"))
                for tt in range(3):
                    for g in range(2):
                        i = act(xtok[:, tt, g * 512:g * 512 + 512], bank(2 + 2 * tt + g, 512), ACT.Copy)
                i.then_inc(S("act_step"), 1)
                e.wait_ge(S("pe_ps"), PH + 2)
                for b in range(4):
                    a = act(sc1[:, 4 * b:4 * b + 4, :].rearrange("p a b -> p (a b)"), bank(b, 512), ACT.Copy)
                a.then_inc(S("act_ps"), 1)

                def numerators(n, p1=P, nh=PH):
                    e.wait_ge(S("dve_top"), n)
                    act(t16[0:p1, 0:nh, :], t16[0:p1, 0:nh, :], ACT.Exp).then_inc(S("act_top"), 1)

                numerators(1)
                def gelu(h):
                    take(e, hid_full[h], 1)
                    act(hge[:, h, :], hid[:, h, :], ACT.Gelu).then_inc(hid_gelu[h], 1)
                def gelus(lo, hi):
                    with e.Fori(lo, hi) as _i:
                        gelu(0)
                        gelu(1)

                gelus(0, EXP_AT[0])
                numerators(2, NS * PH, 1)
                gelus(EXP_AT[0], EXP_AT[1])
                numerators(3)
                gelus(EXP_AT[1], 16)
                gelus(0, 16)
                gelu(0)
                gelu(1)
                layer_end(e, "act")
            root(1, rstd)

        @block.gpsimd
        def _(e):
            own = Own(e, "pool_own")
            tt_ = e.tensor_tensor
            for t in (keyz, vpad, upad):
                n = len(t.shape) - 1
                names = " ".join(f"d{i}" for i in range(n))
                idx = tuple(slice(None) for _ in t.shape)
                i = e.memset(t[idx].rearrange(f"p {names} -> p ({names})"), 0.0)
                i.then_inc(S("pool_zero"), 1)
            e.wait_ge(S("pool_zero"), 3)
            for j in range(2):
                e.sem_inc(u_free[j], 1)
                e.sem_inc(v_free[j], 1)
            with e.Fori(0, L) as l:
                own.clear()

                def by_head(n, src):
                    for q in range(2):
                        h = slice(HD * q, HD * q + HD)
                        i = e.tensor_copy(keyz[h, n, q, :, :], src[h, :, :])
                    return i

                e.wait_ge(S("dve_hg"), 1)
                with e.Fori(0, HD // 4) as i:
                    own.clear()
                    for u in range(4):
                        e.wait_ge(ss_full, i * 4 + u + 1)
                        e.sem_inc(S("pool_turn"), 1)
                        own(e.tensor_copy(hfin[:, bass.ds(i * 4 + u, 1), :].rearrange("p a b -> p (a b)"), ss[:, u, SEQ - 1::SEQ]))
                        tt_(ss[:, u, :], ss[:, u, :], qp[:, :, :].rearrange("p a b -> p (a b)"), ALU.mult).then_inc(qs_full, 1)
                own.clear()
                e.sem_inc(S("pool_hf"), 1)
                e.wait_ge(S("dve_kr"), 1)
                e.wait_ge(S("pool_zero"), 3)
                by_head(0, al)
                by_head(1, kb).then_inc(S("pool_kz"), 1)
                e.wait_ge(S("dve_qk"), 1)
                e.wait_ge(S("pe_cm"), 8)
                by_head(0, kq[:, :, 0:SEQ]).then_inc(S("pool_kz"), 1)
                e.wait_ge(S("dve_qk"), 2)
                by_head(1, kq[:, :, 0:SEQ]).then_inc(S("pool_kz"), 1)
                e.wait_ge(S("sp_svr"), 16 * 5)
                e.wait_ge(S("sp_par"), 16 * 9)
                rw = st[:, 3, :, :]

                def over_v(v, n=1):
                    return bc(gv[:, v:v + n, :], 3, [P, n, 16, HD]) if n > 1 else bc(gv[:, v, :], 2, [P, 16, HD])

                own(tt_(big2, rw, over_v(RW_KK), ALU.mult))
                e.sem_inc(S("pool_sa"), 1)
                gla = st[:, 0:3, :, :]
                own(tt_(gla, gla, over_v(V_F, 3), ALU.mult))
                for m in range(3):
                    i = tt_(big1[:, m, :, :], over_v(V_K + m), bc(gvv[:, m, :], 1, [P, 16, HD]), ALU.mult)
                own(i)
                own(tt_(gla, gla, big1, ALU.add))
                own(tt_(big1, gla, over_v(V_Q, 3), ALU.mult))
                own(tt_(st_n[:, :], st_n[:, :], gv[:, V_F + 2, :], ALU.mult))
                own(tt_(st_n[:, :], st_n[:, :], gv[:, V_K + 2, :], ALU.add))
                own(tt_(nq, st_n[:, :], gv[:, V_Q + 2, :], ALU.mult))
                e.sem_inc(S("pool_gla"), 1)
                own(tt_(rw, rw, over_v(RW_W), ALU.mult))
                e.wait_ge(S("dve_sa"), 2)
                own(tt_(big2, over_v(RW_KKA), bc(sab, 1, [P, 16, HD]), ALU.mult))
                own(tt_(rw, rw, big2, ALU.add))
                own(tt_(big2, over_v(RW_K), bc(gvv[:, 3, :], 1, [P, 16, HD]), ALU.mult))
                own(tt_(rw, rw, big2, ALU.add))
                own(tt_(big2, rw, over_v(RW_R), ALU.mult))
                e.sem_inc(S("pool_st"), 1)
                e.sem_inc(S("pool_rw"), 1)
                e.wait_ge(S("act_ps"), 6)
                u_rows = A["peer_u"]
                v_rows = A["peer_v"]
                own.clear()

                def fetch(h, src, table, rows_, ix, full, free):
                    take(e, free[h], 1)
                    own(e.tensor_copy(ix[:, h, :], src))
                    for j in range(4):
                        e.indirect_dma_start(out=rows_[:, 4 * h + j, :], out_offset=None, in_=table,
                                             in_offset=bass.IndirectOffsetOnAxis(ap=ix[:, h, j:j + 1], axis=0)).then_inc(full[h], 16)

                for tt in range(TT):
                    e.wait_ge(S("dve_route"), 3 if tt else 1)
                    with e.Fori(0, 16) as i:
                        own.clear()
                        for h in range(2):
                            src = eidx[:, tt, bass.ds(i * 8 + 4 * h, 4)].bitcast(U32)
                            fetch(h, src, u_rows, urows, ixu, u_full, u_free)
                            fetch(h, src, v_rows, vrows, ixv, v_full, v_free)
                    own.clear()
                e.wait_ge(S("sp_sr"), 32)
                for h in range(2):
                    fetch(h, es[:, 4 * h:4 * h + 4], u_rows, urows, ixu, u_full, u_free)
                    fetch(h, es[:, 4 * h:4 * h + 4], v_rows, vrows, ixv, v_full, v_free)
                layer_end(e, "pool")

        @block.vector
        def _(e):
            own = Own(e, "dve_own")
            tt_, ts, stt = e.tensor_tensor, e.tensor_scalar, e.scalar_tensor_tensor

            def bank(b, n=N, lo=0, p0=0, p1=P):
                return ps[p0:p1, b, lo:lo + n]

            def squares(sq_):
                tt_(sq_[:, :, :], x[:, :, :], x[:, :, :], ALU.mult).then_inc(S("dve_sq"), 1)

            def norm(k, gain):
                e.wait_ge(S("act_rt"), k)
                own(e.reciprocal(rstd, rstd))
                for kt in range(KT):
                    i = stt(xn[:, kt, :], x[:, kt, :], gain(kt), rstd, ALU.mult, ALU.mult)
                i.then_inc(S("dve_xn"), 1)

            e.memset(layer_off[:, :], 0.0)
            own(e.memset(small[:, :], 0.0))
            e.wait_ge(S("sp_once"), 48)
            lg = glob[:, 8:8 + 2 * L].rearrange("p (a b) -> p a b", b=PR)
            la = lb_all[:, :].rearrange("p (a b) -> p a b", b=PR)
            own(tt_(small[:, 0:2], lg[:, 0, :], lg[:, 1, :], ALU.max))
            tt_(la, lg, bc(small[:, 0:2], 1, [P, L, PR]), ALU.subtract).then_inc(S("dve_lb"), 1)
            e.wait_ge(S("act_lb"), 1)
            own(tt_(small[:, 2:4], la[:, 0, :], la[:, 1, :], ALU.add))
            own(e.reciprocal(small[:, 2:4], small[:, 2:4]))
            own(tt_(la, la, bc(small[:, 2:4], 1, [P, L, PR]), ALU.mult))
            own(tt_(la[:, 1, :], la[:, 1, :], la[:, 0, :], ALU.add))
            own(tt_(la[:, 1, :], la[:, 1, :], la[:, 0, :], ALU.subtract))
            own(tt_(la[:, 0, :], la[:, 0, :], la[:, 0, :], ALU.subtract))
            with e.Fori(0, L) as l:
                own.clear()
                squares(sqs)
                e.wait_ge(S("sp_par"), 16 * 9)
                norm(1, lambda kt: V("ln1", kt))
                own(ts(lb[:, 0, :], lb_all[:, bass.ds(l * PR, PR)], 1e-30, None, ALU.max))
                own(ts(lb[:, 1, :], lb_all[:, bass.ds(l * PR, PR)], -1.0, 1.0, ALU.mult, ALU.add))
                own(tt_(lb[:, 2, :], lb[:, 0, :], lb_all[:, bass.ds(l * PR, PR)], ALU.subtract))

                e.wait_ge(S("act_step"), step("act_hg"))
                for pr in range(PR):
                    ts(proj[:, HG + 2 + pr, :], proj[:, HG + 2 + pr, :], lb[:, 1, pr:pr + 1], lb[:, 0, pr:pr + 1], ALU.mult, ALU.add)
                    i = ts(sgn[:, pr, :], sgn[:, pr, :], lb[:, 1, pr:pr + 1], lb[:, 2, pr:pr + 1], ALU.mult, ALU.subtract)
                own(i)
                e.tensor_copy(sv[:, :, V_F, :], proj[:, HG + 2:HG + 4, SEQ:N])
                e.tensor_copy(sv[:, :, V_K, :], sgn[:, :, SEQ:N])
                e.tensor_copy(qp, proj[:, HG:HG + 2, 0:SEQ])
                e.tensor_copy(kp, sgn[:, :, 0:SEQ])
                own(e.tensor_copy(fp, proj[:, HG + 2:HG + 4, 0:SEQ]))
                own(e.memset(fp[:, :, 0:1], 0.0))
                e.sem_inc(out_done, 4)
                e.sem_inc(S("dve_hg"), 1)
                flat = lambda t: t[:, :, :].rearrange("p a b -> p (a b)")
                with e.Fori(0, HD // 16) as i:
                    own.clear()

                    def key_value(u):
                        take(e, value_full[u % VB], 32)
                        tt_(kv[:, u % VB, :], kv[:, u % VB, :], flat(kp), ALU.mult).then_inc(own.s, 1)

                    key_value(0)
                    for u in range(16):
                        if u < 15:
                            key_value(u + 1)
                        e.wait_ge(out_done, i * 16 + u + 1)
                        e.wait_ge(own.s, u + 1)
                        e.tensor_tensor_scan(ss[:, u % 4, :], flat(fp), kv[:, u % VB, :], 0.0, ALU.mult, ALU.add).then_inc(ss_full, 1)
                e.wait_ge(S("pe_hg"), 1)
                own.clear()
                own(e.tensor_copy(yy[:, 2:4, 0:SEQ], bank(4, 512).rearrange("p (a b) -> p a b", b=SEQ)))

                e.wait_ge(S("act_step"), step("act_proj"))
                e.wait_ge(S("sp_hfin"), 16)
                raw = proj[:, RW:RW + 8, :]
                e.tensor_copy(out_shift[:, :, :], raw[:, :, SEQ - 1:N]).then_inc(S("dve_shift"), 1)
                tt_(diff[:, :, 1:SEQ], raw[:, :, 0:SEQ - 1], raw[:, :, 1:SEQ], ALU.subtract)
                ts(diff[:, :, 0:1], raw[:, :, 0:1], -1.0, None, ALU.mult)
                own(tt_(diff[:, :, SEQ:N], st_shift[:, :, :], raw[:, :, SEQ:N], ALU.subtract))
                for t in (6, 7, 0, 1, 2, 3, 4, 5):
                    i = stt(raw[:, t, :], diff[:, t, :], V("mu", t), raw[:, t, :], ALU.mult, ALU.add)
                    if t == 7:
                        i.then_inc(S("dve_xs"), 1)
                own(i)
                r, k, v = raw[:, 0:2, :], raw[:, 2:4, :], raw[:, 4:6, :]
                for pr in range(PR):
                    i = ts(kk[:, pr, :], k[:, pr, :], V("kk", pr), None, ALU.mult)
                own(i)
                tt_(t1, kk, kk, ALU.mult).then_inc(S("dve_kk2"), 1)
                e.wait_ge(S("act_step"), step("act_kk"))
                own(ts(t1, t1, 1e-12, None, ALU.max))
                own(e.reciprocal(t1, t1))
                own(tt_(kk, kk, t1, ALU.mult))
                e.wait_ge(S("act_wa"), 2)
                for pr in range(PR):
                    i = ts(kn[:, pr, :], aa[:, pr, :], 1.0, V("ka", pr), ALU.subtract, ALU.mult)
                ts(loga, loga, -float(np.exp(-0.5)), None, ALU.mult)
                own(i)
                own(stt(kn, kn, 1.0, k, ALU.add, ALU.mult))
                for pr in range(PR):
                    own(stt(t1[:, pr, :], r[:, pr, :], V("rk", pr), kn[:, pr, :], ALU.mult, ALU.mult))
                e.sem_inc(S("dve_rk"), 1)
                for pr in range(PR):
                    i = e.tensor_tensor_scan(al[:, pr, :], C("chunkstart"), loga[:, pr, 0:SEQ], 0.0, ALU.mult, ALU.add)
                own(i)
                tt_(kb, al, loga[:, :, 0:SEQ], ALU.subtract).then_inc(S("dve_cum"), 1)
                tt_(kka, kk, aa, ALU.mult)
                for n, src in ((RW_K, kn), (RW_R, r), (RW_KK, kk), (RW_V, v)):
                    e.tensor_copy(sv[:, :, n, :], src[:, :, SEQ:N])
                own(tt_(sv[:, :, RW_KKA, :], kk[:, :, SEQ:N], aa[:, :, SEQ:N], ALU.mult))
                e.wait_ge(S("act_step"), step("act_e"))
                q4 = lambda t: t[:, :, 0:SEQ].rearrange("p a (b c) -> p a b c", c=P)
                tt_(kr[:, :, :, 0:P], q4(kk), q4(e_p), ALU.mult)
                tt_(kr[:, :, :, P:256], q4(r), q4(e_b), ALU.mult)
                tt_(al, kka[:, :, 0:SEQ], e_n, ALU.mult)
                tt_(kb, kn[:, :, 0:SEQ], e_n, ALU.mult).then_inc(S("dve_kr"), 1)
                e.wait_ge(S("pe_step"), step("pe_rk"))
                for pr in range(PR):
                    i = tt_(vb[:, pr, :], bank(2 + pr), v[:, pr, :], ALU.mult)
                own(i)
                e.wait_ge(S("act_step"), step("act_vpad"))
                e.wait_ge(S("pool_kz"), 1)
                for n in range(TT * H):
                    e.wait_ge(S("pe_cm"), n + 1)
                    tt_(chunk_m[:, n, :], bank((7, 0, 1)[n % 3], 512), C("chunkmask"), ALU.mult).then_inc(S("dve_cm"), 1)
                e.wait_ge(S("dve_cm"), 8)
                e.wait_ge(S("act_step"), step("act_sv0"))
                ident8 = bc(C("ident"), 1, [P, 8, P])
                e.tensor_copy(xm, ident8)
                e.tensor_copy(xt, ident8).then_inc(S("dve_inv"), 1)
                for k_ in range(6):
                    lev = CONST_AT["levels"][0] + k_ * P
                    for tt in range(TT):
                        e.wait_ge(S("pe_t"), 2 * k_ + tt + 1)
                        tt_(rr[:, tt, :, :], bank(3 + tt, 512).rearrange("p (a b) -> p a b", b=P), bc(const[:, lev:lev + P], 1, [P, H, P]), ALU.mult)\
                            .then_inc(S("dve_r"), 1)
                    for tt in range(TT):
                        e.wait_ge(S("pe_p"), 2 * k_ + tt + 1)
                        for b, m_ in ((5 + tt, xm), ((7, 0)[tt], xt)):
                            d = m_[:, tt * H:tt * H + H, :].rearrange("p a b -> p (a b)")
                            i = tt_(d, d, bank(b, 512), ALU.add)
                        i.then_inc(S("dve_inv"), 1)
                e.wait_ge(S("dve_inv"), 13)
                own(e.memset(sbd, 0.0))
                e.sem_inc(S("dve_sbd"), 1)
                e.wait_ge(S("act_step"), step("act_bv"))
                for c in range(NCH):
                    tt, q = divmod(c, 2)
                    e.wait_ge(S("pe_ks"), c + 1)
                    tt_(pm, bank(3, 256), bv[:, tt, :], ALU.add).then_inc(S("dve_pm"), 1)
                    e.wait_ge(S("pe_u"), c + 1)
                    ts(upad[:, :, HD:2 * HD], bank(4, 256).rearrange("p (h c) -> p h c", c=HD), C("rows")[:, 2 + q:3 + q], None, ALU.mult)\
                        .then_inc(S("dve_u"), 1)
                    e.wait_ge(S("pe_s"), c + 1)
                    own(tt_(sb1, sbd2[:, c % 2, :, :], bank(6, 256).rearrange("p (a b) -> p a b", b=P), ALU.add))
                    for pr in range(PR):
                        at = c * CH + CH - 1
                        i = stt(sbd2[:, (c + 1) % 2, pr, :], sb1[:, pr, :], e_b[:, pr, at:at + 1], C("headsum"), ALU.mult, ALU.mult)
                    i.then_inc(S("dve_sbd"), 1)
                e.wait_ge(S("dve_sbd"), NCH + 1)
                e.wait_ge(S("act_y"), NCH)
                e.wait_ge(S("pe_step"), step("pe_rot"))
                for t in range(4):
                    sc_ = 1.0 if t < 2 else HD ** -0.5
                    dst = (qr, kq)[t // 2][:, t % 2, :]
                    stt(u1[:, 0, :], proj[:, RT + t, :], sc_, C("cos"), ALU.mult, ALU.mult)
                    own(stt(u2[:, 0, :], bank(t), sc_, C("sin"), ALU.mult, ALU.mult))
                    i = tt_(dst, u1[:, 0, :], u2[:, 0, :], ALU.add)
                    own(i)
                for n, src in ((V_K + 1, kq), (V_Q + 1, qr)):
                    e.tensor_copy(sv[:, :, n, :], src[:, :, SEQ:N])
                own(e.tensor_copy(sv[:, :, V_F + 1, :], bc(C("decay_chan"), 2, [P, PR, NS])))
                e.sem_inc(S("dve_qk"), 1)

                def causal(mixer, last):
                    for h in range(H):
                        e.wait_ge(S("pe_sc"), 4 * mixer + h + 1)
                        a = CONST_AT["decay"][0] + h * ATT
                        d = att[:, h, :] if mixer else const[:, a:a + ATT]
                        tt_(att[:, h, :], bank(6 + h % 2, ATT), d, ALU.mult).then_inc(S("dve_att"), 1)
                    e.wait_ge(S("act_cv"), mixer + 1)
                    kt4 = ktok[:, :, :].rearrange("p a (h c) -> p a h c", c=HD)
                    for tt in range(TT):
                        i = tt_(kt4[:, tt, :, :], kt4[:, tt, :, :], bc(last(tt), 2, [P, H, HD]), ALU.mult)
                    i.then_inc(S("dve_kw"), 1)

                a_end = CONST_AT["decay_end"][0]
                causal(0, lambda tt: const[:, a_end + tt * H:a_end + tt * H + H])
                R = lambda n, lo=0, hi=N: rows[0:4, n, lo:hi]
                e.wait_ge(S("act_step"), step("act_r0"))
                own(stt(R(2), R(1), -1.0, R(1), ALU.mult, ALU.max))
                e.sem_inc(S("dve_r1"), 1)
                e.wait_ge(S("act_co"), 1)
                e.memset(cpad[:, :, 0:3], 0.0)
                e.tensor_copy(cpad[:, :, 3:SEQ + 3], proj[:, ML:ML + 4, 0:SEQ])
                for t in range(4):
                    own_s = cpad[:, t, SEQ + 3:].rearrange("p (b j) -> p b j", j=4)
                    e.tensor_copy(own_s[:, :, 0:3], st_conv[:, t, :, :])
                    i = e.tensor_copy(own_s[:, :, 3:4], proj[:, ML + t, SEQ:N].unsqueeze(2))
                own(i)
                for j in range(4):
                    for t in range(4):
                        w = V("cw", 4 * t + j)
                        src = cpad[:, t, j:j + 288]
                        i = ts(cv[:, t, :], src, w, None, ALU.mult) if j == 0 else stt(cv[:, t, :], src, w, cv[:, t, :], ALU.mult, ALU.add)
                    if j < 3:
                        own(i)
                i.then_inc(S("dve_cv"), 1)
                e.wait_ge(S("act_step"), step("act_r2"))
                own(stt(R(4), R(1), 0.0, R(3), ALU.min, ALU.subtract))
                zero4 = const[0:4, CONST_AT["zero"][0]:CONST_AT["zero"][0] + SEQ]
                own(e.tensor_tensor_scan(R(7, 0, SEQ), R(4, 0, SEQ), zero4, 0.0, ALU.add, ALU.add))
                own(e.tensor_tensor_scan(rowx[0:4, 0:SEQ], R(4, 0, SEQ), R(0, 0, SEQ), 0.0, ALU.add, ALU.max))
                tt_(R(5, 0, SEQ), R(7, 0, SEQ), rowx[0:4, 0:SEQ], ALU.subtract)
                tt_(R(6, 0, SEQ), R(0, 0, SEQ), R(7, 0, SEQ), ALU.subtract)
                own(tt_(R(8, 0, NS), R(4, SEQ, N), m_old[:, :], ALU.add))
                own(tt_(rowx[0:4, SEQ:N], R(8, 0, NS), R(0, SEQ, N), ALU.max))
                tt_(rowx[0:4, N:N + NS], R(8, 0, NS), rowx[0:4, SEQ:N], ALU.subtract)
                tt_(rowx[0:4, N + NS:N + 2 * NS], R(0, SEQ, N), rowx[0:4, SEQ:N], ALU.subtract)
                own(e.tensor_copy(out_m[:, :], rowx[0:4, SEQ - 1:N]))
                e.sem_inc(S("dve_rows"), 1)
                e.wait_ge(S("act_silu"), 4)
                own(ts(kq, kq, HD ** -0.5, None, ALU.mult))
                e.wait_ge(S("act_step"), step("act_em"))
                own(e.tensor_copy(ccol, bank(4, 2 * H).rearrange("p (a b) -> p a b", b=H)))
                e.tensor_copy(sv[:, :, V_Q + 2, :], qr[:, :, SEQ:N])
                e.tensor_copy(sv[:, :, V_F + 2, :], fa[:, :, 0:NS])
                tt_(sv[:, :, V_K + 2, :], kq[:, :, SEQ:N], fa[:, :, NS:2 * NS], ALU.mult)
                for h in range(H):
                    src = bank(h // 2, SEQ, SEQ * (h % 2))
                    ts(att[:, h, 0:SEQ], src, ccol[:, 0, h:h + 1], 0.0, ALU.add, ALU.min)
                    i = ts(att[:, h, SEQ:ATT], src[:, P:SEQ], ccol[:, 1, h:h + 1], 0.0, ALU.add, ALU.min)
                own(i)
                e.sem_inc(S("dve_dt"), 1)
                e.sem_inc(S("dve_qk"), 1)
                e.wait_ge(S("act_step"), step("act_dt"))
                own(tt_(att, att, bc(C("causal"), 1, [P, H, ATT]), ALU.mult))
                e.tensor_copy(small[:, 16:20], att[:, :, SEQ - 1])
                own(e.tensor_copy(small[:, 20:24], att[:, :, ATT - 1]))
                causal(1, lambda tt: small[:, 16 + 4 * tt:20 + 4 * tt])
                e.sem_inc(S("dve_sv"), 1)
                e.wait_ge(S("pool_sa"), 1)
                e.tensor_reduce(sa, big2.rearrange("p k v -> p v k"), AX_X, ALU.add).then_inc(S("dve_sa"), 1)
                e.wait_ge(S("pe_step"), step("pe_sa"))
                ts(sab, bank(7, HD), -1.0, None, ALU.mult).then_inc(S("dve_sa"), 1)
                e.wait_ge(S("pool_gla"), 1)
                for m in range(3):
                    e.tensor_reduce(po[:, m, 0, :], big1[:, m, :, :].rearrange("p k v -> p v k"), AX_X, ALU.add)
                e.tensor_reduce(pn, nq, AX_X, ALU.add)
                e.wait_ge(S("pool_rw"), 1)
                own(e.tensor_reduce(po[:, 3, 0, :], big2.rearrange("p k v -> p v k"), AX_X, ALU.add))
                e.tensor_copy(po[:, :, 1, :], po[:, :, 0, :]).then_inc(S("dve_po"), 1)
                e.wait_ge(S("pe_step"), step("pe_po"))
                for q in range(2):
                    p0, p1 = HD * q, HD * q + HD
                    part = lambda lo, n: bank(5, n * 2 * NS, lo, p0, p1).rearrange("p (a q b) -> p a q b", q=2, b=NS)[:, :, q, :]
                    e.tensor_copy(yy[p0:p1, 2:8, SEQ:N], part(0, 6))
                    e.tensor_copy(yy[p0:p1, 0:2, SEQ:N], part(96, 2))
                    i = e.tensor_copy(denk[p0:p1, :, SEQ:N], part(128, 2))
                own(i)
                own(stt(denk, denk, -1.0, denk, ALU.mult, ALU.max))
                own(tt_(denk, denk, emk, ALU.max))
                own(e.reciprocal(denk, denk))
                own(tt_(yy[:, 6:8, :], yy[:, 6:8, :], denk, ALU.mult))
                e.sem_inc(S("dve_yy"), 1)
                e.wait_ge(S("pe_step"), step("pe_mean"))
                for t in (0, 1, 6, 7):
                    i = tt_(yy[:, t, :], yy[:, t, :], bank(t), ALU.subtract)
                own(i)
                e.sem_inc(S("dve_yc"), 1)
                e.wait_ge(S("act_var"), 8)
                e.wait_ge(S("act_step"), step("act_og"))
                own(e.reciprocal(fg8, fg8))
                own(tt_(yy, yy, fg8, ALU.mult))
                for pr in range(PR):
                    i = ts(yy[:, pr, :], yy[:, pr, :], V("ln_g", pr), V("ln_b", pr), ALU.mult, ALU.add)
                    stt(yy[:, 2 + pr, :], yy[:, 2 + pr, :], V("hg", pr), proj[:, HG + 6 + pr, :], ALU.mult, ALU.mult)
                    stt(yy[:, 6 + pr, :], yy[:, 6 + pr, :], V("mg", pr), proj[:, ML + 6 + pr, :], ALU.mult, ALU.mult)
                tt_(yy[:, 4:6, :], yy[:, 4:6, :], proj[:, RT + 6:RT + 8, :], ALU.mult)
                own(i)
                own(tt_(yy[:, 0:2, :], yy[:, 0:2, :], vb, ALU.add))
                own(tt_(yy[:, 0:2, :], yy[:, 0:2, :], gg, ALU.mult))
                e.sem_inc(S("dve_yn"), 1)
                for o in range(KT):
                    g = gates[4 * o:4 * o + 4]
                    for m, b in enumerate(BRANCH_BANKS):
                        take(e, bank_full[b], 1)
                        i = tt_(g[m], g[m], bank(b), ALU.mult)
                        if m < 3:
                            i.then_inc(bank_free[b], 1)
                    own(i)
                    e.sem_inc(bank_free[BRANCH_BANKS[3]], 1)
                    if o % 2:
                        e.sem_inc(w_free[BRANCH_SLOTS[o // 2]], 1)
                    own(tt_(fg8[:, 0, :], g[0], g[1], ALU.add))
                    own(tt_(fg8[:, 1, :], g[2], g[3], ALU.add))
                    own(tt_(merged[:, o, :], fg8[:, 0, :], fg8[:, 1, :], ALU.add))
                for b in BRANCH_BANKS:
                    take(e, bank_free[b], 1)
                e.sem_inc(S("dve_mg"), 1)
                for o in range(KT):
                    e.wait_ge(S("pe_wo"), o + 1)
                    tt_(x[:, o, :], x[:, o, :], bank(o % 2), ALU.add).then_inc(S("dve_x"), 1)
                    if o % 2:
                        e.sem_inc(w_free[o // 2], 1)
                e.wait_ge(S("dve_x"), KT)
                squares(sqs)
                norm(2, lambda kt: V("ln2", kt))
                e.wait_ge(S("dve_xn"), 2)
                own(e.memset(qz, 0.0))
                own(e.tensor_copy(xrep.rearrange("p a (b c) -> p a b c", c=16), bc(xn[:, :, SEQ:N], 3, [P, KT, NS, 16])))
                e.sem_inc(S("dve_qz"), 1)

                def top16(lists, src, tmp, val, idx):
                    for c in lists:
                        j = e.max(val(c)[:, 0:8], src(c))
                    own(j)
                    for c in lists:
                        e.max_index(idx(c)[:, 0:8], val(c)[:, 0:8], src(c))
                        j = e.match_replace(tmp(c), val(c)[:, 0:8], src(c), -BIG)
                    own(j)
                    for c in lists:
                        j = e.max(val(c)[:, 8:16], tmp(c))
                    own(j)
                    for c in lists:
                        j = e.max_index(idx(c)[:, 8:16], val(c)[:, 8:16], tmp(c))
                    own(j)

                def routing(n, p1, nh, scores_, to_idx, to_gate, ready):
                    cut = lambda t: t[0:p1, 0:nh]
                    v, ix, ixf, t_, j_ = cut(v16), cut(i16), cut(i16f), cut(t16), cut(j16)
                    vl, il = (t.rearrange("p a b c -> p (a b) c") for t in (v, ix))

                    def keys_of(lists, ready):
                        if ready:
                            e.wait_ge(S("act_ps"), ready)
                        top16(lists, lambda c: scores_[0:p1, c, :], lambda c: sc2[0:p1, c, :], lambda c: vl[:, c, :], lambda c: il[:, c, :])

                    def candidates(heads_):
                        if 0 in heads_:
                            own(e.tensor_copy(ixf, ix))
                            own(tt_(cut(cand), bc(v[:, :, 0, :], 3, [p1, nh, TOPK, TOPK]), bc(v[:, :, 1, :], 2, [p1, nh, TOPK, TOPK]), ALU.add))
                        cf = cut(cand).rearrange("p a b c -> p a (b c)")
                        c2 = sc2[0:p1, 0:2 * nh, :].rearrange("p (a b) c -> p a (b c)", b=2)
                        top16(heads_, lambda c: cf[:, c, :], lambda c: c2[:, c, :], lambda c: t_[:, c, :], lambda c: j_[:, c, :])

                    def weigh():
                        own(tt_(cut(e1), t_, t_[:, :, 0:1].to_broadcast([p1, nh, TOPK]), ALU.subtract))
                        own(e.tensor_copy(t_, cut(e1)))
                        e.sem_inc(S("dve_top"), 1)
                        ts(cut(ja), j_, 4, None, ALU.logical_shift_right)
                        own(ts(cut(jb), j_, 15, None, ALU.bitwise_and))
                        e.tensor_copy(cut(jaf), cut(ja))
                        own(e.tensor_copy(cut(jbf), cut(jb)))
                        o_ = oh[0:p1, 0:nh]
                        of = o_.rearrange("p a b c -> p (a b) c")
                        iota = bc(C("iota16")[0:p1, :], 1, [p1, nh * TOPK, TOPK])
                        own(tt_(of, bc(cut(jaf).rearrange("p a b -> p (a b)"), 2, [p1, nh * TOPK, TOPK]), iota, ALU.is_equal))
                        own(tt_(o_, o_, bc(ixf[:, :, 0, :], 2, [p1, nh, TOPK, TOPK]), ALU.mult))
                        own(e.tensor_reduce(cut(e1), o_, AX_X, ALU.add))

                    def finish():
                        o_ = oh[0:p1, 0:nh]
                        of = o_.rearrange("p a b c -> p (a b) c")
                        iota = bc(C("iota16")[0:p1, :], 1, [p1, nh * TOPK, TOPK])
                        own(tt_(of, bc(cut(jbf).rearrange("p a b -> p (a b)"), 2, [p1, nh * TOPK, TOPK]), iota, ALU.is_equal))
                        own(tt_(o_, o_, bc(ixf[:, :, 1, :], 2, [p1, nh, TOPK, TOPK]), ALU.mult))
                        own(e.tensor_reduce(cut(e2), o_, AX_X, ALU.add))
                        own(stt(cut(e1), cut(e1), 128.0, cut(e2), ALU.mult, ALU.add))
                        own(ts(to_idx.bitcast(U32), cut(e1).rearrange("p a b -> p (a b)"), layer_off[0:p1, 0:1], None, ALU.add))
                        e.wait_ge(S("act_top"), n)
                        own(e.tensor_reduce(tsum[0:p1, 0:nh], t_, AX_X, ALU.add))
                        own(e.reciprocal(tsum[0:p1, 0:nh], tsum[0:p1, 0:nh]))
                        own(tt_(to_gate.rearrange("p (b c) -> p b c", c=TOPK), t_, bc(tsum[0:p1, 0:nh], 2, [p1, nh, TOPK]), ALU.mult))
                        e.sem_inc(S("dve_route"), 1)

                    if nh == 1:
                        return [lambda: (keys_of(range(2), ready(0)), candidates(range(1))), lambda: (weigh(), finish())]
                    return ([lambda g=g: keys_of(range(4 * g, 4 * g + 4), ready(g)) for g in range(4)]
                            + [lambda: candidates(range(4)), lambda: candidates(range(4, 8)), weigh, finish])

                for part in routing(1, P, PH, sc0, eidx[:, 0, :], gate_w[:, 0, :], lambda g: g + 1):
                    part()
                own(e.memset(acc[0], 0.0))

                def dots(h, tt, nth):
                    e.wait_ge(u_full[h], nth * 64)
                    for j in range(4):
                        i = stt(urows[:, 4 * h + j, :], urows[:, 4 * h + j, :], 1.0, xtok[:, tt, :], ALU.mult, ALU.mult, accum_out=hid[:, h, j:j + 1])
                    own(i)
                    e.sem_inc(u_free[h], 1)
                    e.sem_inc(hid_full[h], 1)

                def weights(h, gates_):
                    take(e, hid_gelu[h], 1)
                    own(tt_(wgt[:, h, :], hge[:, h, :], gates_, ALU.mult))

                def sums(h, tt, nth):
                    e.wait_ge(v_full[h], nth * 64)
                    for j in range(4):
                        own(stt(acc[tt], vrows[:, 4 * h + j, :], wgt[:, h, j:j + 1], acc[tt], ALU.mult, ALU.add))
                    e.sem_inc(v_free[h], 1)

                per = GROUPS + 1
                for tt in range(TT):
                    nth = lambda i: l * per + (tt * 16 + 1) + i
                    gw = lambda i, h: gate_w[:, tt, bass.ds(i * 8 + 4 * h, 4)]
                    own.clear()
                    dots(0, tt, nth(0))
                    dots(1, tt, nth(0))
                    weights(0, gate_w[:, tt, 0:4])
                    sums(0, tt, nth(0))
                    def experts(i):
                        own.clear()
                        dots(0, tt, nth(i))
                        weights(1, gw(i - 1, 1))
                        sums(1, tt, nth(i - 1))
                        dots(1, tt, nth(i))
                        weights(0, gw(i, 0))
                        sums(0, tt, nth(i))

                    parts, ends = [], (1, 16)
                    if tt == 0:
                        parts = (routing(2, NS * PH, 1, sc_s, eidx_s[0:NS * PH, :], gate_s[0:NS * PH, :], lambda g: 5)
                                 + routing(3, P, PH, sc1, eidx[:, 1, :], gate_w[:, 1, :], lambda g: 6))
                        ends = STRETCHES
                        assert len(parts) == len(ends) - 2
                    for k, (lo, hi) in enumerate(zip(ends, ends[1:])):
                        if hi - lo > 1:
                            with e.Fori(lo, hi) as i:
                                experts(i)
                        else:
                            experts(lo)
                        own.clear()
                        if k < len(parts):
                            parts[k]()
                            if k == len(parts) - 1:
                                own(e.memset(acc[1], 0.0))
                                own(e.memset(acc[2], 0.0))
                                own(ts(layer_off[:, :], layer_off[:, :], float(EXPERTS), None, ALU.add))
                    weights(1, gate_w[:, tt, 124:128])
                    sums(1, tt, nth(15))
                last = (l + 1) * per
                e.wait_ge(S("sp_sr"), 32)
                dots(0, 2, last)
                dots(1, 2, last)
                for h in range(2):
                    weights(h, gs[:, 4 * h:4 * h + 4])
                    sums(h, 2, last)
                e.sem_inc(S("dve_acc"), 1)
                e.wait_ge(S("pe_step"), step("pe_acc"))
                for tt in range(TT):
                    for g in range(2):
                        d = x[:, 4 * g:4 * g + 4, tt * P:tt * P + P]
                        tt_(d, d, bank(2 * tt + g, 512).rearrange("p (a b) -> p a b", b=P), ALU.add)
                own(tt_(x[:, :, SEQ:N], x[:, :, SEQ:N], bank(4, NS * KT).rearrange("p (a b) -> p a b", b=NS), ALU.add))
                layer_end(e, "dve")
            own.clear()
            squares(sqs)
            norm(1, lambda kt: glob[:, kt:kt + 1])


INS = dict(x=[P, KT * N], const=[P, NCONST], glob=[P, NGLOB], par=[L, P, NPAR], wa_up=[L, P, 256], g_up=[L, P, 256],
           w_if=[L, P, KT * 8], st=[L, P, 4 * 16 * HD], st_n=[L, P, 16], st_shift=[L, P, 8 * NS], st_conv=[L, P, 4 * NS * 3],
           m_old=[L, 4, NS], keys=[L, P, PH * 256], w=[L * N_BLOCKS, P, BLOCK], peer_u=[L * EXPERTS, D], peer_v=[L * EXPERTS, D])
OUTS = dict(y=[P, KT * N], shift=[L, P, 8 * (NS + 1)], conv=[L, P, 4 * (NS + 1) * 3], m=[L, 4, NS + 1], st=[L, P, 4 * 16 * HD],
            st_n=[L, P, 16], p_rw=[L, P, 2 * P], p_ret=[L, P, 2 * P], p_ml=[L, P, 2 * P], p_n=[L, P, PR], p_hg=[L, P, HD * PR])


def kernel(**inputs):
    import concourse.bacc as bacc
    from concourse.bass_utils import run_bass_kernel_spmd

    a = {k: np.asarray(v) for k, v in inputs.items()}

    def chan(z):
        z = np.moveaxis(z, -1, 0)
        return np.moveaxis(z.reshape((z.shape[0] // P, P) + z.shape[1:]), 1, 0)

    def per_layer(f):
        return np.stack([f(l) for l in range(L)])

    vec = lambda name: (lambda l: chan(a[name][l]).reshape(P, -1))
    tokens = np.concatenate([a["x_prompt"].reshape(SEQ, D), a["x_sample"].reshape(NS, D)])
    order = ["rwkv_mu", "rwkv_w0", "rwkv_a0", "rwkv_k_k", "rwkv_k_a", "rwkv_r_k", "rwkv_ln_g", "rwkv_ln_b", "hgrn_norm_g", "mlstm_norm_g"]

    def params(l):
        cols = [vec(n)(l) for n in order]
        cols.append(chan(a["mlstm_conv_w"][l]).reshape(P, -1))
        cols += [vec(n)(l) for n in ("mlstm_conv_b", "ln1_g", "ln2_g")]
        for n in ("mlstm_ig_b", "mlstm_fg_b"):
            c = np.zeros((P, 1), a[n].dtype)
            c[:H, 0] = a[n][l]
            cols.append(c)
        return np.concatenate(cols, 1)

    o4 = 4 * D
    gate0 = o4 + 8

    def tiles(w):
        k, c = w.shape[0] // P, w.shape[1] // P
        return w.reshape(k, P, c, P).transpose(2, 1, 0, 3).reshape(c, P, k * P)

    def blocks(l):
        w = a["w_in"][l]
        m0 = 3 * D
        mixed = np.concatenate([w[:, D:2 * D], w[:, :D], w[:, 2 * D:m0 + 768], w[:, m0 + 776:m0 + 1032]], 1)
        t = list(tiles(mixed))
        gt = tiles(w[:, gate0:]).reshape(4, 8, P, D)
        br = np.stack([tiles(a["w_branch"][l, m]) for m in range(4)], 1)
        t += [gt[m, o] for o in range(8) for m in range(4)]
        t += [br[o].transpose(1, 0, 2).reshape(P, D) for o in range(8)]
        t += list(tiles(a["w_out"][l])) + list(tiles(a["peer_w_q"][l]))
        t = np.stack(t)
        return t.reshape(N_BLOCKS, 2, P, D).transpose(0, 2, 1, 3).reshape(N_BLOCKS, P, BLOCK)

    def state(l):
        s = [a["state_hgrn_S"][l], a["state_ret_S"][l], a["state_mlstm_C"][l], a["state_rwkv_S"][l].transpose(0, 1, 3, 2)]
        return np.stack(s, 2).reshape(NS, H, 4, 4, 16, HD).transpose(0, 1, 3, 2, 4, 5).reshape(P, -1)

    def keyblocks(l):
        k = a["peer_keys"][l]
        z = np.zeros((2, HD, PH, 2, P), k.dtype)
        for c in range(2):
            z[c, :, :, c, :] = k[:, c].transpose(2, 0, 1)
        return z.reshape(P, -1)

    w_gates = a["w_in"][:, :, 3 * D + 768:3 * D + 776]
    feed = dict(
        x=chan(tokens).reshape(P, -1), const=constants()[0],
        glob=np.concatenate([chan(a["lnf_g"]).reshape(P, -1), chan(a["hgrn_lb_logits"]).transpose(0, 2, 1).reshape(P, -1)], 1),
        par=per_layer(params), wa_up=np.concatenate([a["rwkv_w_up"], a["rwkv_a_up"]], 1), g_up=a["rwkv_g_up"],
        w_if=w_gates.reshape(L, KT, P, 8).transpose(0, 2, 1, 3).reshape(L, P, -1),
        st=per_layer(state),
        st_n=a["state_mlstm_n"].reshape(L, P, 16),
        st_shift=per_layer(lambda l: chan(a["state_rwkv_shift"][l]).reshape(P, -1)),
        st_conv=per_layer(lambda l: chan(a["state_mlstm_conv"][l]).reshape(P, -1)),
        m_old=a["state_mlstm_m"].transpose(0, 2, 1),
        keys=per_layer(keyblocks), w=np.concatenate([blocks(l) for l in range(L)]),
        peer_u=a["peer_u"].reshape(L * EXPERTS, D), peer_v=a["peer_v"].reshape(L * EXPERTS, D))
    nc = bacc.Bacc("TRN2", target_bir_lowering=False, num_devices=1)
    A = {k: nc.dram_tensor(f"in_{k}", INS[k], F32, kind="ExternalInput").ap() for k in INS}
    O = {k: nc.dram_tensor(f"out_{k}", OUTS[k], F32, kind="ExternalOutput").ap() for k in OUTS}
    O["scratch"] = nc.dram_tensor("scratch", [NVEC * NS, 256], F32, kind="Internal").ap()
    O["scratch_v"] = nc.dram_tensor("scratch_v", [PR, P, SEQ], F32, kind="Internal").ap()
    O["scratch_i"] = nc.dram_tensor("scratch_i", [NS * PH, TOPK], F32, kind="Internal").ap()
    O["scratch_g"] = nc.dram_tensor("scratch_g", [NS * PH, TOPK], F32, kind="Internal").ap()
    A["x"] = A["x"].rearrange("p (a b) -> p a b", b=N)
    O["y"] = O["y"].rearrange("p (a b) -> p a b", b=N)
    build(nc, A, O)
    feed = {f"in_{k}": np.ascontiguousarray(feed[k]).reshape(INS[k]) for k in INS}
    r = run_bass_kernel_spmd(nc, [feed], core_ids=[0]).results[0]
    o = {k: np.asarray(r[f"out_{k}"]) for k in OUTS}

    y = o["y"].reshape(P, KT, N).transpose(2, 1, 0).reshape(N, D)
    shift = o["shift"].reshape(L, P, 8, NS + 1).transpose(0, 3, 2, 1).reshape(L, NS + 1, D)
    conv = o["conv"].reshape(L, P, 4, NS + 1, 3).transpose(0, 3, 4, 2, 1).reshape(L, NS + 1, 3, 512)
    m = o["m"].transpose(0, 2, 1)
    st = o["st"].reshape(L, NS, H, 4, 4, 16, HD).transpose(0, 4, 1, 2, 3, 5, 6).reshape(L, 4, NS, H, HD, HD)

    def pair_blocks(z):
        z = z.reshape(L, 2, HD, PR, 2, HD)
        return np.stack([z[:, h % 2, :, h // 2, h % 2, :] for h in range(H)], 1)[:, None]

    p_rw = pair_blocks(o["p_rw"]).transpose(0, 1, 2, 4, 3)
    p_hg = o["p_hg"].reshape(L, 2, HD, HD, PR).transpose(0, 4, 1, 2, 3).reshape(L, 1, H, HD, HD)
    p_n = o["p_n"].reshape(L, 2, HD, PR).transpose(0, 3, 1, 2).reshape(L, 1, H, HD)
    return (y[:SEQ][None], y[SEQ:, None], shift[:, 0:1], p_rw, p_hg, pair_blocks(o["p_ret"]), conv[:, 0:1],
            pair_blocks(o["p_ml"]), p_n, m[:, 0:1],
            shift[:, 1:], st[:, 3].transpose(0, 1, 2, 4, 3), st[:, 0], st[:, 1], conv[:, 1:], st[:, 2],
            o["st_n"].reshape(L, NS, H, HD), m[:, 1:])
```
